# Optimizing a Trainium2 kernel written in Bass

```python
import jax, jax.numpy as jnp
from jax import lax
import numpy as np

D_MODEL = 1024
BATCH = 1
SEQ = 512
DEPTH = 2

D_CONV = D_MODEL
CONV_WIDTH = 3
RET_HEADS = 4
RET_QK_DIM = 128
RET_V_DIM = 256
RET_QK = RET_HEADS * RET_QK_DIM
RET_V = RET_HEADS * RET_V_DIM
CHUNK = 128
ROPE_BASE = 10000.0
D_FF = 4 * D_MODEL
EPS = 1e-6
MAX_START = 1024

IN_SIZES = (D_CONV, D_CONV, D_CONV, RET_QK, RET_QK, RET_V, RET_V, D_MODEL, D_MODEL)
D_IN = 3 * D_CONV + 2 * RET_QK + 2 * RET_V + 2 * D_MODEL


def rmsnorm(x, g):
    xf = x.astype(jnp.float32)
    xf = xf * lax.rsqrt(jnp.mean(xf * xf, axis=-1, keepdims=True) + EPS)
    return (xf * g.astype(jnp.float32)).astype(x.dtype)

def rotary(t, positions):
    half = t.shape[-1] // 2
    inv_freq = ROPE_BASE ** (-jnp.arange(half, dtype=jnp.float32) / half)
    ang = positions.astype(jnp.float32)[..., None] * inv_freq
    cos = jnp.cos(ang)[:, :, None, :].astype(t.dtype)
    sin = jnp.sin(ang)[:, :, None, :].astype(t.dtype)
    t1, t2 = t[..., :half], t[..., half:]
    return jnp.concatenate([t1 * cos - t2 * sin, t1 * sin + t2 * cos], axis=-1)

def short_conv_mixer(b, c, u, conv_w, w_out):
    z = c * u
    z = lax.conv_general_dilated(
        z, conv_w[:, None, :].astype(z.dtype), window_strides=(1,),
        padding=[(CONV_WIDTH - 1, 0)], dimension_numbers=("NWC", "WIO", "NWC"),
        feature_group_count=D_CONV)
    return (b * z) @ w_out

def retention_core(q, k, v, positions):
    bsz, seq = q.shape[0], q.shape[1]
    n_chunks = seq // CHUNK
    q = rotary(q, positions) * (RET_QK_DIM ** -0.5)
    k = rotary(k, positions)

    def to_chunks(t):
        return t.astype(jnp.float32).reshape(bsz, n_chunks, CHUNK, RET_HEADS, t.shape[-1]).swapaxes(0, 1)

    qc, kc, vc = to_chunks(q), to_chunks(k), to_chunks(v)
    log_gamma = jnp.log1p(-jnp.exp2(-5.0 - jnp.arange(RET_HEADS, dtype=jnp.float32)))
    pos = jnp.arange(CHUNK, dtype=jnp.float32)
    rel = pos[:, None] - pos[None, :]
    decay_intra = jnp.where(rel >= 0, jnp.exp(log_gamma[:, None, None] * jnp.maximum(rel, 0.0)), 0.0)
    decay_q = jnp.exp((pos[:, None] + 1.0) * log_gamma)
    decay_k = jnp.exp((CHUNK - 1.0 - pos[:, None]) * log_gamma)
    decay_chunk = jnp.exp(CHUNK * log_gamma)

    scores = jnp.einsum("nbqhd,nbkhd->nbhqk", qc, kc) * decay_intra
    o_intra = jnp.einsum("nbhqk,nbkhv->nbqhv", scores, vc)

    def step(state, inp):
        q_i, k_i, v_i = inp
        o_inter = jnp.einsum("bqhd,bhdv->bqhv", q_i, state) * decay_q[None, :, :, None]
        state = state * decay_chunk[None, :, None, None] + jnp.einsum("bkhd,kh,bkhv->bhdv", k_i, decay_k, v_i)
        return state, o_inter

    state0 = jnp.zeros((bsz, RET_HEADS, RET_QK_DIM, RET_V_DIM), jnp.float32)
    _, o_inter = lax.scan(step, state0, (qc, kc, vc))
    return (o_intra + o_inter).swapaxes(0, 1).reshape(bsz, seq, RET_HEADS, RET_V_DIM)

def retention_mixer(q, k, v, g, positions, ret_norm, w_out):
    bsz, seq = q.shape[0], q.shape[1]
    o = retention_core(q.reshape(bsz, seq, RET_HEADS, RET_QK_DIM),
                       k.reshape(bsz, seq, RET_HEADS, RET_QK_DIM),
                       v.reshape(bsz, seq, RET_HEADS, RET_V_DIM), positions)
    mu = jnp.mean(o, axis=-1, keepdims=True)
    var = jnp.mean(jnp.square(o - mu), axis=-1, keepdims=True)
    o = ((o - mu) * lax.rsqrt(var + EPS)).reshape(bsz, seq, RET_V) * ret_norm.astype(jnp.float32)
    o = o.astype(g.dtype)
    return (jax.nn.silu(g) * o) @ w_out

def hybrid_layer(x, positions, norm_mix, w_in, conv_w, w_conv_out, ret_norm, w_ret_out, w_o,
                 norm_mlp, w_up, w_down):
    h = rmsnorm(x, norm_mix)
    proj = h @ w_in
    split_points = np.cumsum(IN_SIZES)[:-1].tolist()
    cb, cc, cu, q, k, v, g, ga, gb = jnp.split(proj, split_points, axis=-1)
    y_conv = short_conv_mixer(cb, cc, cu, conv_w, w_conv_out)
    y_ret = retention_mixer(q, k, v, g, positions, ret_norm, w_ret_out)
    merged = jax.nn.sigmoid(ga) * y_conv + jax.nn.sigmoid(gb) * y_ret
    x = x + merged @ w_o
    h2 = rmsnorm(x, norm_mlp)
    return x + jnp.square(jax.nn.relu(h2 @ w_up)) @ w_down

def first_inputs(seed: int = 0) -> dict:
    key = jax.random.key(seed)
    ks = jax.random.split(key, 14)
    f32 = jnp.float32

    def dense(k, fan_in, fan_out):
        return jax.random.normal(k, (DEPTH, fan_in, fan_out), f32) * (fan_in ** -0.5)

    def gain(k, shape):
        return 1.0 + 0.02 * jax.random.normal(k, shape, f32)

    x = jax.random.normal(ks[0], (BATCH, SEQ, D_MODEL), f32)
    start = jax.random.randint(ks[1], (BATCH, 1), 0, MAX_START, dtype=jnp.int32)
    positions = (start + jnp.arange(SEQ, dtype=jnp.int32)[None, :]).astype(jnp.int32)
    return {
        "x": x,
        "positions": positions,
        "norm_mix": gain(ks[2], (DEPTH, D_MODEL)),
        "w_in": dense(ks[3], D_MODEL, D_IN),
        "conv_w": jax.random.normal(ks[4], (DEPTH, CONV_WIDTH, D_CONV), f32) * (CONV_WIDTH ** -0.5),
        "w_conv_out": dense(ks[5], D_CONV, D_MODEL),
        "ret_norm": gain(ks[6], (DEPTH, RET_V)),
        "w_ret_out": dense(ks[7], RET_V, D_MODEL),
        "w_o": dense(ks[8], D_MODEL, D_MODEL),
        "norm_mlp": gain(ks[9], (DEPTH, D_MODEL)),
        "w_up": dense(ks[10], D_MODEL, D_FF),
        "w_down": dense(ks[11], D_FF, D_MODEL),
        "norm_final": gain(ks[12], (D_MODEL,)),
    }

def first_block(x, positions, norm_mix, w_in, conv_w, w_conv_out, ret_norm, w_ret_out, w_o,
              norm_mlp, w_up, w_down, norm_final):
    for i in range(DEPTH):
        x = hybrid_layer(x, positions, norm_mix[i], w_in[i], conv_w[i], w_conv_out[i], ret_norm[i],
                         w_ret_out[i], w_o[i], norm_mlp[i], w_up[i], w_down[i])
    return rmsnorm(x, norm_final)


DEPTH_2 = 1

MEM_LEN = 256
NSA_HEADS = 8
NSA_KV_HEADS = 2
NSA_HEAD_DIM = 64
NSA_REP = NSA_HEADS // NSA_KV_HEADS
CMP_BLOCK = 32
CMP_STRIDE = 16
SEL_BLOCK = 64
N_SELECT = 16
WINDOW = 512
Q_BLOCK = 128
NSA_WIDTH = NSA_HEADS * NSA_HEAD_DIM
KV_WIDTH = NSA_KV_HEADS * NSA_HEAD_DIM
GMLP_WIDTH = 256
GMLP_GROUPS = 4
GMLP_CHUNK = 128
CONV_WIDTH_2 = 256
CONV_TAPS = 31
MIX_WIDTH = NSA_WIDTH + GMLP_WIDTH + CONV_WIDTH_2
IN_SPLITS = (NSA_WIDTH, KV_WIDTH, KV_WIDTH, KV_WIDTH, KV_WIDTH, KV_WIDTH, KV_WIDTH,
             NSA_HEADS * 3, 2 * GMLP_WIDTH, 2 * CONV_WIDTH_2)
IN_WIDTH = sum(IN_SPLITS)
XATTN_HEADS = 4
XATTN_HEAD_DIM = D_MODEL // XATTN_HEADS
D_FF_2 = 2816
FFN_CONV_TAPS = 3

NEG_INF = -1e30
TINY = 1e-30
FORCE = 1e4


def _split_cols(z, widths):
    outs, off = [], 0
    for w in widths:
        outs.append(z[..., off:off + w])
        off += w
    return outs

def rms_norm(x, g):
    xf = x.astype(jnp.float32)
    y = xf * lax.rsqrt(jnp.mean(xf * xf, axis=-1, keepdims=True) + EPS)
    return (y * g.astype(jnp.float32)).astype(x.dtype)

def layer_norm(x, g, b):
    xf = x.astype(jnp.float32)
    mu = jnp.mean(xf, axis=-1, keepdims=True)
    var = jnp.mean(jnp.square(xf - mu), axis=-1, keepdims=True)
    y = (xf - mu) * lax.rsqrt(var + EPS)
    return (y * g.astype(jnp.float32) + b.astype(jnp.float32)).astype(x.dtype)

def masked_softmax(s, mask):
    s = jnp.where(mask, s, NEG_INF)
    m = jnp.max(s, axis=-1, keepdims=True)
    e = jnp.where(mask, jnp.exp(s - m), 0.0)
    return e / jnp.maximum(jnp.sum(e, axis=-1, keepdims=True), TINY)

def causal_depthwise_conv(x, w, b):
    taps = w.shape[0]
    y = lax.conv_general_dilated(x, w[:, None, :], window_strides=(1,), padding=[(taps - 1, 0)],
                                 dimension_numbers=("NWC", "WIO", "NWC"),
                                 feature_group_count=x.shape[-1])
    return y + b

def _to_heads(z, n):
    b, s, _ = z.shape
    return z.reshape(b, s, n, NSA_HEAD_DIM).transpose(0, 2, 1, 3)

def compress_blocks(kv, pe, w1, w2):
    b, g, s, dh = kv.shape
    n_cmp = (s - CMP_BLOCK) // CMP_STRIDE + 1
    idx = jnp.arange(n_cmp)[:, None] * CMP_STRIDE + jnp.arange(CMP_BLOCK)[None, :]
    blocks = kv[:, :, idx, :] + pe
    flat = blocks.reshape(b, g, n_cmp, CMP_BLOCK * dh)
    return jax.nn.gelu(flat @ w1) @ w2

def nsa_mixer(q, k_c_raw, v_c_raw, k_s, v_s, k_w, v_w, gate_logits, cmp_pe, cmp_w1, cmp_w2):
    b, s, _ = q.shape
    dh, G, R = NSA_HEAD_DIM, NSA_KV_HEADS, NSA_REP
    scale = dh ** -0.5
    k_cmp = compress_blocks(_to_heads(k_c_raw, G), cmp_pe[0], cmp_w1[0], cmp_w2[0])
    v_cmp = compress_blocks(_to_heads(v_c_raw, G), cmp_pe[1], cmp_w1[1], cmp_w2[1])
    n_cmp = k_cmp.shape[2]
    cmp_end = jnp.arange(n_cmp) * CMP_STRIDE + CMP_BLOCK - 1
    n_slc = s // SEL_BLOCK
    k_sel = min(N_SELECT, n_slc)
    k_slc_b = _to_heads(k_s, G).reshape(b, G, n_slc, SEL_BLOCK, dh)
    v_slc_b = _to_heads(v_s, G).reshape(b, G, n_slc, SEL_BLOCK, dh)
    ci = jnp.arange(n_cmp)[:, None] * CMP_STRIDE
    sj = jnp.arange(n_slc)[None, :] * SEL_BLOCK
    overlap = ((ci < sj + SEL_BLOCK) & (ci + CMP_BLOCK > sj)).astype(jnp.float32)
    pad = ((0, 0), (0, 0), (WINDOW, 0), (0, 0))
    k_win_p = jnp.pad(_to_heads(k_w, G), pad)
    v_win_p = jnp.pad(_to_heads(v_w, G), pad)
    nb = s // Q_BLOCK
    q_blocks = q.reshape(b, nb, Q_BLOCK, G, R, dh).transpose(1, 0, 3, 4, 2, 5)
    gather = jax.vmap(jax.vmap(lambda kb, ix: kb[ix]))

    def block_fn(args):
        qb, bi = args
        t = bi * Q_BLOCK + jnp.arange(Q_BLOCK)
        s_c = jnp.einsum("bgrtd,bgnd->bgrtn", qb, k_cmp).astype(jnp.float32) * scale
        p_c = masked_softmax(s_c, cmp_end[None, :] <= t[:, None])
        o_c = jnp.einsum("bgrtn,bgnd->bgrtd", p_c.astype(v_cmp.dtype), v_cmp)
        imp = jnp.einsum("bgtn,nj->bgtj", jnp.sum(p_c, axis=2), overlap)
        cur = (t // SEL_BLOCK)[:, None]
        jj = jnp.arange(n_slc)[None, :]
        forced = (jj == 0) | (jj == cur) | (jj == cur - 1)
        imp = jnp.where(forced, FORCE, imp)
        imp = jnp.where(jj <= cur, imp, -FORCE)
        _, sel = lax.top_k(imp, k_sel)
        gk = gather(k_slc_b, sel).reshape(b, G, Q_BLOCK, k_sel * SEL_BLOCK, dh)
        gv = gather(v_slc_b, sel).reshape(b, G, Q_BLOCK, k_sel * SEL_BLOCK, dh)
        kpos = (sel[..., None] * SEL_BLOCK + jnp.arange(SEL_BLOCK)).reshape(b, G, Q_BLOCK, k_sel * SEL_BLOCK)
        mask_s = (kpos <= t[None, None, :, None])[:, :, None]
        s_s = jnp.einsum("bgrtd,bgtmd->bgrtm", qb, gk).astype(jnp.float32) * scale
        p_s = masked_softmax(s_s, mask_s)
        o_s = jnp.einsum("bgrtm,bgtmd->bgrtd", p_s.astype(gv.dtype), gv)
        kw = lax.dynamic_slice_in_dim(k_win_p, bi * Q_BLOCK, Q_BLOCK + WINDOW, axis=2)
        vw = lax.dynamic_slice_in_dim(v_win_p, bi * Q_BLOCK, Q_BLOCK + WINDOW, axis=2)
        kp = (bi * Q_BLOCK - WINDOW + jnp.arange(Q_BLOCK + WINDOW))[None, :]
        mask_w = (kp <= t[:, None]) & (kp > t[:, None] - WINDOW) & (kp >= 0)
        s_w = jnp.einsum("bgrtd,bgkd->bgrtk", qb, kw).astype(jnp.float32) * scale
        p_w = masked_softmax(s_w, mask_w)
        o_w = jnp.einsum("bgrtk,bgkd->bgrtd", p_w.astype(vw.dtype), vw)
        return o_c, o_s, o_w

    o_c, o_s, o_w = lax.map(block_fn, (q_blocks, jnp.arange(nb)))
    def unblock(o):
        return o.transpose(1, 0, 4, 2, 3, 5).reshape(b, s, NSA_HEADS, dh)
    gates = jax.nn.sigmoid(gate_logits.reshape(b, s, NSA_HEADS, 3))
    o = (gates[..., 0:1] * unblock(o_c) + gates[..., 1:2] * unblock(o_s)
         + gates[..., 2:3] * unblock(o_w))
    return o.reshape(b, s, NSA_WIDTH)

def gmlp_mixer(z, ln_g, ln_b, w_s, b_s):
    b, s, _ = z.shape
    z = jax.nn.gelu(z)
    u, v = z[..., :GMLP_WIDTH], z[..., GMLP_WIDTH:]
    v = layer_norm(v, ln_g, ln_b)
    nc = s // GMLP_CHUNK
    v = v.reshape(b, nc, GMLP_CHUNK, GMLP_GROUPS, GMLP_WIDTH // GMLP_GROUPS)
    causal = jnp.tril(jnp.ones((GMLP_CHUNK, GMLP_CHUNK), dtype=w_s.dtype))
    mixed = jnp.einsum("gts,bcsgd->bctgd", w_s * causal, v) + b_s.T[:, :, None]
    return u * mixed.reshape(b, s, GMLP_WIDTH)

def conformer_conv_mixer(z, dw_w, dw_b, ln_g, ln_b):
    a, gt = z[..., :CONV_WIDTH_2], z[..., CONV_WIDTH_2:]
    h = a * jax.nn.sigmoid(gt)
    h = causal_depthwise_conv(h, dw_w, dw_b)
    h = layer_norm(h, ln_g, ln_b)
    return jax.nn.silu(h)

def memory_cross_attention(x, mem, g_x, g_m, wq, wk, wv, wo):
    b, s, _ = x.shape
    h = rms_norm(x, g_x)
    m = rms_norm(mem, g_m)
    q = (h @ wq).reshape(b, s, XATTN_HEADS, XATTN_HEAD_DIM)
    k = (m @ wk).reshape(b, m.shape[1], XATTN_HEADS, XATTN_HEAD_DIM)
    v = (m @ wv).reshape(b, m.shape[1], XATTN_HEADS, XATTN_HEAD_DIM)
    sc = jnp.einsum("bshd,bmhd->bhsm", q, k).astype(jnp.float32) * (XATTN_HEAD_DIM ** -0.5)
    p = jax.nn.softmax(sc, axis=-1)
    o = jnp.einsum("bhsm,bmhd->bshd", p.astype(v.dtype), v).reshape(b, s, D_MODEL)
    return o @ wo

def conv_ffn(x, g, w_up, dw_w, dw_b, w_down):
    h = causal_depthwise_conv(rms_norm(x, g) @ w_up, dw_w, dw_b)
    gate, up = h[..., :D_FF_2], h[..., D_FF_2:]
    return (jax.nn.silu(gate) * up) @ w_down

def second_inputs(seed: int = 0) -> dict:
    key = jax.random.key(seed)
    ks = iter(jax.random.split(key, 40))
    def nrm(shape, scale):
        return jax.random.normal(next(ks), shape, jnp.float32) * scale
    def gain(shape):
        return 1.0 + 0.02 * jax.random.normal(next(ks), shape, jnp.float32)
    L, dh = DEPTH_2, NSA_HEAD_DIM
    return {
        "x": nrm((BATCH, SEQ, D_MODEL), 1.0),
        "mem": nrm((BATCH, MEM_LEN, D_MODEL), 1.0),
        "mix_norm_g": gain((L, D_MODEL)),
        "w_in": nrm((L, D_MODEL, IN_WIDTH), D_MODEL ** -0.5),
        "cmp_pe": nrm((L, 2, CMP_BLOCK, dh), 0.1),
        "cmp_w1": nrm((L, 2, CMP_BLOCK * dh, dh), (CMP_BLOCK * dh) ** -0.5),
        "cmp_w2": nrm((L, 2, dh, dh), dh ** -0.5),
        "gmlp_ln_g": gain((L, GMLP_WIDTH)),
        "gmlp_ln_b": nrm((L, GMLP_WIDTH), 0.02),
        "gmlp_ws": nrm((L, GMLP_GROUPS, GMLP_CHUNK, GMLP_CHUNK), GMLP_CHUNK ** -0.5),
        "gmlp_bs": gain((L, GMLP_GROUPS, GMLP_CHUNK)),
        "conv_dw_w": nrm((L, CONV_TAPS, CONV_WIDTH_2), CONV_TAPS ** -0.5),
        "conv_dw_b": nrm((L, CONV_WIDTH_2), 0.02),
        "conv_ln_g": gain((L, CONV_WIDTH_2)),
        "conv_ln_b": nrm((L, CONV_WIDTH_2), 0.02),
        "mix_out_g": gain((L, MIX_WIDTH)),
        "w_out": nrm((L, MIX_WIDTH, D_MODEL), MIX_WIDTH ** -0.5),
        "xattn_norm_g": gain((L, D_MODEL)),
        "mem_norm_g": gain((L, D_MODEL)),
        "xattn_wq": nrm((L, D_MODEL, D_MODEL), D_MODEL ** -0.5),
        "xattn_wk": nrm((L, D_MODEL, D_MODEL), D_MODEL ** -0.5),
        "xattn_wv": nrm((L, D_MODEL, D_MODEL), D_MODEL ** -0.5),
        "xattn_wo": nrm((L, D_MODEL, D_MODEL), D_MODEL ** -0.5),
        "ffn_norm_g": gain((L, D_MODEL)),
        "ffn_w_up": nrm((L, D_MODEL, 2 * D_FF_2), D_MODEL ** -0.5),
        "ffn_dw_w": nrm((L, FFN_CONV_TAPS, 2 * D_FF_2), FFN_CONV_TAPS ** -0.5),
        "ffn_dw_b": nrm((L, 2 * D_FF_2), 0.02),
        "ffn_w_down": nrm((L, D_FF_2, D_MODEL), D_FF_2 ** -0.5),
        "final_norm_g": gain((D_MODEL,)),
    }

def second_block(x, mem, mix_norm_g, w_in, cmp_pe, cmp_w1, cmp_w2, gmlp_ln_g, gmlp_ln_b, gmlp_ws,
              gmlp_bs, conv_dw_w, conv_dw_b, conv_ln_g, conv_ln_b, mix_out_g, w_out,
              xattn_norm_g, mem_norm_g, xattn_wq, xattn_wk, xattn_wv, xattn_wo,
              ffn_norm_g, ffn_w_up, ffn_dw_w, ffn_dw_b, ffn_w_down, final_norm_g):
    for l in range(DEPTH_2):
        z = rms_norm(x, mix_norm_g[l]) @ w_in[l]
        (q, kc, vc, ks, vs, kw, vw, gl, zg, zc) = _split_cols(z, IN_SPLITS)
        y_nsa = nsa_mixer(q, kc, vc, ks, vs, kw, vw, gl, cmp_pe[l], cmp_w1[l], cmp_w2[l])
        y_gmlp = gmlp_mixer(zg, gmlp_ln_g[l], gmlp_ln_b[l], gmlp_ws[l], gmlp_bs[l])
        y_conv = conformer_conv_mixer(zc, conv_dw_w[l], conv_dw_b[l], conv_ln_g[l], conv_ln_b[l])
        g_nsa, g_gmlp, g_conv = _split_cols(mix_out_g[l], (NSA_WIDTH, GMLP_WIDTH, CONV_WIDTH_2))
        y = jnp.concatenate([rms_norm(y_nsa, g_nsa), rms_norm(y_gmlp, g_gmlp),
                             rms_norm(y_conv, g_conv)], axis=-1)
        x = x + y @ w_out[l]
        x = x + memory_cross_attention(x, mem, xattn_norm_g[l], mem_norm_g[l], xattn_wq[l],
                                       xattn_wk[l], xattn_wv[l], xattn_wo[l])
        x = x + conv_ffn(x, ffn_norm_g[l], ffn_w_up[l], ffn_dw_w[l], ffn_dw_b[l], ffn_w_down[l])
    return rms_norm(x, final_norm_g)


def setup_inputs(seed=0):
    out = dict(first_inputs(seed))
    for name, value in second_inputs(seed + 1).items():
        if name != "x":
            out[name + "_2"] = value
    return out


def reference(
    x, positions, norm_mix, w_in, conv_w, w_conv_out, ret_norm, w_ret_out, w_o, norm_mlp, w_up,
    w_down, norm_final, mem_2, mix_norm_g_2, w_in_2, cmp_pe_2, cmp_w1_2, cmp_w2_2, gmlp_ln_g_2,
    gmlp_ln_b_2, gmlp_ws_2, gmlp_bs_2, conv_dw_w_2, conv_dw_b_2, conv_ln_g_2, conv_ln_b_2,
    mix_out_g_2, w_out_2, xattn_norm_g_2, mem_norm_g_2, xattn_wq_2, xattn_wk_2, xattn_wv_2,
    xattn_wo_2, ffn_norm_g_2, ffn_w_up_2, ffn_dw_w_2, ffn_dw_b_2, ffn_w_down_2, final_norm_g_2,
):
    x = first_block(
        x, positions, norm_mix, w_in, conv_w, w_conv_out, ret_norm, w_ret_out, w_o, norm_mlp,
        w_up, w_down, norm_final,
    )
    return second_block(
        x, mem_2, mix_norm_g_2, w_in_2, cmp_pe_2, cmp_w1_2, cmp_w2_2, gmlp_ln_g_2, gmlp_ln_b_2,
        gmlp_ws_2, gmlp_bs_2, conv_dw_w_2, conv_dw_b_2, conv_ln_g_2, conv_ln_b_2, mix_out_g_2,
        w_out_2, xattn_norm_g_2, mem_norm_g_2, xattn_wq_2, xattn_wk_2, xattn_wv_2, xattn_wo_2,
        ffn_norm_g_2, ffn_w_up_2, ffn_dw_w_2, ffn_dw_b_2, ffn_w_down_2, final_norm_g_2,
    )


_drawn_inputs = setup_inputs


def setup_inputs(seed=0):
    import zlib

    import numpy as np

    out = dict(_drawn_inputs(seed))
    spreads = {}
    factors = {'ret_norm': 6.43,
     'mix_norm_g_2': 3.499,
     'gmlp_ln_g_2': 8.0,
     'gmlp_ln_b_2': 8.0,
     'gmlp_bs_2': 8.0,
     'conv_dw_b_2': 3.565,
     'conv_ln_g_2': 6.051,
     'conv_ln_b_2': 7.83,
     'mix_out_g_2': 3.609,
     'xattn_norm_g_2': 8.0,
     'mem_norm_g_2': 8.0,
     'ffn_norm_g_2': 4.938,
     'ffn_dw_b_2': 4.994,
     'final_norm_g_2': 2.913}
    for name, (base, spread) in spreads.items():
        noise = np.random.default_rng([zlib.crc32(name.encode()), seed]).standard_normal(out[name].shape)
        drawn = base * np.exp(spread * noise) if base else spread * noise
        out[name] = __import__('jax').numpy.asarray(drawn.astype(out[name].dtype))
    for name, factor in factors.items():
        out[name] = (out[name] * factor).astype(out[name].dtype)
    return out
```

```python
from contextlib import ExitStack

import numpy as np

import concourse.bass as bass
from concourse import mybir

F32 = mybir.dt.float32
F32R = mybir.dt.float32r
I32 = mybir.dt.int32
ALU = mybir.AluOpType
ACT = mybir.ActivationFunctionType
AX = mybir.AxisListType.X

P = 128
T = 512
D = 1024
KB = D // P
NC = T // P
LAYERS = 2
HEADS = 4
DV = 256
EPS = 1e-6
PANEL = KB * P
TWO_PI = 2 * np.pi
PI_1 = np.float32(6.28125)
PI_2 = np.float32(np.float64(TWO_PI) - np.float64(PI_1))
PI_3 = np.float32(np.float64(TWO_PI) - np.float64(PI_1) - np.float64(PI_2))
ROUND = np.float32(1.5 * 2 ** 23)
PI_UNDER = float(np.nextafter(np.float32(np.pi), np.float32(0)))

QK, VV, CC, CU, CB, G, GA, CONV, GB, RET, WO = 0, 8, 16, 24, 32, 40, 48, 56, 64, 72, 80
UP0, UP1, DN0, UP2, DN1, UP3, DN2, DN3 = 88, 96, 104, 112, 120, 128, 136, 144
UNITS = 152
LAYER_SPLITS = 72
LAYER_SRC = 48
W_IN_COL = {QK: 3 * D, VV: 4 * D, CC: D, CU: 2 * D, CB: 0, G: 5 * D, GA: 6 * D, GB: 7 * D}
U2 = LAYERS * UNITS
NSA_HEADS, NSA_KV, HD, REP = 8, 2, 64, 4
CMP_BLOCK, CMP_STRIDE = 32, 16
N_CMP = (T - CMP_BLOCK) // CMP_STRIDE + 1
TAPS, FFN_TAPS = 31, 3
MEM = 256
XH = 4
F2 = 2816
FB = F2 // P
KV0 = NSA_HEADS * HD
GATES = 3 * NSA_HEADS
GL0 = KV0 + 6 * P
ZG0 = GL0 + GATES
ZC0 = ZG0 + T
Z_COLS = [KV0 + i * P for i in range(6)] + [i * P for i in range(4)] + [GL0] + [ZG0 + i * P for i in range(4)] + [ZC0 + i * P for i in range(4)]
Z_Q, Z_GL, Z_U, Z_V, Z_A, Z_GT = 6, 10, 11, 13, 15, 17
NZ = len(Z_COLS)
MK = U2 + NZ
MV = MK + KB
OUT = MV + KB
XQ = OUT + KB
XO = XQ + KB
FFN = XO + KB
GROUPS = [(0, 8), (8, 8), (16, FB - 16)]
UPG = [FFN, FFN + 16, FFN + 40]
DNG = [FFN + 32, FFN + 52, FFN + 60]
U_END = FFN + 68
ITS = [(c, g) for c in range(NC) for g in range(NSA_KV)]
TINY = 1e-30
C2_LOADS = 23
NEG = -1e30
S_COLS = [T - P * j for j in range(NC)]
S_AT = [(0, 0), (1, 0), (2, 0), (1, S_COLS[1])]
P_AT = [sum(S_COLS[:j]) for j in range(NC)]


def layer_stack_kernel(nc, d, out):
    ctx = ExitStack()
    with ctx:
        def sb(name, shape, dt=F32):
            return ctx.enter_context(nc.sbuf_tensor(name, shape, dt))

        def sem(name):
            return ctx.enter_context(nc.semaphore(name))

        x = sb("x", [P, KB * T])
        raw = [sb(f"raw{i}", [P, KB, P]) for i in range(2)]
        wh = [sb(f"wh{i}", [P, KB, P], F32R) for i in range(4)]
        wl = [sb(f"wl{i}", [P, KB, P], F32R) for i in range(4)]
        with nc.sbuf_tensor("a_f32", [P, 2 * KB * T], F32) as a_f32:
            af = a_f32
        ah, al = sb("ah", [P, KB * T], F32R), sb("al", [P, KB * T], F32R)
        with nc.sbuf_tensor("b_f32", [P, 2 * KB * T], F32) as b_f32:
            bf = b_f32
        bh, bl = sb("bh", [P, KB * T], F32R), sb("bl", [P, KB * T], F32R)
        with nc.sbuf_tensor("c_f32", [P, 2 * KB * T], F32) as c_f32:
            cf = c_f32
        ch, cl = sb("ch", [P, KB * T], F32R), sb("cl", [P, KB * T], F32R)
        d1, d2 = sb("d1", [P, KB * T]), sb("d2", [P, KB * T])
        with (nc.sbuf_tensor("decay_t", [P, HEADS * T], F32) as decay_t, nc.sbuf_tensor("cos_t", [P, T], F32) as cos_t,
              nc.sbuf_tensor("sin_t", [P, T], F32) as sin_t):
            decay, cos, sin = decay_t, cos_t, sin_t
        hp = [sb(f"hp{i}", [P, TAPS - 1 + T]) for i in range(2)]
        ln_rows = sb("ln_rows", [P, 2, DV])
        diag = sb("diag", [P, P])
        tril = sb("tril", [P, P])
        cmp_add, cmp_keep = sb("cmp_add", [P, NC, N_CMP]), sb("cmp_keep", [P, NC, N_CMP])
        k_cmp = [sb(f"k_cmp{g}", [P, N_CMP]) for g in range(NSA_KV)]
        v_cmp = sb("v_cmp", [N_CMP, NSA_KV, HD])
        cmp_hid = [sb(f"cmp_hid{i}", [P, N_CMP]) for i in range(2)]
        cmp_w2 = [sb(f"cmp_w2{i}", [P, HD]) for i in range(2)]
        cmp_pe = [sb(f"cmp_pe{i}", [P, CMP_BLOCK]) for i in range(2)]
        gates = sb("gates", [P, NC, GATES])
        gains2 = sb("gains2", [P, 6, KB])
        conv_taps = sb("conv_taps", [P, TAPS + 3, 2])
        ffn_taps = sb("ffn_taps", [P, FFN_TAPS + 1, 2 * FB])
        p_cmp = sb("p_cmp", [P, REP, N_CMP])
        row = sb("row", [P, 12, REP])
        bn = sb("bn", [P, NC, 6])
        mv = sb("mv", [P, NC, 2])
        mem_ms = sb("mem_ms", [P, 2])
        one_row = sb("one_row", [1, HD])
        rstd = sb("rstd", [P, T])
        tmp = [sb(f"tmp{i}", [P, T]) for i in range(2)]
        tmp2 = sb("tmp2", [P, T])
        ident = sb("ident", [P, P])
        mean_d = sb("mean_d", [P, P])
        mean_v = sb("mean_v", [P, P])
        mean_n = sb("mean_n", [P, P])
        gains = sb("gains", [P, 2 * LAYERS + 1, KB])
        conv_w = sb("conv_w", [P, LAYERS * 3, KB])
        ret_g = sb("ret_g", [P, LAYERS, KB])
        inv_freq = sb("inv_freq", [P, 1])
        eps = sb("eps", [P, 1])

        acc, sq, rstd2 = d2[:, 0:T], d2[:, T:2 * T], d2[:, 2 * T:3 * T]
        cos_r, sin_r = d2[:, 3 * T:4 * T], d2[:, 4 * T:5 * T]
        p_dec = [d1[:, 1280 * i:1280 * (i + 1)] for i in range(2)]
        o_blk = [d1[:, 2560 + T * i:2560 + T * (i + 1)] for i in range(2)]
        o_sum = d1[:, 2560 + 2 * T:2560 + 3 * T]
        v_tok = cf[:, KB * T:2 * KB * T].rearrange("p (c v) -> p c v", c=NC)

        q_t = [cf[:, f * T:(f + 1) * T] for f in range(4)]
        k_att = [[cf[:, (4 + 2 * b + g) * T:(5 + 2 * b + g) * T] for g in range(2)] for b in range(2)]
        v_att = [cf[:, (8 + b) * T:(9 + b) * T].rearrange("p (c v) -> p c v", c=NC) for b in range(2)]
        cmp_in = [cf[:, (10 + i) * T:(11 + i) * T] for i in range(2)]
        v_ln = cf[:, 10 * T:12 * T].rearrange("p (c v) -> p c v", c=NC)
        gm_u = [cf[:, (12 + i) * T:(13 + i) * T] for i in range(2)]
        cv_a = [cf[:, (14 + i) * T:(15 + i) * T] for i in range(2)]
        cmp_w1 = [d1[:, i * 2048:(i + 1) * 2048].rearrange("p (n j) -> p n j", j=HD) for i in range(2)]
        cmp_win = [d2[:, i * 1024:i * 1024 + CMP_BLOCK * N_CMP].rearrange("p (n b) -> p n b", b=N_CMP) for i in range(2)]
        y_nsa = [d2[:, f * T:(f + 1) * T] for f in range(4)]
        y_gm = [d2[:, (4 + f) * T:(5 + f) * T] for f in range(2)]
        y_cv = [d2[:, (6 + f) * T:(7 + f) * T] for f in range(2)]
        gm_ws, gm_wt = d2[:, 6 * T:7 * T], d2[:, 7 * T:8 * T]
        p_att = [af[:, b * 2048:(b + 1) * 2048].rearrange("p (r k) -> p r k", r=REP) for b in range(2)]
        pt_att = [af[:, (2 + b) * 2048:(3 + b) * 2048] for b in range(2)]
        mem_k = bf[:, 4 * T:8 * T]
        mem_v = bf[:, 12 * T:16 * T].rearrange("p (c v) -> p c v", c=2)
        mem_raw = bf[:, 12 * T:16 * T].rearrange("p (c f) -> p c f", c=2)
        memh, meml = bh[:, 0:4 * T], bl[:, 0:4 * T]
        part_r = [d1[:, i * T:(i + 1) * T] for i in range(3)]
        part_acc = [d1[:, (3 + i) * T:(4 + i) * T] for i in range(3)]
        part_sq = d1[:, 6 * T:7 * T]
        xq_t = [d1[:, f * T:(f + 1) * T] for f in range(KB)]
        x_p = cf[:, 0:1024].rearrange("p (h m) -> p h m", h=XH)
        x_pt = d2[:].rearrange("p (m h q) -> p m h q", m=2, h=XH)

        unit_ps = [ctx.enter_context(nc.psum_tensor(f"unit_ps{i}", [P, T], F32)) for i in range(2)]
        aux = ctx.enter_context(nc.psum_tensor("aux", [P, 4, T], F32))
        o_banks = ctx.enter_context(nc.psum_tensor("o_banks", [P, 2, T], F32))
        o_ps = [o_banks[:, i] for i in range(2)]
        stat_ps = aux[:, 3]

        raw_in = [sem(f"raw_in{i}") for i in range(2)]
        w_hi, w_lo, mm, evac = sem("w_hi"), sem("w_lo"), sem("mm"), sem("evac")
        x_in, const_in, pos_in = sem("x_in"), sem("const_in"), sem("pos_in")
        ones_set = sem("ones_set")
        x_tr, x_src = sem("x_tr"), sem("x_src")
        in_src, in_hi, in_lo = sem("in_src"), sem("in_hi"), sem("in_lo")
        sq_done, ssq_src, ssq_mm, std_done = sem("sq_done"), sem("ssq_src"), sem("ssq_mm"), sem("std_done")
        ang_done, trig_done = sem("ang_done"), sem("trig_done")
        dve_step = sem("dve_step")
        qk_done, v_tr, v_done = sem("qk_done"), sem("v_tr"), sem("v_done")
        tap_done, gate_done = sem("tap_done"), sem("gate_done")
        s_done, p_done, pv_done, o_out = sem("s_done"), sem("p_done"), sem("pv_done"), sem("o_out")
        o_sum_done, mean_done, cen_done = sem("o_sum_done"), sem("mean_done"), sem("cen_done")
        o_sq, o_sq_sum, var_done, o_std, y_done = (sem("o_sq"), sem("o_sq_sum"), sem("var_done"), sem("o_std"),
                                                   sem("y_done"))
        c2_in, mem_in = sem("c2_in"), sem("mem_in")
        x2_src = sem("x2_src")
        win_done, att_v, z_act, gate_tok = sem("win_done"), sem("att_v"), sem("z_act"), sem("gate_tok")
        z_tr, cmp_mm, cmp_gelu, cmp_out = sem("z_tr"), sem("cmp_mm"), sem("cmp_gelu"), sem("cmp_out")
        gm_tr, gm_var, gm_std, gm_ready, ws_ready, mix_mm, mixed = (sem("gm_tr"), sem("gm_var"), sem("gm_std"), sem("gm_ready"),
                                                             sem("ws_ready"), sem("mix_mm"), sem("mixed"))
        mem_sq, mem_rms, mem_scaled, mem_tr, mem_hi, mem_lo = (sem("mem_sq"), sem("mem_rms"), sem("mem_scaled"), sem("mem_tr"),
                                                               sem("mem_hi"), sem("mem_lo"))
        s_att, s_cmp, shift_att, shift_cmp = sem("s_att"), sem("s_cmp"), sem("shift_att"), sem("shift_cmp")
        exp_att, exp_cmp, p_ready, pc_ready = sem("exp_att"), sem("exp_cmp"), sem("p_ready"), sem("pc_ready")
        t_att, pt_ready, o_att, o_taken = sem("t_att"), sem("pt_ready"), sem("o_att"), sem("o_taken")
        cv_sum, cv_mean, cv_cen, cv_sq, cv_sqs, cv_var, cv_std, cv_n, cv_y = (sem(n) for n in (
            "cv_sum", "cv_mean", "cv_cen", "cv_sq", "cv_sqs", "cv_var", "cv_std", "cv_n", "cv_y"))
        part_src, part_sqd, part_sum, part_ms, part_std = (sem(n) for n in ("part_src", "part_sqd", "part_sum", "part_ms", "part_std"))
        src2 = sem("src2")
        xs_mm, xs_shift, x_exp, xp_ready, xt_mm, xt_copy, xo_mm = (sem(n) for n in (
            "xs_mm", "xs_shift", "x_exp", "xp_ready", "xt_mm", "xt_copy", "xo_mm"))
        ffn_src, ffn_tap, ffn_pre, ffn_silu = sem("ffn_src"), sem("ffn_tap"), sem("ffn_pre"), sem("ffn_silu")
        fin_x, fin_tr, fin_cp = sem("fin_x"), sem("fin_tr"), sem("fin_cp")
        out_st = sem("out_st")
        dve_begun, pe_begun = sem("dve_begun"), sem("pe_begun")

        block = ctx.enter_context(nc.Block())

        def blk(t, f):
            return t[:, bass.ds(f * T, T)]

        def units(eng, n, body):
            with eng.Fori(0, n // 4) as i:
                for j in range(4):
                    body(i * 4 + j, j)

        @block.sync
        def _(sp):
            sp.dma_start(d1[:].rearrange("p (c f) -> p c f", c=NC), d["x"].rearrange("(c p) f -> p c f", p=P)).then_inc(x_in, 16)
            w_in = d["w_in"].rearrange("l (k p) f -> p (l k) f", p=P)
            w_sq = {n: d[n].rearrange("l (k p) f -> p (l k) f", p=P) for n in ("w_conv_out", "w_ret_out", "w_o", "w_up", "w_down")}

            with sp.Fori(0, LAYERS) as l:
                def load(first, src, k0, col, n=KB):
                    def body(f, j):
                        u = l * UNITS + first + f
                        sp.wait_ge(w_lo, u + 1)
                        sp.dma_start(raw[j % 2][:], src[:, bass.ds(k0, KB), bass.ds(f * P + col, P)]).then_inc(raw_in[j % 2], 16)
                    units(sp, n, body)

                k_l = l * KB
                for first, col, n in ((QK, W_IN_COL[QK], 16), (CC, W_IN_COL[CC], 16), (CB, W_IN_COL[CB], 8), (G, W_IN_COL[G], 16)):
                    load(first, w_in, k_l, col, n)
                load(CONV, w_sq["w_conv_out"], k_l, 0)
                load(GB, w_in, k_l, W_IN_COL[GB])
                load(RET, w_sq["w_ret_out"], k_l, 0)
                load(WO, w_sq["w_o"], k_l, 0)
                for first, g in ((UP0, 0), (UP1, 1), (DN0, 0), (UP2, 2), (DN1, 1), (UP3, 3), (DN2, 2), (DN3, 3)):
                    if first in (UP0, UP1, UP2, UP3):
                        load(first, w_sq["w_up"], k_l, g * D)
                    else:
                        load(first, w_sq["w_down"], l * 4 * KB + g * KB, 0)

            def load2(u, src, col, n_col=P, k0=0, n_k=KB):
                sp.wait_ge(w_lo, u + 1)
                sp.dma_start(raw[u % 2][:, 0:n_k, 0:n_col], src[:, k0:k0 + n_k, col:col + n_col]).then_inc(raw_in[u % 2], 16)

            def load_units(u0, n, src, col, step=P):
                with sp.Fori(0, n // 4) as i:
                    for j in range(4):
                        u = u0 + j
                        sp.wait_ge(w_lo, i * 4 + (u + 1))
                        sp.dma_start(raw[u % 2][:], src[:, :, bass.ds(i * (4 * step) + (col + j * step), P)]).then_inc(raw_in[u % 2], 16)

            v2 = {n: d[n].rearrange("(k p) f -> p k f", p=P) for n in ("w_in_2", "w_out_2", "wq_2", "wk_2", "wv_2", "wo_2", "up_2", "down_2")}
            for f, col in enumerate(Z_COLS):
                load2(U2 + f, v2["w_in_2"], col)
            for first, name in ((MK, "wk_2"), (MV, "wv_2"), (OUT, "w_out_2"), (XQ, "wq_2"), (XO, "wo_2")):
                load_units(first, KB, v2[name], 0)

            def load_pairs(u0, b0, n):
                with sp.Fori(0, n // 2) as i:
                    for j in range(4):
                        u = u0 + j
                        sp.wait_ge(w_lo, i * 4 + (u + 1))
                        sp.dma_start(raw[u % 2][:], v2["up_2"][:, :, bass.ds(i * (2 * P) + ((j % 2) * F2 + (b0 + j // 2) * P), P)]).then_inc(raw_in[u % 2], 16)

            def load_down(u0, b0, n):
                with sp.Fori(0, 2) as i:
                    for j in range(4):
                        u = u0 + j
                        sp.wait_ge(w_lo, i * 4 + (u + 1))
                        sp.dma_start(raw[u % 2][:, 0:n], v2["down_2"][:, b0:b0 + n, bass.ds(i * (4 * P) + j * P, P)]).then_inc(raw_in[u % 2], 16)
            load_pairs(UPG[0], *GROUPS[0])
            load_pairs(UPG[1], *GROUPS[1])
            load_down(DNG[0], *GROUPS[0])
            load_pairs(UPG[2], *GROUPS[2])
            load_down(DNG[1], *GROUPS[1])
            load_down(DNG[2], *GROUPS[2])

        @block.gpsimd
        def _(pool):
            pool.memset(eps[:], EPS)
            pool.memset(mean_d[:], 1.0 / D)
            pool.memset(mean_n[:], 1.0 / (NSA_HEADS * HD))
            pool.memset(mean_v[:], 1.0 / DV).then_inc(ones_set, 1)
            pool.sem_inc(w_lo, 2)

            def body(u, j):
                pool.wait_ge(w_hi, u + 1)
                pool.tensor_tensor(wl[j][:], raw[j % 2][:], wh[j][:].bitcast(F32), ALU.subtract).then_inc(w_lo, 1)
            units(pool, U_END // 4 * 4, body)
            for u in range(U_END // 4 * 4, U_END):
                body(u, u % 4)

        @block.scalar
        def _(act):
            for name, tile in (("gains", gains), ("conv_w", conv_w), ("ret_norm", ret_g)):
                act.dma_start(tile[:], d[name].rearrange("l (k p) -> p l k", p=P), allow_slow_non_contiguous=True).then_inc(const_in, 16)
            act.dma_start(tmp2[:].bitcast(I32), d["positions"].to_broadcast([P, T])).then_inc(pos_in, 16)
            for name, tile in (("inv_freq", inv_freq), ("ident", ident), ("decay", decay)):
                act.dma_start(tile[:], d[name]).then_inc(const_in, 16)
            act.sem_inc(gate_done, 2)

            def split_w(u, j):
                act.wait_ge(raw_in[j % 2], 16 * 1 + (u - j % 2) * 8)
                act.activation(wh[j][:], raw[j % 2][:], ACT.Copy).then_inc(w_hi, 1)

            for u in range(4):
                split_w(u, u)
            act.wait_ge(const_in, 16 * 6)
            act.wait_ge(ones_set, 1)

            def split_norm(src, g, k):
                act.activation(blk(ah if g[0] == "a" else bh, k), src, ACT.Copy, scale=g[1]).then_inc(in_hi, 1)
                act.activation(sq, src, ACT.Square).then_inc(sq_done, 1)

            for k in range(KB):
                act.wait_ge(x_src, k + 1)
                split_norm(blk(x, k), ("a", gains[:, 0, k:k + 1]), k)
            act.wait_ge(ang_done, 1)
            act.activation(sin[:], sin[:], ACT.Sin).then_inc(trig_done, 1)
            act.activation(cos[:], cos[:], ACT.Sin).then_inc(trig_done, 1)

            def sqrt_ms(n):
                act.wait_ge(ssq_mm, n)
                act.activation(rstd[:], stat_ps, ACT.Sqrt, bias=eps[:, 0:1]).then_inc(std_done, 1)

            with act.Fori(0, LAYERS) as l:
                u0 = l * UNITS

                def ahead(first, f, j):
                    u = u0 + first + f
                    act.wait_ge(mm, u + 1)
                    split_w_in_loop(u, j)

                def split_w_in_loop(u, j):
                    act.wait_ge(raw_in[j % 2], (u - j % 2) * 8 + 16 * 3)
                    act.activation(wh[j][:], raw[j % 2][:], ACT.Copy).then_inc(w_hi, 1)

                def only_ahead(first, n=KB):
                    units(act, n, lambda f, j: ahead(first, f, j))

                sqrt_ms(l * 2 + 1)
                only_ahead(QK, 24)

                def conv_units(f, j):
                    ahead(CU, f, j)
                    act.wait_ge(evac, u0 + CU + f + 3)
                    act.activation(blk(d2, f), blk(d1, f), ACT.Copy, scale=conv_w[:, bass.ds(l * 3 + 2, 1), bass.ds(f, 1)].rearrange("p a b -> p (a b)")).then_inc(tap_done, 1)
                units(act, KB, conv_units)

                def hi_units(first, src0, dst, dst_from=None):
                    def body(f, j):
                        ahead(first, f, j)
                        act.wait_ge(in_src, l * LAYER_SRC + src0 + f + 1)
                        act.activation(blk(dst, f), tmp2[:], ACT.Copy).then_inc(in_hi, 1)
                    units(act, KB, body)
                hi_units(CB, 0, bh)

                for h in range(HEADS):
                    for f in (2 * h, 2 * h + 1):
                        ahead(G, f, f % 4)
                        act.wait_ge(evac, u0 + G + f + 3)
                        act.activation(blk(d2, f), tmp[f % 2][:], ACT.Silu).then_inc(gate_done, 1)
                        if f % 2 == 0 and h:
                            act.wait_ge(var_done, l * HEADS + h)
                            act.activation(o_sum, stat_ps, ACT.Sqrt, bias=eps[:, 0:1]).then_inc(o_std, 1)
                    act.wait_ge(cen_done, l * HEADS + h + 1)
                    act.activation(o_sum, o_blk[0], ACT.Square)
                    act.activation(tmp2[:], o_blk[1], ACT.Square).then_inc(o_sq, 1)
                act.wait_ge(var_done, l * HEADS + HEADS)
                act.activation(o_sum, stat_ps, ACT.Sqrt, bias=eps[:, 0:1]).then_inc(o_std, 1)

                act.wait_ge(y_done, l * HEADS + HEADS)

                def ga_units(f, j):
                    ahead(GA, f, j)
                    act.wait_ge(evac, u0 + GA + f + 3)
                    act.activation(blk(d1, f), tmp[j % 2][:], ACT.Sigmoid).then_inc(gate_done, 1)
                units(act, KB, ga_units)
                only_ahead(CONV)

                def gb_units(f, j):
                    ahead(GB, f, j)
                    act.wait_ge(evac, u0 + GB + f + 3)
                    act.activation(blk(cf, f), tmp[j % 2][:], ACT.Sigmoid).then_inc(gate_done, 1)
                    act.activation(blk(bh, f), blk(d2, f), ACT.Copy).then_inc(in_hi, 1)
                units(act, KB, gb_units)
                hi_units(RET, 8, ah)

                def norm_units(first, dst, gain):
                    def body(f, j):
                        ahead(first, f, j)
                        act.wait_ge(evac, u0 + first + f + 3)
                        split_norm(blk(x, f), (dst, gains[:, bass.ds(l * 2 + gain, 1), bass.ds(f, 1)].rearrange("p a b -> p (a b)")), f)
                    units(act, KB, body)
                norm_units(WO, "b", 1)
                sqrt_ms(l * 2 + 2)
                hi_units(UP0, 16, ah)
                hi_units(UP1, 24, ch)
                only_ahead(DN0)
                hi_units(UP2, 32, ah)
                only_ahead(DN1)
                hi_units(UP3, 40, ch)
                only_ahead(DN2)
                norm_units(DN3, "a", 2)
            sqrt_ms(LAYERS * 2 + 1)

            def load(dst, src):
                act.dma_start(dst, src, allow_slow_non_contiguous=True).then_inc(c2_in, 16)
                loads[0] += 16
            loads = [0]
            for i in range(2):
                for half in range(2):
                    lanes = slice(half * HD, half * HD + HD)
                    load(cmp_w1[i][lanes], d["cmp_w1"][i].rearrange("(n e) j -> e n j", e=HD))
                    load(cmp_w2[i][lanes], d["cmp_w2"][i])
                    load(cmp_pe[i][lanes], d["cmp_pe"][i].rearrange("n e -> e n"))
            load(gm_ws.rearrange("p (g s) -> p g s", g=4), d["gmlp_ws"].rearrange("g t s -> t g s"))
            load(tmp2[0:1, :], d["gmlp_bs"])
            for i, name in enumerate(("gmlp_ln_g", "gmlp_ln_b")):
                load(ln_rows[:, i], d[name].to_broadcast([P, DV]))
            load(diag[:], d["diag"])
            load(tril[:], d["tril"])
            load(cmp_add[:], d["cmp_add"])
            load(cmp_keep[:], d["cmp_keep"])
            load(gains2[:], d["gains2"].rearrange("l (k p) -> p l k", p=P))
            load(conv_taps[:], d["conv_taps"].rearrange("l (k p) -> p l k", p=P))
            load(ffn_taps[:], d["ffn_taps"].rearrange("l (k p) -> p l k", p=P))
            assert loads[0] == C2_LOADS * 16, loads
            act.dma_start(mem_raw, d["mem"].rearrange("(c p) f -> p c f", p=P)).then_inc(mem_in, 16)

            def ahead2(u):
                act.wait_ge(mm, u + 1)
                if u + 4 < U_END:
                    split_w(u + 4, u % 4)

            def loop_ahead(u0, n, body=None):
                with act.Fori(0, n // 4) as i:
                    for j in range(4):
                        u = u0 + j
                        act.wait_ge(mm, i * 4 + (u + 1))
                        slot = u % 4
                        act.wait_ge(raw_in[u % 2], i * 32 + 16 * ((u + 4) // 2 + 1))
                        act.activation(wh[slot][:], raw[u % 2][:], ACT.Copy).then_inc(w_hi, 1)
                        if body:
                            body(i * 4 + j, j)

            act.wait_ge(c2_in, C2_LOADS * 16)
            for k in range(KB):
                act.wait_ge(x2_src, k + 1)
                split_norm(blk(x, k), ("a", gains2[:, 0, k:k + 1]), k)
            act.wait_ge(mem_in, 16)
            for c in range(2):
                act.activation(bf[:, 4 * T:4 * T + D], mem_raw[:, c], ACT.Square, accum_out=mem_ms[:, c:c + 1]).then_inc(mem_sq, 1)
                act.wait_ge(mem_sq, c + 1)
            act.activation(mem_ms[:], mem_ms[:], ACT.Sqrt, scale=1.0 / D, bias=eps[:, 0:1]).then_inc(mem_rms, 1)
            sqrt_ms(LAYERS * 2 + 2)
            for f in range(Z_GL):
                ahead2(U2 + f)
            done_act = [0]

            def z_gate(f, func, dst, lanes=P):
                ahead2(U2 + f)
                act.wait_ge(evac, U2 + f + 3)
                act.activation(dst, tmp[f % 2][0:lanes], func).then_inc(z_act, 1)

            z_gate(Z_GL, ACT.Sigmoid, tmp[Z_GL % 2][0:GATES], GATES)
            z_gate(Z_U, ACT.Gelu_apprx_tanh, gm_u[0])
            z_gate(Z_U + 1, ACT.Gelu_apprx_tanh, gm_u[1])
            z_gate(Z_V, ACT.Gelu_apprx_tanh, y_gm[0])
            for i in range(2):
                act.wait_ge(cmp_mm, 2 * i + 2)
                for g in range(2):
                    lanes = slice(g * HD, g * HD + HD)
                    act.activation(cmp_hid[i][lanes], aux[lanes, 2 * i + g, 0:N_CMP], ACT.Gelu_apprx_tanh).then_inc(cmp_gelu, 1)
            z_gate(Z_V + 1, ACT.Gelu_apprx_tanh, y_gm[1])
            ahead2(U2 + Z_A)
            ahead2(U2 + Z_A + 1)
            act.wait_ge(gm_var, 1)
            act.activation(mv[:, :, 1], mv[:, :, 1], ACT.Sqrt, bias=eps[:, 0:1]).then_inc(gm_std, 1)
            for f in (Z_GT, Z_GT + 1):
                z_gate(f, ACT.Sigmoid, tmp[f % 2][:])

            for k in range(KB):
                act.wait_ge(mem_tr, k // 2 + 1)
                act.activation(memh[:, k * MEM:(k + 1) * MEM], aux[:, k // 2, (k % 2) * MEM:(k % 2 + 1) * MEM], ACT.Copy,
                               scale=gains2[:, 3, k:k + 1]).then_inc(mem_hi, 1)

            scale = HD ** -0.5
            exps, pts = [0], [0]

            def exp_heads(b, nk, it):
                act.wait_ge(shift_att, 2 * it + b + 1)
                for h in range(REP):
                    act.activation(p_att[b][:, h, 0:nk], aux[:, h, 0:nk], ACT.Exp, scale=scale, bias=row[:, 4 * b, h:h + 1],
                                   accum_out=row[:, 4 * b + 1, h:h + 1]).then_inc(exp_att, 1)

            def take_t(dst, src):
                act.wait_ge(t_att, pts[0] + 1)
                act.activation(dst, src, ACT.Copy).then_inc(pt_ready, 1)
                pts[0] += 1

            for it, (c, g) in enumerate(ITS):
                nk = (c + 1) * P
                act.wait_ge(shift_cmp, it + 1)
                act.activation(p_cmp[:], p_cmp[:], ACT.Exp, scale=scale).then_inc(exp_cmp, 1)
                exp_heads(0, nk, it)
                ahead2(MK + 2 * it)
                take_t(tmp[0][0:N_CMP, :], o_ps[0][0:N_CMP, :])
                exp_heads(1, nk, it)
                for n in range(c + 1):
                    take_t(pt_att[0][:, n * T:(n + 1) * T], o_ps[(n + 1) % 2][:])
                ahead2(MK + 2 * it + 1)
                for n in range(c + 1):
                    take_t(pt_att[1][:, n * T:(n + 1) * T], o_ps[(n + c) % 2][:])

            act.wait_ge(cv_cen, 1)
            act.activation(part_r[0], y_cv[0], ACT.Square)
            act.activation(part_r[1], y_cv[1], ACT.Square).then_inc(cv_sq, 1)
            act.wait_ge(cv_var, 1)
            act.activation(part_r[2], stat_ps, ACT.Sqrt, bias=eps[:, 0:1]).then_inc(cv_std, 1)
            act.wait_ge(cv_n, 1)
            for i in range(2):
                act.activation(y_cv[i], y_cv[i], ACT.Silu, scale=conv_taps[:, TAPS + 1, i:i + 1], bias=conv_taps[:, TAPS + 2, i:i + 1]).then_inc(cv_y, 1)
            act.wait_ge(cv_y, 2)
            for f in range(KB):
                act.wait_ge(part_src, f + 1)
                act.activation(part_sq, d2[:, f * T:(f + 1) * T], ACT.Square).then_inc(part_sqd, 1)
            for i in range(3):
                act.wait_ge(part_ms, i + 1)
                act.activation(part_r[i], aux[:, i], ACT.Sqrt, bias=eps[:, 0:1]).then_inc(part_std, 1)

            def hi_of(n, dst, k):
                act.wait_ge(src2, n + 1)
                act.activation(blk(dst, k), tmp2[:], ACT.Copy).then_inc(in_hi, 1)
            for k in range(KB):
                hi_of(k, ah, k)

            def norm_units2(first, gain, dst):
                def body(f, j):
                    act.wait_ge(evac, f + (first + 3))
                    act.activation(blk(dst, f), blk(x, f), ACT.Copy, scale=gains2[:, gain, bass.ds(f, 1)]).then_inc(in_hi, 1)
                    act.activation(sq, blk(x, f), ACT.Square).then_inc(sq_done, 1)
                loop_ahead(first, KB, body)

            norm_units2(OUT, 2, ch)
            sqrt_ms(LAYERS * 2 + 3)
            loop_ahead(XQ, KB)
            for c in range(NC):
                act.wait_ge(xs_shift, c + 1)
                for h in range(XH):
                    act.activation(x_p[:, h], aux[:, h // 2, (h % 2) * MEM:(h % 2 + 1) * MEM], ACT.Exp, scale=DV ** -0.5,
                                   bias=row[:, 0, h:h + 1], accum_out=row[:, 1, h:h + 1]).then_inc(x_exp, 1)
                for m in range(2):
                    act.wait_ge(xt_mm, 2 * c + m + 1)
                    act.activation(x_pt[:, m, :, c * P:(c + 1) * P], aux[:, 2 + m].rearrange("p (h q) -> p h q", h=XH), ACT.Copy).then_inc(xt_copy, 1)
            for k in range(KB):
                act.wait_ge(xo_mm, k + 1)
                act.activation(blk(ah, k), aux[:, k % 4], ACT.Copy).then_inc(in_hi, 1)
            norm_units2(XO, 4, ch)
            sqrt_ms(LAYERS * 2 + 4)

            def up_pairs(first, b0, n, dst):
                def tap(f, j):
                    return f
                with act.Fori(0, n // 2) as i:
                    for j in range(4):
                        u = first + j
                        act.wait_ge(mm, i * 4 + (u + 1))
                        act.wait_ge(raw_in[u % 2], i * 32 + 16 * ((u + 4) // 2 + 1))
                        act.activation(wh[u % 4][:], raw[u % 2][:], ACT.Copy).then_inc(w_hi, 1)
                        b = i * 2 + ((j % 2) * FB + b0 + j // 2)
                        act.wait_ge(evac, i * 4 + (u + 3))
                        act.activation(part_r[j % 2], tmp[j % 2][:], ACT.Identity, scale=ffn_taps[:, FFN_TAPS - 1, bass.ds(b, 1)],
                                       bias=ffn_taps[:, FFN_TAPS, bass.ds(b, 1)]).then_inc(ffn_tap, 1)
                        if j % 2 == 0:
                            act.wait_ge(ffn_pre, i * 2 + (b0 + j // 2 + 1))
                            act.activation(part_r[0], part_r[0], ACT.Silu).then_inc(ffn_silu, 1)
                        else:
                            act.wait_ge(ffn_src, i * 2 + (b0 + j // 2 + 1))
                            act.activation(blk(dst, i * 2 + j // 2), tmp2[:], ACT.Copy).then_inc(in_hi, 1)

            up_pairs(UPG[0], *GROUPS[0], ah)
            up_pairs(UPG[1], *GROUPS[1], bh)
            loop_ahead(DNG[0], KB)
            up_pairs(UPG[2], *GROUPS[2], ah)
            loop_ahead(DNG[1], KB)

            def last_units(f, j):
                act.wait_ge(evac, f + (DNG[2] + 3))
                act.activation(sq, blk(x, f), ACT.Square).then_inc(sq_done, 1)
            for f in range(KB):
                ahead2(DNG[2] + f)
                last_units(f, f % 4)
            sqrt_ms(LAYERS * 2 + 5)

        @block.vector
        def _(dve):
            step = [0]

            def done(ins):
                step[0] = step[0] + 1
                ins.then_inc(dve_step, 1)

            def wait_step():
                dve.wait_ge(dve_step, step[0])

            dve.sem_inc(evac, 2)
            dve.sem_inc(v_done, 2)
            dve.sem_inc(qk_done, 1)
            dve.wait_ge(const_in, 16 * 6)
            done(dve.memset(acc, 0.0))

            def split_lo_norm(dst_h, dst_l, src, gain, k, sq_n):
                dve.scalar_tensor_tensor(out=blk(dst_l, k), in0=src, scalar=gain, in1=blk(dst_h, k).bitcast(F32),
                                         op0=ALU.mult, op1=ALU.subtract).then_inc(in_lo, 1)
                dve.wait_ge(sq_done, sq_n)
                wait_step()
                done(dve.tensor_tensor(acc, acc, sq, ALU.add))

            for k in range(KB):
                dve.wait_ge(x_tr, k + 1)
                dve.tensor_copy(blk(x, k), (aux[:, k % 4])).then_inc(x_src, 1)
                dve.wait_ge(in_hi, k + 1)
                split_lo_norm(ah, al, blk(x, k), gains[:, 0, k:k + 1], k, k + 1)
            wait_step()
            dve.sem_inc(ssq_src, 1)

            dve.wait_ge(pos_in, 16)
            done(dve.tensor_copy(tmp[0][:], tmp2[:].bitcast(I32)))
            wait_step()
            done(dve.tensor_scalar(tmp[1][:], tmp[0][:], inv_freq[:, 0:1], None, ALU.mult))
            for dst, turn in ((sin, 0.0), (cos, 0.25)):
                wait_step()
                done(dve.tensor_scalar(tmp2[:], tmp[1][:], float(np.float32(1 / TWO_PI)), turn, ALU.mult, ALU.add))
                wait_step()
                done(dve.tensor_scalar(tmp2[:], tmp2[:], float(ROUND), None, ALU.add))
                wait_step()
                done(dve.tensor_scalar(tmp2[:], tmp2[:], float(-ROUND), None, ALU.add))
                src = tmp[1]
                for part in (PI_1, PI_2, PI_3):
                    wait_step()
                    done(dve.scalar_tensor_tensor(out=dst[:], in0=tmp2[:], scalar=float(-part), in1=src[:], op0=ALU.mult, op1=ALU.add))
                    src = dst
                wait_step()
                done(dve.tensor_scalar(dst[:], dst[:], turn * TWO_PI, PI_UNDER, ALU.add, ALU.min))
                wait_step()
                ins = dve.tensor_scalar(dst[:], dst[:], -PI_UNDER, None, ALU.max)
                if turn:
                    ins.then_inc(ang_done, 1)
                else:
                    done(ins)
            dve.wait_ge(trig_done, 2)
            done(dve.tensor_scalar(sin[64:128], sin[64:128], -1.0, None, ALU.mult))

            base = step[0]
            STEPS = 51
            with dve.Fori(0, LAYERS) as l:
                u0 = l * UNITS
                begun = l * STEPS + base
                step[0] = begun
                cnt = [0]

                def done_l(ins):
                    cnt[0] += 1
                    ins.then_inc(dve_step, 1)

                def wait_l():
                    dve.wait_ge(dve_step, l * STEPS + (base + cnt[0]))

                def loop(n, per, body):
                    with dve.Fori(0, n // 4) as i:
                        for j in range(4):
                            used = [0]

                            def step_done(ins):
                                used[0] += 1
                                ins.then_inc(dve_step, 1)

                            def step_wait(i=i, j=j, used=used):
                                dve.wait_ge(dve_step, l * STEPS + i * (4 * per) + (base + cnt[0] + j * per + used[0]))

                            body(i * 4 + j, j, step_done, step_wait)
                            assert used[0] == per, (used, per)
                    cnt[0] += n * per

                def unit_done(first, f):
                    dve.wait_ge(mm, u0 + first + f + 1)

                def norm_factor(n):
                    dve.wait_ge(std_done, n)
                    done_l(dve.reciprocal(rstd[:], rstd[:]))
                    wait_l()
                    dve.sem_inc(dve_begun, 1)

                norm_factor(l * 2 + 1)
                done_l(dve.tensor_tensor(rstd2, rstd[:], rstd[:], ALU.mult))
                done_l(dve.tensor_tensor(cos_r, cos[:], rstd[:], ALU.mult))
                done_l(dve.tensor_tensor(sin_r, sin[:], rstd[:], ALU.mult))
                wait_l()
                dve.sem_inc(dve_begun, 1)

                def rope(f, j, step_done, step_wait):
                    ps = unit_ps[j % 2]
                    unit_done(QK, f)
                    dve.wait_ge(qk_done, l * KB + f + 1)
                    dve.tensor_tensor(tmp[0][:], ps[:], cos_r, ALU.mult)
                    dve.tensor_tensor(tmp[1][0:64], ps[64:128], sin_r[64:128], ALU.mult)
                    dve.tensor_tensor(tmp[1][64:128], ps[0:64], sin_r[0:64], ALU.mult).then_inc(evac, 1)
                    dve.wait_ge(evac, u0 + QK + f + 3)
                    dve.tensor_tensor(blk(cf, f), tmp[0][:], tmp[1][:], ALU.add).then_inc(qk_done, 1)
                loop(KB, 0, rope)

                def v_units(f, j, step_done, step_wait):
                    unit_done(VV, f)
                    dve.wait_ge(qk_done, l * KB + KB + 1)
                    dve.tensor_tensor(tmp[j % 2][:], unit_ps[j % 2][:], rstd[:], ALU.mult).then_inc(evac, 1)
                    dve.wait_ge(v_tr, l * KB + f + 1)
                    dve.tensor_copy(v_tok[:, :, bass.ds(f * P, P)], aux[:, j % 2].rearrange("p (c v) -> p c v", c=NC)).then_inc(v_done, 1)
                loop(KB, 0, v_units)

                def c_units(f, j, step_done, step_wait):
                    unit_done(CC, f)
                    dve.tensor_tensor(blk(d1, f), unit_ps[j % 2][:], rstd2, ALU.mult).then_inc(evac, 1)
                loop(KB, 0, c_units)

                def tap(n, f):
                    return conv_w[:, bass.ds(l * 3 + n, 1), bass.ds(f, 1)].rearrange("p a b -> p (a b)")

                def u_units(f, j, step_done, step_wait):
                    unit_done(CU, f)
                    dve.tensor_tensor(blk(d1, f), unit_ps[j % 2][:], blk(d1, f), ALU.mult).then_inc(evac, 1)
                    dve.wait_ge(tap_done, l * KB + f + 1)
                    for shift, n in ((1, 1), (2, 0)):
                        into = d2[:, bass.ds(f * T + shift, T - shift)]
                        step_done(dve.scalar_tensor_tensor(out=into, in0=d1[:, bass.ds(f * T, T - shift)], scalar=tap(n, f), in1=into,
                                                           op0=ALU.mult, op1=ALU.add))
                        step_wait()
                loop(KB, 2, u_units)

                def split_lo(dst_h, dst_l, f, n):
                    dve.wait_ge(in_hi, l * LAYER_SPLITS + KB + n + f + 1)
                    dve.tensor_tensor(blk(dst_l, f), tmp2[:], blk(dst_h, f).bitcast(F32), ALU.subtract).then_inc(in_lo, 1)

                def b_units(f, j, step_done, step_wait):
                    unit_done(CB, f)
                    dve.tensor_tensor(tmp[0][:], unit_ps[j % 2][:], rstd[:], ALU.mult).then_inc(evac, 1)
                    dve.wait_ge(evac, u0 + CB + f + 3)
                    dve.wait_ge(in_lo, l * LAYER_SPLITS + KB + f)
                    dve.tensor_tensor(tmp2[:], tmp[0][:], blk(d2, f), ALU.mult).then_inc(in_src, 1)
                    split_lo(bh, bl, f, 0)
                loop(KB, 0, b_units)

                def g_unit(f):
                    unit_done(G, f)
                    dve.wait_ge(gate_done, l * 24 + f + 1)
                    dve.tensor_tensor(tmp[f % 2][:], unit_ps[f % 2][:], rstd[:], ALU.mult).then_inc(evac, 1)

                def decay_scores(h):
                    dve.wait_ge(s_done, l * HEADS + h + 1)
                    for n in range(NC):
                        bank, col = S_AT[n]
                        ins = dve.tensor_tensor(p_dec[h % 2][:, P_AT[n]:P_AT[n] + S_COLS[n]], aux[:, bank, col:col + S_COLS[n]],
                                                decay[:, h * T:h * T + S_COLS[n]], ALU.mult)
                    ins.then_inc(p_done, 1)

                def take_o(h):
                    dve.wait_ge(pv_done, l * HEADS + h + 1)
                    if h:
                        dve.wait_ge(y_done, l * HEADS + h)
                    dve.tensor_copy(o_blk[0], o_ps[0][:])
                    dve.tensor_copy(o_blk[1], o_ps[1][:]).then_inc(o_out, 1)
                    dve.wait_ge(o_out, l * HEADS + h + 1)
                    dve.tensor_tensor(o_sum, o_blk[0], o_blk[1], ALU.add).then_inc(o_sum_done, 1)

                def centre(h):
                    dve.wait_ge(mean_done, l * HEADS + h + 1)
                    dve.tensor_tensor(o_blk[0], o_blk[0], stat_ps, ALU.subtract)
                    dve.tensor_tensor(o_blk[1], o_blk[1], stat_ps, ALU.subtract).then_inc(cen_done, 1)
                    dve.wait_ge(o_sq, l * HEADS + h + 1)
                    dve.tensor_tensor(o_sum, o_sum, tmp2[:], ALU.add).then_inc(o_sq_sum, 1)

                def head_norm(h):
                    dve.wait_ge(o_std, l * HEADS + h + 1)
                    done_l(dve.reciprocal(o_sum, o_sum))
                    wait_l()
                    for n in range(2):
                        f = 2 * h + n
                        done_l(dve.scalar_tensor_tensor(out=o_blk[n], in0=o_blk[n], scalar=ret_g[:, bass.ds(l, 1), f:f + 1].rearrange("p a b -> p (a b)"),
                                                        in1=o_sum, op0=ALU.mult, op1=ALU.mult))
                    dve.wait_ge(gate_done, l * 24 + 2 * h + 2 + 2)
                    for n in range(2):
                        f = 2 * h + n
                        wait_l()
                        ins = dve.tensor_tensor(blk(d2, f), o_blk[n], blk(d2, f), ALU.mult)
                    ins.then_inc(y_done, 1)

                decay_scores(0)
                for h in range(HEADS):
                    g_unit(2 * h)
                    if h:
                        head_norm(h - 1)
                    if h + 1 < HEADS:
                        decay_scores(h + 1)
                    take_o(h)
                    g_unit(2 * h + 1)
                    centre(h)
                head_norm(HEADS - 1)

                def gate_units(first, n):
                    def body(f, j, step_done, step_wait):
                        unit_done(first, f)
                        dve.wait_ge(gate_done, l * 24 + n + f + 1)
                        dve.tensor_tensor(tmp[j % 2][:], unit_ps[j % 2][:], rstd[:], ALU.mult).then_inc(evac, 1)
                        if first == GB:
                            dve.wait_ge(in_hi, l * LAYER_SPLITS + KB + 8 + f + 1)
                            dve.tensor_tensor(blk(bl, f), blk(d2, f), blk(bh, f).bitcast(F32), ALU.subtract).then_inc(in_lo, 1)
                    return body
                loop(KB, 0, gate_units(GA, 8))

                dve.wait_ge(gate_done, l * 24 + 16 + 2)
                dve.sem_inc(dve_begun, 1)

                def conv_units(f, j, step_done, step_wait):
                    unit_done(CONV, f)
                    dve.tensor_tensor(blk(d1, f), unit_ps[j % 2][:], blk(d1, f), ALU.mult).then_inc(evac, 1)
                loop(KB, 0, conv_units)
                loop(KB, 0, gate_units(GB, 16))

                dve.wait_ge(gate_done, l * 24 + 24 + 2)
                dve.sem_inc(dve_begun, 1)

                def ret_units(f, j, step_done, step_wait):
                    unit_done(RET, f)
                    dve.tensor_tensor(tmp[0][:], unit_ps[j % 2][:], blk(cf, f), ALU.mult).then_inc(evac, 1)
                    dve.wait_ge(evac, u0 + RET + f + 3)
                    dve.wait_ge(in_lo, l * LAYER_SPLITS + KB + 16 + f)
                    dve.tensor_tensor(tmp2[:], tmp[0][:], blk(d1, f), ALU.add).then_inc(in_src, 1)
                    split_lo(ah, al, f, 16)
                loop(KB, 0, ret_units)

                def norm_units(first, dst_h, dst_l, gain, n, sq0):
                    done_l(dve.memset(acc, 0.0))

                    def body(f, j, step_done, step_wait):
                        unit_done(first, f)
                        dve.tensor_tensor(blk(x, f), unit_ps[j % 2][:], blk(x, f), ALU.add).then_inc(evac, 1)
                        dve.wait_ge(in_hi, l * LAYER_SPLITS + KB + n + f + 1)
                        dve.scalar_tensor_tensor(out=blk(dst_l, f), in0=blk(x, f), scalar=gains[:, bass.ds(l * 2 + gain, 1), bass.ds(f, 1)].rearrange("p a b -> p (a b)"),
                                                 in1=blk(dst_h, f).bitcast(F32), op0=ALU.mult, op1=ALU.subtract).then_inc(in_lo, 1)
                        dve.wait_ge(sq_done, l * 16 + KB + sq0 + f + 1)
                        step_wait()
                        step_done(dve.tensor_tensor(acc, acc, sq, ALU.add))
                    loop(KB, 1, body)
                    wait_l()
                    dve.sem_inc(ssq_src, 1)
                norm_units(WO, bh, bl, 1, 24, 0)

                norm_factor(l * 2 + 2)

                def up_units(first, dst_h, dst_l, n):
                    def body(f, j, step_done, step_wait):
                        unit_done(first, f)
                        dve.tensor_tensor(tmp[0][:], unit_ps[j % 2][:], rstd[:], ALU.mult).then_inc(evac, 1)
                        dve.wait_ge(evac, u0 + first + f + 3)
                        dve.wait_ge(in_lo, l * LAYER_SPLITS + KB + n + f)
                        dve.scalar_tensor_tensor(out=tmp2[:], in0=tmp[0][:], scalar=0.0, in1=tmp[0][:], op0=ALU.max, op1=ALU.mult).then_inc(in_src, 1)
                        split_lo(dst_h, dst_l, f, n)
                    loop(KB, 0, body)

                def down_units(first):
                    def body(f, j, step_done, step_wait):
                        unit_done(first, f)
                        dve.tensor_tensor(blk(x, f), unit_ps[j % 2][:], blk(x, f), ALU.add).then_inc(evac, 1)
                    loop(KB, 0, body)

                up_units(UP0, ah, al, 32)
                up_units(UP1, ch, cl, 40)
                down_units(DN0)
                up_units(UP2, ah, al, 48)
                down_units(DN1)
                up_units(UP3, ch, cl, 56)
                down_units(DN2)
                norm_units(DN3, ah, al, 2, 64, 8)
                assert cnt[0] == STEPS, cnt
            step[0] = base + LAYERS * STEPS

            IL = KB + LAYERS * LAYER_SPLITS
            SQ = KB + LAYERS * 2 * KB
            count = {id(dve_step): step[0], id(evac): 2 + U2, id(in_lo): IL}
            last = [(dve_step, step[0])]

            def go():
                dve.wait_ge(*last[0])

            def did(ins, s=dve_step):
                count[id(s)] = count.get(id(s), 0) + 1
                ins.then_inc(s, 1)
                last[0] = (s, count[id(s)])

            def mult(dst, a, b, s=dve_step):
                go()
                did(dve.tensor_tensor(dst, a, b, ALU.mult), s)

            def copy(dst, src, s=dve_step):
                go()
                did(dve.tensor_copy(dst, src), s)

            def factor(n):
                dve.wait_ge(std_done, n)
                go()
                did(dve.reciprocal(rstd[:], rstd[:]))

            factor(LAYERS * 2 + 1)
            go()
            did(dve.memset(acc, 0.0))
            for k in range(KB):
                go()
                did(dve.scalar_tensor_tensor(out=blk(x, k), in0=blk(x, k), scalar=gains[:, 2 * LAYERS, k:k + 1], in1=rstd[:],
                                             op0=ALU.mult, op1=ALU.mult), x2_src)
                dve.wait_ge(in_hi, IL + k + 1)
                go()
                did(dve.scalar_tensor_tensor(out=blk(al, k), in0=blk(x, k), scalar=gains2[:, 0, k:k + 1], in1=blk(ah, k).bitcast(F32),
                                             op0=ALU.mult, op1=ALU.subtract), in_lo)
                dve.wait_ge(sq_done, SQ + k + 1)
                go()
                did(dve.tensor_tensor(acc, acc, sq, ALU.add))
            go()
            dve.sem_inc(ssq_src, 1)
            dve.wait_ge(mem_rms, 1)
            go()
            did(dve.reciprocal(mem_ms[:], mem_ms[:]))
            for c in range(2):
                go()
                did(dve.tensor_scalar(mem_raw[:, c], mem_raw[:, c], mem_ms[:, c:c + 1], None, ALU.mult), mem_scaled)
            for i in range(2):
                go()
                did(dve.memset(hp[i][:, 0:TAPS - 1], 0.0))
            go()
            did(dve.memset(one_row[:], 1.0))
            factor(LAYERS * 2 + 2)

            def z_done(f):
                dve.wait_ge(mm, U2 + f + 1)

            def z_ps(f):
                return unit_ps[f % 2]

            def z_scaled(f, dst):
                z_done(f)
                mult(dst, z_ps(f)[:], rstd[:], evac)

            for i in range(2):
                z_scaled(i, cmp_in[i])
                go()
                src = cmp_in[i]
                win_src = bass.AP(src.tensor, src.offset, [src.ap[0], [1, CMP_BLOCK], [CMP_STRIDE, N_CMP]])
                did(dve.tensor_tensor(cmp_win[i], win_src, cmp_pe[i][:].unsqueeze(2).broadcast_to([P, CMP_BLOCK, N_CMP]), ALU.add), win_done)

            def z_keys(f, b):
                z_done(f)
                for g in range(2):
                    src = slice(g * HD, g * HD + HD)
                    for half in range(2):
                        mult(k_att[b][g][half * HD:half * HD + HD], z_ps(f)[src], rstd[src], evac if (g, half) == (1, 1) else dve_step)

            def z_values(b):
                dve.wait_ge(z_tr, b + 1)
                copy(v_att[b], aux[:, b].rearrange("p (c v) -> p c v", c=NC), att_v)

            z_keys(2, 0)
            z_scaled(3, tmp[1][:])
            z_keys(4, 1)
            z_values(0)
            z_scaled(5, tmp[1][:])
            z_scaled(6, q_t[0])
            z_values(1)
            for f in range(1, 4):
                z_scaled(Z_Q + f, q_t[f])
            z_done(Z_GL)
            mult(tmp[0][0:GATES], z_ps(Z_GL)[0:GATES], rstd[0:GATES], evac)
            z_scaled(Z_U, tmp[1][:])
            dve.wait_ge(z_tr, 3)
            copy(gates[:], aux[:, 2, 0:NC * GATES].rearrange("p (c h) -> p c h", c=NC), gate_tok)
            z_scaled(Z_U + 1, tmp[0][:])
            dve.wait_ge(z_act, 2)
            z_scaled(Z_V, tmp[1][:])
            dve.wait_ge(z_act, 3)
            z_scaled(Z_V + 1, tmp[0][:])
            dve.wait_ge(cmp_mm, 6)
            for g in range(2):
                copy(k_cmp[g][0:HD], o_ps[g][0:HD, 0:N_CMP])
                copy(k_cmp[g][HD:2 * HD], o_ps[g][0:HD, 0:N_CMP])
                copy(v_cmp[:, g], o_ps[g][0:N_CMP, HD:2 * HD], cmp_out)
            for i in range(2):
                z_scaled(Z_A + i, cv_a[i])
            dve.wait_ge(gm_tr, 1)
            for n in range(2):
                copy(v_ln[:, 2 * n:2 * n + 2], aux[:, n].rearrange("p (c v) -> p c v", c=2))
            for c in range(NC):
                go()
                did(dve.bn_stats(bn[:, c], v_ln[:, c]))
            for c in range(NC):
                go()
                did(dve.bn_aggr(mv[:, c], bn[:, c]), gm_var if c == NC - 1 else dve_step)
            dve.wait_ge(gm_std, 1)
            go()
            did(dve.reciprocal(mv[:, :, 1], mv[:, :, 1]))
            for c in range(NC):
                go()
                did(dve.tensor_scalar(v_ln[:, c], v_ln[:, c], mv[:, c, 0:1], mv[:, c, 1:2], ALU.subtract, ALU.mult))
            mult(v_ln, v_ln, ln_rows[:, 0].unsqueeze(1).broadcast_to([P, NC, DV]))
            go()
            did(dve.tensor_tensor(v_ln, v_ln, ln_rows[:, 1].unsqueeze(1).broadcast_to([P, NC, DV]), ALU.add), gm_ready)
            ws = gm_ws.rearrange("p (g s) -> p g s", g=4)
            mult(ws, ws, tril[:].unsqueeze(1).broadcast_to([P, 4, P]), ws_ready)
            dve.wait_ge(z_act, 4)
            z_scaled(Z_GT, tmp[1][:])
            dve.wait_ge(z_act, 5)
            z_scaled(Z_GT + 1, tmp[0][:])
            for i in range(2):
                dve.wait_ge(z_act, 6 + i)
                mult(hp[i][:, TAPS - 1:], cv_a[i], tmp[(Z_GT + i) % 2][:])
            dve.wait_ge(gm_tr, 2)
            copy(gm_wt, aux[:, 2], ws_ready)
            for k in range(KB):
                dve.wait_ge(mem_hi, k // 2 * 2 + 2)
                lanes = slice(k * MEM, (k + 1) * MEM)
                go()
                did(dve.scalar_tensor_tensor(out=meml[:, lanes], in0=aux[:, k // 2, (k % 2) * MEM:(k % 2 + 1) * MEM], scalar=gains2[:, 3, k:k + 1],
                                             in1=memh[:, lanes].bitcast(F32), op0=ALU.mult, op1=ALU.subtract), mem_lo)
            dve.wait_ge(mix_mm, 1)
            for i in range(2):
                mult(y_gm[i], gm_u[i], o_ps[i][:], mixed)

            def taps():
                for n in range(TAPS):
                    for i in range(2):
                        src, w = hp[i][:, n:n + T], conv_taps[:, n, i:i + 1]
                        go()
                        if n == 0:
                            did(dve.tensor_scalar(y_cv[i], src, w, conv_taps[:, TAPS, i:i + 1], ALU.mult, ALU.add))
                        else:
                            did(dve.scalar_tensor_tensor(out=y_cv[i], in0=src, scalar=w, in1=y_cv[i], op0=ALU.mult, op1=ALU.add))
                        yield
            tap = taps()

            def some_taps(n):
                for _ in range(n):
                    next(tap, None)

            def mem_unit(f):
                dve.wait_ge(mm, MK + f + 1)
                src = unit_ps[0][:, (f % 2) * MEM:(f % 2 + 1) * MEM]
                if f < KB:
                    copy(mem_k[:, f * MEM:(f + 1) * MEM], src, evac)
                else:
                    copy(mem_v[:, :, (f - KB) * P:(f - KB + 1) * P], src.rearrange("p (c v) -> p c v", c=2), evac)

            scale = HD ** -0.5

            def shift(b, it, c):
                nk = (c + 1) * P
                dve.wait_ge(s_att, 2 * (2 * it + b + 1))
                here = aux[:, :, c * P:nk]
                go()
                did(dve.tensor_tensor(here, here, diag[:].unsqueeze(1).broadcast_to([P, REP, P]), ALU.add))
                go()
                did(dve.tensor_reduce(row[:, 4 * b + 2], aux[:, :, 0:nk], AX, ALU.max))
                go()
                did(dve.tensor_scalar(row[:, 4 * b], row[:, 4 * b + 2], -scale, None, ALU.mult), shift_att)

            def gate_of(c, g, branch):
                return gates[:, c, g * REP * 3 + branch:(g + 1) * REP * 3 - 2 + branch:3]

            def weigh(b, it, c, g):
                nk = (c + 1) * P
                dve.wait_ge(exp_att, (2 * it + b + 1) * REP)
                go()
                did(dve.reciprocal(row[:, 4 * b + 3], row[:, 4 * b + 1]))
                mult(row[:, 4 * b + 3], row[:, 4 * b + 3], gate_of(c, g, 1 + b))
                for h in range(REP):
                    go()
                    did(dve.tensor_scalar(p_att[b][:, h, 0:nk], p_att[b][:, h, 0:nk], row[:, 4 * b + 3, h:h + 1], None, ALU.mult),
                        p_ready if h == REP - 1 else dve_step)

            for it, (c, g) in enumerate(ITS):
                shift(0, it, c)
                dve.wait_ge(s_cmp, 2 * it + 2)
                go()
                for b in range(2):
                    did(dve.tensor_tensor(p_cmp[:, b::2], o_ps[b][:, 0:64].rearrange("p (r n) -> p r n", n=32)[:, :, 0:N_CMP],
                                          cmp_add[:, c].unsqueeze(1).broadcast_to([P, 2, N_CMP]), ALU.add))
                go()
                did(dve.tensor_reduce(row[:, 8], p_cmp[:], AX, ALU.max))
                go()
                did(dve.tensor_tensor(p_cmp[:], p_cmp[:], row[:, 8].unsqueeze(2).broadcast_to([P, REP, N_CMP]), ALU.subtract), shift_cmp)
                dve.wait_ge(exp_cmp, it + 1)
                mult(p_cmp[:], p_cmp[:], cmp_keep[:, c].unsqueeze(1).broadcast_to([P, REP, N_CMP]))
                go()
                did(dve.tensor_reduce(row[:, 9], p_cmp[:], AX, ALU.add))
                go()
                did(dve.tensor_scalar(row[:, 9], row[:, 9], TINY, None, ALU.max))
                go()
                did(dve.reciprocal(row[:, 9], row[:, 9]))
                mult(row[:, 9], row[:, 9], gate_of(c, g, 0))
                mult(p_cmp[:], p_cmp[:], row[:, 9].unsqueeze(2).broadcast_to([P, REP, N_CMP]), pc_ready)
                weigh(0, it, c, g)
                mem_unit(2 * it)
                shift(1, it, c)
                some_taps(4)
                weigh(1, it, c, g)
                some_taps(4)
                mem_unit(2 * it + 1)
                dve.wait_ge(o_att, it + 1)
                o = unit_ps[1][0:HD].rearrange("p (b r t) -> p b r t", b=2, r=2)
                for half in range(2):
                    dst = d2[half * HD:half * HD + HD, 2 * g * T:(2 * g + 2) * T].rearrange("p (b t) -> p b t", b=2)[:, :, c * P:(c + 1) * P]
                    copy(dst, o[:, :, half], o_taken)
            some_taps(2 * TAPS)

            go()
            did(dve.tensor_tensor(part_acc[0], y_cv[0], y_cv[1], ALU.add), cv_sum)
            dve.wait_ge(cv_mean, 1)
            for i in range(2):
                go()
                did(dve.tensor_tensor(y_cv[i], y_cv[i], stat_ps, ALU.subtract), cv_cen if i else dve_step)
            dve.wait_ge(cv_sq, 1)
            go()
            did(dve.tensor_tensor(part_acc[0], part_r[0], part_r[1], ALU.add), cv_sqs)
            dve.wait_ge(cv_std, 1)
            go()
            did(dve.reciprocal(part_r[2], part_r[2]))
            for i in range(2):
                mult(y_cv[i], y_cv[i], part_r[2], cv_n if i else dve_step)
            part_of = [0] * 4 + [1] * 2 + [2] * 2
            go()
            dve.sem_inc(part_src, 1)
            for f in range(KB):
                n = part_of[f]
                dve.wait_ge(part_sqd, f + 1)
                go()
                if f == 0 or part_of[f - 1] != n:
                    did(dve.tensor_copy(part_acc[n], part_sq), part_src)
                else:
                    did(dve.tensor_tensor(part_acc[n], part_acc[n], part_sq, ALU.add), part_src)
            IL = IL + KB
            dve.wait_ge(cv_y, 2)
            for k in range(KB):
                n = part_of[k]
                if k == 0 or part_of[k - 1] != n:
                    dve.wait_ge(part_std, n + 1)
                    go()
                    did(dve.reciprocal(part_r[n], part_r[n]))
                go()
                did(dve.scalar_tensor_tensor(out=tmp2[:], in0=d2[:, k * T:(k + 1) * T], scalar=gains2[:, 1, k:k + 1], in1=part_r[n],
                                             op0=ALU.mult, op1=ALU.mult), src2)
                dve.wait_ge(in_hi, IL + k + 1)
                go()
                did(dve.tensor_tensor(blk(al, k), tmp2[:], blk(ah, k).bitcast(F32), ALU.subtract), in_lo)
            IL += KB
            SQ += KB

            def norm_product(first, gain, il, sq_n):
                go()
                did(dve.memset(acc, 0.0))
                go()
                base = count[id(dve_step)]
                dve.sem_inc(dve_begun, 1)
                with dve.Fori(0, KB // 4) as i:
                    for j in range(4):
                        f = i * 4 + j
                        dve.wait_ge(mm, i * 4 + (first + j + 1))
                        dve.tensor_tensor(blk(x, f), unit_ps[(first + j) % 2][:], blk(x, f), ALU.add).then_inc(evac, 1)
                        dve.wait_ge(in_hi, i * 4 + (il + j + 1))
                        dve.scalar_tensor_tensor(out=blk(cl, f), in0=blk(x, f), scalar=gains2[:, gain, bass.ds(f, 1)],
                                                 in1=blk(ch, f).bitcast(F32), op0=ALU.mult, op1=ALU.subtract).then_inc(in_lo, 1)
                        dve.wait_ge(sq_done, i * 4 + (sq_n + j + 1))
                        dve.wait_ge(dve_step, i * 4 + (base + j))
                        dve.tensor_tensor(acc, acc, sq, ALU.add).then_inc(dve_step, 1)
                for s in (evac, in_lo, dve_step):
                    count[id(s)] += KB
                last[0] = (dve_step, count[id(dve_step)])
                go()
                dve.sem_inc(ssq_src, 1)

            norm_product(OUT, 2, IL, SQ)
            IL += KB
            SQ += KB
            factor(LAYERS * 2 + 3)
            go()
            for f in range(KB):
                dve.wait_ge(mm, XQ + f + 1)
                mult(xq_t[f], unit_ps[(XQ + f) % 2][:], rstd[:], evac)
            for c in range(NC):
                dve.wait_ge(xs_mm, c + 1)
                go()
                did(dve.tensor_reduce(row[:, 2], aux[:, 0:2].rearrange("p b (h m) -> p (b h) m", m=MEM), AX, ALU.max))
                go()
                did(dve.tensor_scalar(row[:, 0], row[:, 2], -(DV ** -0.5), None, ALU.mult), xs_shift)
                dve.wait_ge(x_exp, XH * (c + 1))
                go()
                did(dve.reciprocal(row[:, 3], row[:, 1]))
                for h in range(XH):
                    go()
                    did(dve.tensor_scalar(x_p[:, h], x_p[:, h], row[:, 3, h:h + 1], None, ALU.mult), xp_ready)
            for k in range(KB):
                dve.wait_ge(in_hi, IL + k + 1)
                go()
                did(dve.tensor_tensor(blk(al, k), aux[:, k % 4], blk(ah, k).bitcast(F32), ALU.subtract), in_lo)
            IL += KB
            norm_product(XO, 4, IL, SQ)
            IL += KB
            SQ += KB

            factor(LAYERS * 2 + 4)

            def up_pairs(first, b0, n, dst_h, dst_l):
                go()
                base = count[id(dve_step)]
                dve.sem_inc(dve_begun, 1)
                with dve.Fori(0, n // 2) as i:
                    for j in range(4):
                        u = first + j
                        used = 3 * (j // 2) + j % 2
                        pair = j // 2 + b0
                        b = i * 2 + ((j % 2) * FB + b0 + j // 2)
                        dve.wait_ge(mm, i * 4 + (u + 1))
                        dve.wait_ge(in_lo, i * 2 + (IL + pair))
                        dve.tensor_tensor(tmp[j % 2][:], unit_ps[u % 2][:], rstd[:], ALU.mult).then_inc(evac, 1)
                        dve.wait_ge(ffn_tap, i * 4 + (2 * b0 + j + 1))
                        for s_, w_, sem_ in ((1, 1, dve_step), (2, 0, dve_step if j % 2 else ffn_pre)):
                            into = part_r[j % 2][:, s_:T]
                            dve.scalar_tensor_tensor(out=into, in0=tmp[j % 2][:, 0:T - s_], scalar=ffn_taps[:, w_, bass.ds(b, 1)], in1=into,
                                                     op0=ALU.mult, op1=ALU.add).then_inc(sem_, 1)
                            if sem_ is dve_step:
                                used += 1
                                dve.wait_ge(dve_step, i * 6 + (base + used))
                        if j % 2:
                            dve.wait_ge(ffn_silu, i * 2 + (pair + 1))
                            dve.tensor_tensor(tmp2[:], part_r[0], part_r[1], ALU.mult).then_inc(ffn_src, 1)
                            dve.wait_ge(in_hi, i * 2 + (IL + pair + 1))
                            dve.tensor_tensor(blk(dst_l, i * 2 + j // 2), tmp2[:], blk(dst_h, i * 2 + j // 2).bitcast(F32), ALU.subtract).then_inc(in_lo, 1)
                count[id(evac)] += 2 * n
                count[id(in_lo)] += n
                count[id(dve_step)] += 3 * n
                last[0] = (in_lo, count[id(in_lo)])

            def down(first):
                go()
                dve.sem_inc(dve_begun, 1)
                with dve.Fori(0, KB // 4) as i:
                    for j in range(4):
                        u = first + j
                        f = i * 4 + j
                        dve.wait_ge(mm, i * 4 + (u + 1))
                        dve.wait_ge(evac, i * 4 + (u + 2))
                        dve.tensor_tensor(blk(x, f), unit_ps[u % 2][:], blk(x, f), ALU.add).then_inc(evac, 1)
                count[id(evac)] += KB
                last[0] = (evac, count[id(evac)])

            up_pairs(UPG[0], *GROUPS[0], ah, al)
            up_pairs(UPG[1], *GROUPS[1], bh, bl)
            down(DNG[0])
            up_pairs(UPG[2], *GROUPS[2], ah, al)
            down(DNG[1])
            go()
            did(dve.memset(acc, 0.0))
            for f in range(KB):
                u = DNG[2] + f
                dve.wait_ge(mm, u + 1)
                go()
                did(dve.tensor_tensor(blk(x, f), unit_ps[u % 2][:], blk(x, f), ALU.add), evac)
                dve.wait_ge(sq_done, SQ + f + 1)
                go()
                did(dve.tensor_tensor(acc, acc, sq, ALU.add))
            go()
            dve.sem_inc(ssq_src, 1)
            factor(LAYERS * 2 + 5)
            for k in range(KB):
                go()
                did(dve.scalar_tensor_tensor(out=blk(x, k), in0=blk(x, k), scalar=gains2[:, 5, k:k + 1], in1=rstd[:],
                                             op0=ALU.mult, op1=ALU.mult), fin_x)
            for n in range(2 * NC):
                dve.wait_ge(fin_tr, n + 1)
                copy(d1[:, n * T:(n + 1) * T], aux[:, n % 4], fin_cp)


        @block.tensor
        def _(pe):
            pe.wait_ge(x_in, 16)
            pe.wait_ge(const_in, 16 * 6)
            pe.wait_ge(ones_set, 1)
            for k in range(KB):
                if k >= 4:
                    pe.wait_ge(x_src, k - 3)
                for c in range(NC):
                    last = pe.transpose(aux[:, k % 4, c * P:(c + 1) * P], d1[:, c * D + k * P:c * D + (k + 1) * P], ident[:])
                last.then_inc(x_tr, 1)

            def ssq(n):
                pe.wait_ge(ssq_src, n)
                pe.matmul(stat_ps, mean_d[:], acc, start=True, stop=True).then_inc(ssq_mm, 1)

            with pe.Fori(0, LAYERS) as l:
                u0 = l * UNITS

                def unit(first, f, j, x_hi, x_lo):
                    u = u0 + first + f
                    pe.wait_ge(w_lo, u + 3)
                    pe.wait_ge(evac, u + 1)
                    for k in range(KB):
                        for n, (w, v) in enumerate(((wh, x_hi), (wh, x_lo), (wl, x_hi))):
                            last = pe.matmul(unit_ps[j % 2][:], w[j][:, k], v[:, k * T:(k + 1) * T],
                                             start=(k == 0 and n == 0), stop=(k == KB - 1 and n == 2))
                    last.then_inc(mm, 1)

                def product(first, x_hi, x_lo, splits=None, n=KB):
                    if splits is not None:
                        pe.wait_ge(in_lo, l * LAYER_SPLITS + KB + splits)
                        pe.sem_inc(pe_begun, 1)
                    units(pe, n, lambda f, j: unit(first, f, j, x_hi, x_lo))

                pe.wait_ge(in_lo, l * LAYER_SPLITS + KB)
                ssq(l * 2 + 1)
                product(QK, ah, al)

                def v_transposes(f, j):
                    pe.wait_ge(evac, u0 + VV + f + 3)
                    pe.wait_ge(v_done, l * KB + f + 1)
                    for c in range(NC):
                        last = pe.transpose(aux[:, j % 2, c * P:(c + 1) * P], tmp[j % 2][:, c * P:(c + 1) * P], ident[:])
                    last.then_inc(v_tr, 1)

                with pe.Fori(0, 2) as i:
                    for j in range(4):
                        unit(VV, i * 4 + j, j, ah, al)
                        if j:
                            v_transposes(i * 4 + j - 1, j - 1)
                    v_transposes(i * 4 + 3, 3)
                product(CC, ah, al, n=24)

                def scores(h):
                    if h:
                        pe.wait_ge(p_done, l * HEADS + h)
                    for n in range(NC):
                        bank, col = S_AT[n]
                        last = pe.matmul(aux[:, bank, col:col + S_COLS[n]], cf[:, (HEADS + h) * T + n * P:(HEADS + h) * T + (n + 1) * P],
                                         cf[:, h * T + n * P:(h + 1) * T], start=True, stop=True)
                    last.then_inc(s_done, 1)

                def values(h):
                    pe.wait_ge(p_done, l * HEADS + h + 1)
                    if h:
                        pe.wait_ge(o_out, l * HEADS + h)
                    for b in range(2):
                        for n in range(NC):
                            col = h * DV + b * P
                            last = pe.matmul(o_ps[b][:, n * P:T], v_tok[:, n, col:col + P], p_dec[h % 2][:, P_AT[n]:P_AT[n] + S_COLS[n]],
                                             start=(n == 0), stop=(n == NC - 1))
                    last.then_inc(pv_done, 1)

                def head_mean(h):
                    pe.wait_ge(o_sum_done, l * HEADS + h + 1)
                    pe.matmul(stat_ps, mean_v[:], o_sum, start=True, stop=True).then_inc(mean_done, 1)

                def head_var(h):
                    pe.wait_ge(o_sq_sum, l * HEADS + h + 1)
                    pe.matmul(stat_ps, mean_v[:], o_sum, start=True, stop=True).then_inc(var_done, 1)

                pe.wait_ge(qk_done, l * KB + KB + 1)
                pe.wait_ge(v_done, l * KB + KB + 2)
                scores(0)
                for h in range(HEADS):
                    unit(G, 2 * h, 2 * h % 4, ah, al)
                    if h:
                        head_var(h - 1)
                    if h + 1 < HEADS:
                        scores(h + 1)
                    values(h)
                    unit(G, 2 * h + 1, (2 * h + 1) % 4, ah, al)
                    head_mean(h)
                head_var(HEADS - 1)
                product(GA, ah, al)
                product(CONV, bh, bl, 8)
                product(GB, ah, al)
                product(RET, bh, bl, 16)
                product(WO, ah, al, 24)
                pe.wait_ge(in_lo, l * LAYER_SPLITS + KB + 32)
                ssq(l * 2 + 2)
                product(UP0, bh, bl)
                product(UP1, bh, bl)
                product(DN0, ah, al, 40)
                product(UP2, bh, bl)
                product(DN1, ch, cl, 48)
                product(UP3, bh, bl)
                product(DN2, ah, al, 56)
                product(DN3, ch, cl, 64)
            ssq(LAYERS * 2 + 1)

            IL = KB + LAYERS * LAYER_SPLITS

            def run(u, x_hi, x_lo, dst, n_k=KB, n=T):
                pe.wait_ge(w_lo, u + 3)
                pe.wait_ge(evac, u + 1)
                for k in range(n_k):
                    for q, (w, v) in enumerate(((wh, x_hi), (wh, x_lo), (wl, x_hi))):
                        last = pe.matmul(dst, w[u % 4][:, k], v[:, k * n:(k + 1) * n], start=(k == 0 and q == 0), stop=(k == n_k - 1 and q == 2))
                last.then_inc(mm, 1)

            def loop_units(first, n, x_hi, x_lo, n_k=KB):
                with pe.Fori(0, n // 4) as i:
                    for j in range(4):
                        u = first + j
                        pe.wait_ge(w_lo, i * 4 + (u + 3))
                        pe.wait_ge(evac, i * 4 + (u + 1))
                        for k in range(n_k):
                            for q, (w, v) in enumerate(((wh, x_hi), (wh, x_lo), (wl, x_hi))):
                                last = pe.matmul(unit_ps[u % 2][:], w[u % 4][:, k], v[:, k * T:(k + 1) * T],
                                                 start=(k == 0 and q == 0), stop=(k == n_k - 1 and q == 2))
                        last.then_inc(mm, 1)

            def z(f):
                run(U2 + f, ah, al, unit_ps[f % 2][:])

            def turn(dst, src):
                for c in range(NC):
                    last = pe.transpose(dst[:, c * P:(c + 1) * P], src[:, c * P:(c + 1) * P], ident[:])
                return last

            pe.wait_ge(in_lo, IL + KB)
            ssq(LAYERS * 2 + 2)
            for f in range(5):
                z(f)
            pe.wait_ge(evac, U2 + 3 + 3)
            turn(aux[:, 0], tmp[1][:]).then_inc(z_tr, 1)
            z(5)
            z(6)
            pe.wait_ge(evac, U2 + 5 + 3)
            turn(aux[:, 1], tmp[1][:]).then_inc(z_tr, 1)
            for f in range(7, 12):
                z(f)
            pe.wait_ge(z_act, 1)
            for c in range(NC):
                last = pe.transpose(aux[:, 2, c * GATES:(c + 1) * GATES], tmp[0][0:GATES, c * P:(c + 1) * P], ident[0:GATES, 0:GATES])
            last.then_inc(z_tr, 1)
            z(12)
            z(13)
            pe.wait_ge(c2_in, C2_LOADS * 16)
            pe.wait_ge(win_done, 2)
            pe.wait_ge(att_v, 2)
            pe.wait_ge(gate_tok, 1)
            for i in range(2):
                for g in range(2):
                    lanes = slice(g * HD, g * HD + HD)
                    for n in range(CMP_BLOCK):
                        last = pe.matmul(aux[lanes, 2 * i + g, 0:N_CMP], cmp_w1[i][lanes, n], cmp_win[i][lanes, n],
                                         start=(n == 0), stop=(n == CMP_BLOCK - 1))
                    last.then_inc(cmp_mm, 1)
            z(14)
            pe.wait_ge(cmp_gelu, 4)
            for g in range(2):
                lanes = slice(g * HD, g * HD + HD)
                pe.matmul(o_ps[g][0:HD, 0:N_CMP], cmp_w2[0][lanes], cmp_hid[0][lanes], start=True, stop=True)
                last = pe.matmul(o_ps[g][0:N_CMP, HD:2 * HD], cmp_hid[1][lanes], cmp_w2[1][lanes], start=True, stop=True)
                last.then_inc(cmp_mm, 1)
            z(15)
            z(16)
            pe.wait_ge(z_act, 5)
            for c in range(NC):
                for i in range(2):
                    last = pe.transpose(aux[:, c // 2, (c % 2) * DV + i * P:(c % 2) * DV + (i + 1) * P], y_gm[i][:, c * P:(c + 1) * P], ident[:])
            last.then_inc(gm_tr, 1)
            z(17)
            z(18)
            pe.wait_ge(ws_ready, 1)
            turn(aux[:, 2], gm_ws).then_inc(gm_tr, 1)
            pe.wait_ge(mem_scaled, 2)
            pe.wait_ge(ws_ready, 2)
            for k in range(KB):
                for c in range(2):
                    col = (k % 2) * MEM + c * P
                    last = pe.transpose(aux[:, k // 2, col:col + P], mem_raw[:, c, k * P:(k + 1) * P], ident[:])
                if k % 2:
                    last.then_inc(mem_tr, 1)
            pe.wait_ge(gm_ready, 1)
            pe.wait_ge(cmp_out, 2)
            for g in range(4):
                lanes = slice((g % 2) * HD, (g % 2) * HD + HD)
                for c in range(NC):
                    dst = o_ps[g // 2][lanes, c * P:(c + 1) * P]
                    pe.matmul(dst, v_ln[:, c, g * HD:(g + 1) * HD], gm_wt[:, g * P:(g + 1) * P], start=True, stop=False)
                    last = pe.matmul(dst, one_row[:], tmp2[0:1, g * P:(g + 1) * P], start=False, stop=True)
            last.then_inc(mix_mm, 1)

            pe.wait_ge(mem_lo, KB)

            def mem_unit(f):
                u = MK + f
                dst = unit_ps[0][:, (f % 2) * MEM:(f % 2 + 1) * MEM]
                pe.wait_ge(evac, u + 2)
                if f < KB:
                    run(u, memh, meml, dst, n=MEM)
                    return
                pe.wait_ge(w_lo, u + 3)
                for c in range(2):
                    for k in range(KB):
                        at = slice(k * MEM + c * P, k * MEM + (c + 1) * P)
                        for q, (v, w) in enumerate(((memh, wh), (meml, wh), (memh, wl))):
                            last = pe.matmul(dst[:, c * P:(c + 1) * P], v[:, at], w[u % 4][:, k], start=(k == 0 and q == 0), stop=(k == KB - 1 and q == 2))
                last.then_inc(mm, 1)

            def query(c, g, r):
                lanes = slice((r % 2) * HD, (r % 2) * HD + HD)
                return lanes, q_t[2 * g + r // 2][lanes, c * P:(c + 1) * P]

            def att_scores(b, c, g):
                for r in range(REP):
                    lanes, q = query(c, g, r)
                    last = pe.matmul(aux[:, r, 0:(c + 1) * P], q, k_att[b][g][lanes, 0:(c + 1) * P], start=True, stop=True)
                    if r >= 2:
                        last.then_inc(s_att, 1)

            taken = [0]

            def att_values(b, c, g, stop):
                first = taken[0]
                for n in range(c + 2):
                    if n <= c:
                        bank = o_ps[(n + 1) % 2] if b == 0 else o_ps[(n + c) % 2]
                        if n == 0:
                            pe.wait_ge(pt_ready, taken[0])
                        elif n >= 2:
                            pe.wait_ge(pt_ready, first + n - 1)
                        for r in range(REP):
                            last = pe.transpose(bank[:, r * P:(r + 1) * P], p_att[b][:, r, n * P:(n + 1) * P], ident[:])
                        last.then_inc(t_att, 1)
                        taken[0] += 1
                    if n:
                        m = n - 1
                        pe.wait_ge(pt_ready, first + m + 1)
                        last = pe.matmul(unit_ps[1][0:HD], v_att[b][:, m, g * HD:(g + 1) * HD], pt_att[b][:, m * T:(m + 1) * T],
                                         start=False, stop=(stop and m == c))
                return last

            for it, (c, g) in enumerate(ITS):
                if it:
                    pe.wait_ge(exp_att, 2 * it * REP)
                    pe.wait_ge(pt_ready, taken[0])
                att_scores(0, c, g)
                if it == 0:
                    pe.wait_ge(mixed, 2)
                for r in range(REP):
                    lanes, q = query(c, g, r)
                    last = pe.matmul(o_ps[r % 2][:, r // 2 * 32:r // 2 * 32 + N_CMP], q, k_cmp[g][lanes], start=True, stop=True)
                    if r >= 2:
                        last.then_inc(s_cmp, 1)
                mem_unit(2 * it)
                pe.wait_ge(exp_att, (2 * it + 1) * REP)
                att_scores(1, c, g)
                pe.wait_ge(pc_ready, it + 1)
                for r in range(REP):
                    last = pe.transpose(o_ps[0][0:N_CMP, r * P:(r + 1) * P], p_cmp[:, r], ident[:])
                last.then_inc(t_att, 1)
                taken[0] += 1
                if it:
                    pe.wait_ge(o_taken, 2 * it)
                pe.wait_ge(pt_ready, taken[0])
                pe.matmul(unit_ps[1][0:HD], v_cmp[:, g], tmp[0][0:N_CMP, :], start=True, stop=False)
                pe.wait_ge(p_ready, 2 * it + 1)
                att_values(0, c, g, False)
                mem_unit(2 * it + 1)
                pe.wait_ge(p_ready, 2 * it + 2)
                att_values(1, c, g, True).then_inc(o_att, 1)

            pe.wait_ge(cv_sum, 1)
            pe.matmul(stat_ps, mean_v[:], part_acc[0], start=True, stop=True).then_inc(cv_mean, 1)
            pe.wait_ge(cv_sqs, 1)
            pe.matmul(stat_ps, mean_v[:], part_acc[0], start=True, stop=True).then_inc(cv_var, 1)
            for i, (mean, n) in enumerate(((mean_n, 4), (mean_v, 6), (mean_v, 8))):
                pe.wait_ge(part_src, n + 1)
                pe.matmul(aux[:, i], mean[:], part_acc[i], start=True, stop=True).then_inc(part_ms, 1)
            IL += 2 * KB
            pe.wait_ge(in_lo, IL)
            pe.sem_inc(pe_begun, 1)
            loop_units(OUT, KB, ah, al)
            IL += KB
            pe.wait_ge(in_lo, IL)
            ssq(LAYERS * 2 + 3)
            loop_units(XQ, KB, ch, cl)

            pe.wait_ge(evac, XQ + KB + 2)
            for c in range(NC):
                if c:
                    pe.wait_ge(x_exp, XH * c)
                for h in range(XH):
                    for b in range(2):
                        last = pe.matmul(aux[:, h // 2, (h % 2) * MEM:(h % 2 + 1) * MEM], xq_t[2 * h + b][:, c * P:(c + 1) * P],
                                         mem_k[:, (2 * h + b) * MEM:(2 * h + b + 1) * MEM], start=(b == 0), stop=(b == 1))
                last.then_inc(xs_mm, 1)
                pe.wait_ge(xp_ready, XH * (c + 1))
                if c:
                    pe.wait_ge(xt_copy, 2 * c)
                for m in range(2):
                    for h in range(XH):
                        last = pe.transpose(aux[:, 2 + m, h * P:(h + 1) * P], x_p[:, h, m * P:(m + 1) * P], ident[:])
                    last.then_inc(xt_mm, 1)
            pe.wait_ge(xt_copy, 2 * NC)
            for k in range(KB):
                if k >= 4:
                    pe.wait_ge(in_lo, IL + k - 3)
                for m in range(2):
                    last = pe.matmul(aux[:, k % 4], mem_v[:, m, k * P:(k + 1) * P], x_pt[:, m, k // 2], start=(m == 0), stop=(m == 1))
                last.then_inc(xo_mm, 1)
            IL += KB
            pe.wait_ge(in_lo, IL)
            pe.sem_inc(pe_begun, 1)
            loop_units(XO, KB, ah, al)
            IL += KB
            pe.wait_ge(in_lo, IL)
            ssq(LAYERS * 2 + 4)

            loop_units(UPG[0], 16, ch, cl)
            loop_units(UPG[1], 16, ch, cl)
            pe.wait_ge(in_lo, IL + 8)
            pe.sem_inc(pe_begun, 1)
            loop_units(DNG[0], KB, ah, al)
            loop_units(UPG[2], 12, ch, cl)
            pe.wait_ge(in_lo, IL + 16)
            pe.sem_inc(pe_begun, 1)
            loop_units(DNG[1], KB, bh, bl)
            pe.wait_ge(in_lo, IL + FB)
            pe.sem_inc(pe_begun, 1)
            loop_units(DNG[2], KB, ah, al, GROUPS[2][1])
            ssq(LAYERS * 2 + 5)
            pe.wait_ge(fin_x, KB)
            for c in range(NC):
                for half in range(2):
                    n = 2 * c + half
                    if n >= 4:
                        pe.wait_ge(fin_cp, n - 3)
                    for q in range(4):
                        k = half * 4 + q
                        last = pe.transpose(aux[:, n % 4, q * P:(q + 1) * P], x[:, k * T + c * P:k * T + (c + 1) * P], ident[:])
                    last.then_inc(fin_tr, 1)


        @block.sync
        def _(sp):
            o = out.rearrange("(c p) f -> p c f", p=P)
            for c in range(NC):
                sp.wait_ge(fin_cp, 2 * c + 2)
                sp.dma_start(o[:, c], d1[:, c * D:(c + 1) * D]).then_inc(out_st, 16)
            sp.wait_ge(out_st, 16 * NC)


def shape_constants():
    half = P // 2
    freq = (10000.0 ** (-np.arange(half, dtype=np.float64) / half)).astype(np.float32)
    log_gamma = np.log1p(-np.exp2(-5.0 - np.arange(HEADS, dtype=np.float64)))
    rel = np.arange(T)[None, :] - np.arange(P)[:, None]
    dec = [np.where(rel >= 0, np.exp(g * np.maximum(rel, 0)), 0.0) * P ** -0.5 for g in log_gamma]
    i = np.arange(P)
    tril = i[:, None] >= i[None, :]
    t = i[:, None, None] + P * np.arange(NC)[None, :, None]
    seen = np.arange(N_CMP)[None, None, :] * CMP_STRIDE + CMP_BLOCK - 1 <= t
    return {
        "inv_freq": np.concatenate([freq, freq])[:, None].copy(),
        "ident": np.eye(P, dtype=np.float32),
        "decay": np.concatenate(dec, axis=1).astype(np.float32),
        "tril": tril.astype(np.float32),
        "diag": np.where(tril, 0.0, NEG).astype(np.float32),
        "cmp_add": np.where(seen, 0.0, NEG).astype(np.float32),
        "cmp_keep": seen.astype(np.float32),
    }


def kernel(x, positions, norm_mix, w_in, conv_w, w_conv_out, ret_norm, w_ret_out, w_o, norm_mlp, w_up, w_down, norm_final,
           mem_2, mix_norm_g_2, w_in_2, cmp_pe_2, cmp_w1_2, cmp_w2_2, gmlp_ln_g_2, gmlp_ln_b_2, gmlp_ws_2, gmlp_bs_2,
           conv_dw_w_2, conv_dw_b_2, conv_ln_g_2, conv_ln_b_2, mix_out_g_2, w_out_2, xattn_norm_g_2, mem_norm_g_2,
           xattn_wq_2, xattn_wk_2, xattn_wv_2, xattn_wo_2, ffn_norm_g_2, ffn_w_up_2, ffn_dw_w_2, ffn_dw_b_2, ffn_w_down_2,
           final_norm_g_2):
    import concourse.bacc as bacc
    from concourse.bass_utils import run_bass_kernel_spmd

    nc = bacc.Bacc("TRN2", target_bir_lowering=False, num_devices=1)
    arrays = {
        "x": np.asarray(x).reshape(T, D),
        "positions": np.asarray(positions).reshape(1, T),
        "w_in": w_in, "w_conv_out": w_conv_out, "w_ret_out": w_ret_out, "w_o": w_o, "w_up": w_up, "w_down": w_down,
        "conv_w": np.asarray(conv_w).reshape(LAYERS * 3, D),
        "ret_norm": ret_norm,
        "gains": np.concatenate([np.stack([norm_mix, norm_mlp], axis=1).reshape(2 * LAYERS, D), np.asarray(norm_final)[None]]),
        "mem": np.asarray(mem_2).reshape(MEM, D),
        "w_in_2": w_in_2[0], "w_out_2": w_out_2[0], "wq_2": xattn_wq_2[0], "wk_2": xattn_wk_2[0], "wv_2": xattn_wv_2[0],
        "wo_2": xattn_wo_2[0], "up_2": ffn_w_up_2[0], "down_2": ffn_w_down_2[0],
        "cmp_pe": cmp_pe_2[0], "cmp_w1": cmp_w1_2[0], "cmp_w2": cmp_w2_2[0],
        "gmlp_ws": gmlp_ws_2[0], "gmlp_bs": np.asarray(gmlp_bs_2).reshape(1, 4 * P),
        "gmlp_ln_g": gmlp_ln_g_2, "gmlp_ln_b": gmlp_ln_b_2,
        "gains2": np.concatenate([mix_norm_g_2, mix_out_g_2, xattn_norm_g_2, mem_norm_g_2, ffn_norm_g_2, np.asarray(final_norm_g_2)[None]]),
        "conv_taps": np.concatenate([conv_dw_w_2[0], conv_dw_b_2, conv_ln_g_2, conv_ln_b_2]),
        "ffn_taps": np.concatenate([ffn_dw_w_2[0], ffn_dw_b_2]),
        **shape_constants(),
    }
    arrays = {n: np.ascontiguousarray(a) for n, a in arrays.items()}
    d = {n: nc.dram_tensor(n + "_dram", a.shape, mybir.dt.from_np(a.dtype), kind="ExternalInput").ap() for n, a in arrays.items()}
    out = nc.dram_tensor("out_dram", (T, D), F32, kind="ExternalOutput").ap()
    layer_stack_kernel(nc, d, out)
    r = run_bass_kernel_spmd(nc, [{n + "_dram": a for n, a in arrays.items()}], core_ids=[0])
    return r.results[0]["out_dram"].reshape(1, T, D)
```

```python
from contextlib import ExitStack

import numpy as np

import concourse.bass as bass
from concourse import mybir

F32 = mybir.dt.float32
F32R = mybir.dt.float32r
I32 = mybir.dt.int32
ALU = mybir.AluOpType
ACT = mybir.ActivationFunctionType
AX = mybir.AxisListType.X

P = 128
T = 512
D = 1024
KB = D // P
NC = T // P
LAYERS = 2
HEADS = 4
DV = 256
EPS = 1e-6
TWO_PI = 2 * np.pi
PI_1 = np.float32(6.28125)
PI_2 = np.float32(np.float64(TWO_PI) - np.float64(PI_1))
PI_3 = np.float32(np.float64(TWO_PI) - np.float64(PI_1) - np.float64(PI_2))
ROUND = np.float32(1.5 * 2 ** 23)
PI_UNDER = float(np.nextafter(np.float32(np.pi), np.float32(0)))

VV, QK, CC, CU, CB, G, GA, CONV, GB, RET, WO = 0, 8, 16, 24, 32, 40, 48, 56, 64, 72, 80
UP0, UP1, DN0, UP2, DN1, UP3, DN2, DN3 = 88, 96, 104, 112, 120, 128, 136, 144
UNITS = 152
LAYER_SPLITS = 72
LAYER_SRC = 48
W_IN_COL = {QK: 3 * D, VV: 4 * D, CC: D, CU: 2 * D, CB: 0, G: 5 * D, GA: 6 * D, GB: 7 * D}
U2 = LAYERS * UNITS
NSA_HEADS, NSA_KV, HD, REP = 8, 2, 64, 4
CMP_BLOCK, CMP_STRIDE = 32, 16
N_CMP = (T - CMP_BLOCK) // CMP_STRIDE + 1
TAPS, FFN_TAPS = 31, 3
MEM = 256
XH = 4
F2 = 2816
FB = F2 // P
KV0 = NSA_HEADS * HD
GATES = 3 * NSA_HEADS
GL0 = KV0 + 6 * P
ZG0 = GL0 + GATES
ZC0 = ZG0 + T
Z_COLS = [KV0 + i * P for i in range(6)] + [ZC0 + i * P for i in range(4)] + [GL0] + [ZG0 + i * P for i in range(4)] + [i * P for i in range(4)]
Z_A, Z_GT, Z_GL, Z_U, Z_V, Z_Q = 6, 8, 10, 11, 13, 15
NZ = len(Z_COLS)
MK = U2 + NZ
MV = MK + KB
OUT = MV + KB
XQ = OUT + KB
XO = XQ + KB
FFN = XO + KB
GROUPS = [(0, 8), (8, 8), (16, FB - 16)]
UPG = [FFN, FFN + 16, FFN + 40]
DNG = [FFN + 32, FFN + 52, FFN + 60]
U_END = FFN + 68
ITS = [(c, g) for c in range(NC) for g in range(NSA_KV)]
STEPS2 = [(it, b, c, g) for it, (c, g) in enumerate(ITS) for b in range(2)]
GM_STEP, CV_STEP, TAPS_IN_STEP = 3, 11, (3, 4, 5, 5)
PART_ORDER = [4, 5, 6, 7, 0, 1, 2, 3]
TINY = 1e-30
V1_GAINS2, V1_CONV = 0, 7 * KB
V1_RET = V1_CONV + 3 * LAYERS * KB
V1_FREQ = V1_RET + LAYERS * KB
V1_GAINS = V1_FREQ + 1
V1_END = V1_GAINS + 2 * LAYERS * KB
V2_FFN = 2 * (TAPS + 3)
V2_PE = V2_FFN + 2 * FB * (FFN_TAPS + 1)
V2_END = V2_PE + 2 * CMP_BLOCK
C2_LOADS = 16
NEG = -1e30
S_COLS = [T - P * j for j in range(NC)]
S_AT = [(0, 0), (1, 0), (2, 0), (1, S_COLS[1])]
P_AT = [sum(S_COLS[:j]) for j in range(NC)]


def layer_stack_kernel(nc, d, out):
    ctx = ExitStack()
    with ctx:
        def sb(name, shape, dt=F32):
            return ctx.enter_context(nc.sbuf_tensor(name, shape, dt))

        def sem(name):
            return ctx.enter_context(nc.semaphore(name))

        x = sb("x", [P, KB * T])
        raw = [sb(f"raw{i}", [P, KB, P]) for i in range(2)]
        wh = [sb(f"wh{i}", [P, KB, P], F32R) for i in range(4)]
        wl = [sb(f"wl{i}", [P, KB, P], F32R) for i in range(4)]
        with nc.sbuf_tensor("a_f32", [P, 2 * KB * T], F32) as a_f32:
            af = a_f32
        ah, al = sb("ah", [P, KB * T], F32R), sb("al", [P, KB * T], F32R)
        with nc.sbuf_tensor("b_f32", [P, 2 * KB * T], F32) as b_f32:
            bf = b_f32
        bh, bl = sb("bh", [P, KB * T], F32R), sb("bl", [P, KB * T], F32R)
        with nc.sbuf_tensor("c_f32", [P, 2 * KB * T], F32) as c_f32:
            cf = c_f32
        ch, cl = sb("ch", [P, KB * T], F32R), sb("cl", [P, KB * T], F32R)
        d1, d2 = sb("d1", [P, KB * T]), sb("d2", [P, KB * T])
        with (nc.sbuf_tensor("decay_t", [P, HEADS * T], F32) as decay_t, nc.sbuf_tensor("cos_t", [P, T], F32) as cos_t,
              nc.sbuf_tensor("sin_t", [P, T], F32) as sin_t):
            decay, cos, sin = decay_t, cos_t, sin_t
        hp = [sb(f"hp{i}", [P, TAPS - 1 + T]) for i in range(2)]
        ln_rows = sb("ln_rows", [P, 2, DV])
        diag = sb("diag", [P, P])
        tril = sb("tril", [P, P])
        cmp_add, cmp_keep = sb("cmp_add", [P, NC, N_CMP]), sb("cmp_keep", [P, NC, N_CMP])
        k_cmp = [sb(f"k_cmp{g}", [P, N_CMP]) for g in range(NSA_KV)]
        v_cmp = sb("v_cmp", [N_CMP, NSA_KV, HD])
        cmp_hid = [sb(f"cmp_hid{i}", [P, N_CMP]) for i in range(2)]
        cmp_w2 = [sb(f"cmp_w2{i}", [P, HD]) for i in range(2)]
        gates = sb("gates", [P, NC, GATES])
        vectors2 = sb("vectors2", [P, V2_END])
        p_cmp = sb("p_cmp", [P, REP, N_CMP])
        row = sb("row", [P, 12, REP])
        bn = sb("bn", [P, NC, 6])
        mv = sb("mv", [P, NC, 2])
        mem_ms = sb("mem_ms", [P, 2])
        v_mean = sb("v_mean", [P, NC])
        one_row = sb("one_row", [1, HD])
        rstd = sb("rstd", [P, T])
        tmp = [sb(f"tmp{i}", [P, T]) for i in range(2)]
        tmp2 = sb("tmp2", [P, T])
        ident = sb("ident", [P, P])
        mean_d = sb("mean_d", [P, P])
        mean_v = sb("mean_v", [P, P])
        mean_n = sb("mean_n", [P, P])
        vectors1 = sb("vectors1", [P, V1_END + 2 * KB])
        eps = sb("eps", [P, 2])

        def columns(t, at, n):
            return t[:, at:at + n].rearrange("p (l k) -> p l k", k=KB)
        gains2, conv_w, ret_g = columns(vectors1, V1_GAINS2, 7 * KB), columns(vectors1, V1_CONV, 3 * LAYERS * KB), columns(vectors1, V1_RET, LAYERS * KB)
        inv_freq = vectors1[:, V1_FREQ:V1_FREQ + 1]
        gains = columns(vectors1, V1_GAINS, (2 * LAYERS + 1) * KB)
        gain_sq = vectors1[:, V1_END + KB:]
        conv_taps = vectors2[:, 0:V2_FFN].rearrange("p (l k) -> p l k", k=2)
        ffn_taps = vectors2[:, V2_FFN:V2_PE].rearrange("p (l k) -> p l k", k=2 * FB)
        cmp_pe = [vectors2[:, V2_PE + i * CMP_BLOCK:V2_PE + (i + 1) * CMP_BLOCK] for i in range(2)]

        acc2, rstd_x = d2[:, 5 * T:6 * T], d2[:, 4 * T:5 * T]
        acc, sq, rstd2 = d2[:, 0:T], d2[:, T:2 * T], d2[:, 2 * T:3 * T]
        cos_r, sin_r = d2[:, 3 * T:4 * T], d2[:, 4 * T:5 * T]
        p_dec = [d1[:, 1280 * i:1280 * (i + 1)] for i in range(2)]
        o_at = [(t[:, at:at + T], t[:, at + T:at + 2 * T]) for t, at in ((d2, 4 * T), (d2, 6 * T), (d1, 2560), (d1, 0))]
        o_sum = d1[:, 2560 + 2 * T:2560 + 3 * T]
        v_tok = cf[:, KB * T:2 * KB * T].rearrange("p (c v) -> p c v", c=NC)

        q_t = [cf[:, f * T:(f + 1) * T] for f in range(4)]
        k_att = [[cf[:, (4 + 2 * b + g) * T:(5 + 2 * b + g) * T] for g in range(2)] for b in range(2)]
        v_att = [cf[:, (8 + b) * T:(9 + b) * T].rearrange("p (c v) -> p c v", c=NC) for b in range(2)]
        cmp_in = [cf[:, (10 + i) * T:(11 + i) * T] for i in range(2)]
        v_ln = cf[:, 10 * T:12 * T].rearrange("p (c v) -> p c v", c=NC)
        gm_u = [cf[:, (12 + i) * T:(13 + i) * T] for i in range(2)]
        cv_a = [cf[:, (14 + i) * T:(15 + i) * T] for i in range(2)]
        cmp_w1 = [d1[:, i * 2048:(i + 1) * 2048].rearrange("p (n j) -> p n j", j=HD) for i in range(2)]
        cmp_win = [d2[:, i * 1024:i * 1024 + CMP_BLOCK * N_CMP].rearrange("p (n b) -> p n b", b=N_CMP) for i in range(2)]
        y_nsa = [d2[:, f * T:(f + 1) * T] for f in range(4)]
        y_gm = [d2[:, (4 + f) * T:(5 + f) * T] for f in range(2)]
        y_cv = [d2[:, (6 + f) * T:(7 + f) * T] for f in range(2)]
        gm_ws, gm_wt = d2[:, 6 * T:7 * T], d2[:, 7 * T:8 * T]
        p_att = [af[:, b * 2048:(b + 1) * 2048].rearrange("p (r k) -> p r k", r=REP) for b in range(2)]
        pt_att = [af[:, (2 + b) * 2048:(3 + b) * 2048] for b in range(2)]
        mem_k = bf[:, 4 * T:8 * T]
        mem_v = bf[:, 12 * T:16 * T].rearrange("p (c v) -> p c v", c=2)
        mem_raw = bf[:, 12 * T:16 * T].rearrange("p (c f) -> p c f", c=2)
        memh, meml = bh[:, 0:4 * T], bl[:, 0:4 * T]
        part_r = [d1[:, i * T:(i + 1) * T] for i in range(3)]
        part_acc = [d1[:, (3 + i) * T:(4 + i) * T] for i in range(3)]
        part_sq = [d1[:, 6 * T:7 * T], d1[:, 7 * T:8 * T], cf[:, 14 * T:15 * T], cf[:, 15 * T:16 * T]]
        part_x = [tmp2[:], tmp[0][:]]
        mem_vt = cf[:, 10 * T:14 * T]
        xq_t = [d1[:, f * T:(f + 1) * T] for f in range(KB)]
        x_p = bf[:, 0:2 * T].rearrange("p (c m) -> p c m", c=NC)
        x_pt = d2[:, 2 * T:4 * T].rearrange("p (m q) -> p m q", m=2)

        unit_ps = [ctx.enter_context(nc.psum_tensor(f"unit_ps{i}", [P, T], F32)) for i in range(2)]
        aux = ctx.enter_context(nc.psum_tensor("aux", [P, 4, T], F32))
        o_banks = ctx.enter_context(nc.psum_tensor("o_banks", [P, 2, T], F32))
        o_ps = [o_banks[:, i] for i in range(2)]
        stat_ps = aux[:, 3]

        raw_in = [sem(f"raw_in{i}") for i in range(2)]
        w_hi, w_lo, mm, evac = sem("w_hi"), sem("w_lo"), sem("mm"), sem("evac")
        x_in = [sem(f"x_in{i}") for i in range(4)]
        vec_in, const_in, pos_in = sem("vec_in"), sem("const_in"), sem("pos_in")
        ones_set = sem("ones_set")
        in_src, in_hi, in_lo = sem("in_src"), sem("in_hi"), sem("in_lo")
        sq_done, ssq_src, ssq_mm, std_done = sem("sq_done"), sem("ssq_src"), sem("ssq_mm"), sem("std_done")
        ang_done, trig_done = sem("ang_done"), sem("trig_done")
        dve_step = sem("dve_step")
        qk_done, v_tr, v_done = sem("qk_done"), sem("v_tr"), sem("v_done")
        tap_done, gate_done = sem("tap_done"), sem("gate_done")
        s_done, p_done, pv_done, o_out = sem("s_done"), sem("p_done"), sem("pv_done"), sem("o_out")
        v_mean_done, v_centred = sem("v_mean_done"), sem("v_centred")
        o_sq_sum = sem("o_sq_sum")
        o_sq, var_done, o_std, y_done = sem("o_sq"), sem("var_done"), sem("o_std"), sem("y_done")
        vec2_in, c2_in, mem_in = sem("vec2_in"), sem("c2_in"), sem("mem_in")
        win_done, att_v, z_act, gate_tok = sem("win_done"), sem("att_v"), sem("z_act"), sem("gate_tok")
        z_tr, cmp_mm, cmp_gelu, cmp_out = sem("z_tr"), sem("cmp_mm"), sem("cmp_gelu"), sem("cmp_out")
        gm_tr, gm_var, gm_std, gm_ready, ws_ready, mix_mm, mixed = (sem("gm_tr"), sem("gm_var"), sem("gm_std"), sem("gm_ready"),
                                                             sem("ws_ready"), sem("mix_mm"), sem("mixed"))
        mem_sq, mem_rms, mem_scaled, mem_tr, mem_hi, mem_lo = (sem("mem_sq"), sem("mem_rms"), sem("mem_scaled"), sem("mem_tr"),
                                                               sem("mem_hi"), sem("mem_lo"))
        s_att, s_cmp, shift_att, shift_cmp = sem("s_att"), sem("s_cmp"), sem("shift_att"), sem("shift_cmp")
        exp_att, exp_cmp, p_ready, pc_ready = sem("exp_att"), sem("exp_cmp"), sem("p_ready"), sem("pc_ready")
        t_att, pt_ready, o_att, o_taken = sem("t_att"), sem("pt_ready"), sem("o_att"), sem("o_taken")
        cv_sum, cv_mean, cv_cen, cv_sq, cv_sqs, cv_var, cv_std, cv_n, cv_y = (sem(n) for n in (
            "cv_sum", "cv_mean", "cv_cen", "cv_sq", "cv_sqs", "cv_var", "cv_std", "cv_n", "cv_y"))
        part_src, part_sqd, part_sum, part_ms, part_std = (sem(n) for n in ("part_src", "part_sqd", "part_sum", "part_ms", "part_std"))
        src2 = sem("src2")
        mv_tr, mv_ready, gm_ms_out = sem("mv_tr"), sem("mv_ready"), sem("gm_ms_out")
        xs_mm, xs_shift, x_exp, xp_ready, xt_mm, xt_copy, xo_mm = (sem(n) for n in (
            "xs_mm", "xs_shift", "x_exp", "xp_ready", "xt_mm", "xt_copy", "xo_mm"))
        ffn_src, ffn_tap, ffn_pre, ffn_silu = sem("ffn_src"), sem("ffn_tap"), sem("ffn_pre"), sem("ffn_silu")
        gained, rstd_half, fin_x = sem("gained"), sem("rstd_half"), [sem(f"fin_x{i}") for i in range(2)]
        out_st = sem("out_st")
        dve_begun, pe_begun = sem("dve_begun"), sem("pe_begun")

        block = ctx.enter_context(nc.Block())

        def blk(t, f):
            return t[:, bass.ds(f * T, T)]

        def units(eng, n, body):
            with eng.Fori(0, n // 4) as i:
                for j in range(4):
                    body(i * 4 + j, j)

        @block.sync
        def _(sp):
            w_in = d["w_in"].rearrange("l (k p) f -> p (l k) f", p=P)
            w_sq = {n: d[n].rearrange("l (k p) f -> p (l k) f", p=P) for n in ("w_conv_out", "w_ret_out", "w_o", "w_up", "w_down")}

            with sp.Fori(0, LAYERS) as l:
                def load(first, src, k0, col, n=KB):
                    def body(f, j):
                        u = l * UNITS + first + f
                        sp.wait_ge(w_lo, u + 1)
                        sp.dma_start(raw[j % 2][:], src[:, bass.ds(k0, KB), bass.ds(f * P + col, P)]).then_inc(raw_in[j % 2], 16)
                    units(sp, n, body)

                k_l = l * KB
                for first, col, n in ((VV, W_IN_COL[VV], 8), (QK, W_IN_COL[QK], 8), (CC, W_IN_COL[CC], 16), (CB, W_IN_COL[CB], 8), (G, W_IN_COL[G], 16)):
                    load(first, w_in, k_l, col, n)
                load(CONV, w_sq["w_conv_out"], k_l, 0)
                load(GB, w_in, k_l, W_IN_COL[GB])
                load(RET, w_sq["w_ret_out"], k_l, 0)
                load(WO, w_sq["w_o"], k_l, 0)
                for first, g in ((UP0, 0), (UP1, 1), (DN0, 0), (UP2, 2), (DN1, 1), (UP3, 3), (DN2, 2), (DN3, 3)):
                    if first in (UP0, UP1, UP2, UP3):
                        load(first, w_sq["w_up"], k_l, g * D)
                    else:
                        load(first, w_sq["w_down"], l * 4 * KB + g * KB, 0)

            sp.wait_ge(y_done, LAYERS * HEADS)
            sp.wait_ge(in_lo, LAYERS * LAYER_SPLITS)
            sp.dma_start(vectors2[:], d["vectors2"]).then_inc(vec2_in, 16)
            loads = []
            for i in range(2):
                for half in range(2):
                    lanes = slice(half * HD, half * HD + HD)
                    loads.append((cmp_w1[i][lanes], d["cmp_w1"][i].rearrange("(n e) j -> e n j", e=HD)))
                    loads.append((cmp_w2[i][lanes], d["cmp_w2"][i]))
            loads.append((gm_ws.rearrange("p (g s) -> p g s", g=4), d["gmlp_ws"].rearrange("g t s -> t g s")))
            loads.append((tmp2[0:1, :], d["gmlp_bs"]))
            for i, name in enumerate(("gmlp_ln_g", "gmlp_ln_b")):
                loads.append((ln_rows[:, i], d[name].to_broadcast([P, DV])))
            for name, tile in (("diag", diag), ("tril", tril), ("cmp_add", cmp_add), ("cmp_keep", cmp_keep)):
                loads.append((tile[:], d[name]))
            assert len(loads) == C2_LOADS, len(loads)

            def load2(u, src, col, n_col=P, k0=0, n_k=KB):
                sp.wait_ge(w_lo, u + 1)
                sp.dma_start(raw[u % 2][:, 0:n_k, 0:n_col], src[:, k0:k0 + n_k, col:col + n_col]).then_inc(raw_in[u % 2], 16)

            def load_units(u0, n, src, col, step=P):
                with sp.Fori(0, n // 4) as i:
                    for j in range(4):
                        u = u0 + j
                        sp.wait_ge(w_lo, i * 4 + (u + 1))
                        sp.dma_start(raw[u % 2][:], src[:, :, bass.ds(i * (4 * step) + (col + j * step), P)]).then_inc(raw_in[u % 2], 16)

            v2 = {n: d[n].rearrange("(k p) f -> p k f", p=P) for n in ("w_in_2", "w_out_2", "wq_2", "wk_2", "wv_2", "wo_2", "up_2", "down_2")}
            for f, col in enumerate(Z_COLS):
                load2(U2 + f, v2["w_in_2"], col)
                if f == 0:
                    sp.dma_start(mem_raw, d["mem"].rearrange("(c p) f -> p c f", p=P)).then_inc(mem_in, 16)
                for dst, src in loads[2 * f:2 * f + 2]:
                    sp.dma_start(dst, src).then_inc(c2_in, 16)
            for first, name in ((MK, "wk_2"), (MV, "wv_2"), (OUT, "w_out_2"), (XQ, "wq_2"), (XO, "wo_2")):
                load_units(first, KB, v2[name], 0)

            def load_pairs(u0, b0, n):
                with sp.Fori(0, n // 2) as i:
                    for j in range(4):
                        u = u0 + j
                        sp.wait_ge(w_lo, i * 4 + (u + 1))
                        sp.dma_start(raw[u % 2][:], v2["up_2"][:, :, bass.ds(i * (2 * P) + ((j % 2) * F2 + (b0 + j // 2) * P), P)]).then_inc(raw_in[u % 2], 16)

            def load_down(u0, b0, n):
                with sp.Fori(0, 2) as i:
                    for j in range(4):
                        u = u0 + j
                        sp.wait_ge(w_lo, i * 4 + (u + 1))
                        sp.dma_start(raw[u % 2][:, 0:n], v2["down_2"][:, b0:b0 + n, bass.ds(i * (4 * P) + j * P, P)]).then_inc(raw_in[u % 2], 16)
            load_pairs(UPG[0], *GROUPS[0])
            load_pairs(UPG[1], *GROUPS[1])
            load_down(DNG[0], *GROUPS[0])
            load_pairs(UPG[2], *GROUPS[2])
            load_down(DNG[1], *GROUPS[1])
            load_down(DNG[2], *GROUPS[2])

        @block.gpsimd
        def _(pool):
            pool.memset(eps[:, 0:1], EPS)
            pool.memset(eps[:, 1:2], EPS * EPS)
            pool.memset(mean_d[:], 1.0 / D)
            pool.memset(mean_n[:], 1.0 / (NSA_HEADS * HD))
            pool.memset(mean_v[:], 1.0 / DV).then_inc(ones_set, 1)
            pool.sem_inc(w_lo, 2)

            def body(u, j):
                pool.wait_ge(w_hi, u + 1)
                pool.tensor_tensor(wl[j][:], raw[j % 2][:], wh[j][:].bitcast(F32), ALU.subtract).then_inc(w_lo, 1)
            units(pool, U_END // 4 * 4, body)
            for u in range(U_END // 4 * 4, U_END):
                body(u, u % 4)
            pool.wait_ge(gained, KB)
            pool.wait_ge(rstd_half, 1)
            for k in range(KB):
                early = x[:, k * T:k * T + T // 2]
                pool.tensor_tensor(early, early, rstd[:, 0:T // 2], ALU.mult).then_inc(fin_x[0], 1)

        @block.scalar
        def _(act):
            x_src = d["x"].rearrange("(k p) t -> p k t", p=P)
            x_dst = x[:].rearrange("p (k t) -> p k t", k=KB)

            def load_x(i):
                act.dma_start(x_dst[:, 2 * i:2 * i + 2], x_src[:, 2 * i:2 * i + 2]).then_inc(x_in[i], 16)

            act.dma_start(vectors1[:, 0:V1_END], d["vectors1"]).then_inc(vec_in, 16)
            act.dma_start(tmp2[:].bitcast(I32), d["positions"].to_broadcast([P, T])).then_inc(pos_in, 16)
            for i in range(KB // 2):
                load_x(i)
            act.sem_inc(gate_done, 2)

            def split_w(u, j):
                act.wait_ge(raw_in[j % 2], 16 * 1 + (u - j % 2) * 8)
                act.activation(wh[j][:], raw[j % 2][:], ACT.Copy).then_inc(w_hi, 1)

            split_w(0, 0)
            act.wait_ge(vec_in, 16)
            for k in range(KB):
                act.wait_ge(x_in[k // 2], 16)
                act.activation(blk(ah, k), blk(x, k), ACT.Copy, scale=gains[:, 0, k:k + 1]).then_inc(in_hi, 1)
                act.activation(blk(d1, k), blk(x, k), ACT.Square).then_inc(sq_done, 1)
                if k == 3:
                    split_w(1, 1)
            split_w(2, 2)
            split_w(3, 3)
            for name, tile in (("ident", ident), ("decay", decay)):
                act.dma_start(tile[:], d[name]).then_inc(const_in, 16)
            act.wait_ge(ang_done, 1)
            act.activation(sin[:], sin[:], ACT.Sin).then_inc(trig_done, 1)
            act.activation(cos[:], cos[:], ACT.Sin).then_inc(trig_done, 1)
            act.wait_ge(ones_set, 1)

            def sqrt_ms(n, dst=rstd[:], src=stat_ps, bias=eps[:, 0:1]):
                act.wait_ge(ssq_mm, n)
                act.activation(dst, src, ACT.Sqrt, bias=bias).then_inc(std_done, 1)

            with act.Fori(0, LAYERS) as l:
                u0 = l * UNITS

                def ahead(first, f, j):
                    u = u0 + first + f
                    act.wait_ge(mm, u + 1)
                    split_w_in_loop(u, j)

                def split_w_in_loop(u, j):
                    act.wait_ge(raw_in[j % 2], (u - j % 2) * 8 + 16 * 3)
                    act.activation(wh[j][:], raw[j % 2][:], ACT.Copy).then_inc(w_hi, 1)

                def only_ahead(first, n=KB):
                    units(act, n, lambda f, j: ahead(first, f, j))

                sqrt_ms(l * 2 + 1)
                only_ahead(VV, 24)

                def conv_units(f, j):
                    ahead(CU, f, j)
                    act.wait_ge(evac, u0 + CU + f + 3)
                    act.activation(blk(d2, f), blk(d1, f), ACT.Copy, scale=conv_w[:, bass.ds(l * 3 + 2, 1), bass.ds(f, 1)].rearrange("p a b -> p (a b)")).then_inc(tap_done, 1)
                units(act, KB, conv_units)

                def hi_units(first, src0, dst):
                    def body(f, j):
                        ahead(first, f, j)
                        act.wait_ge(in_src, l * LAYER_SRC + src0 + f + 1)
                        act.activation(blk(dst, f), tmp2[:], ACT.Copy).then_inc(in_hi, 1)
                    units(act, KB, body)
                hi_units(CB, 0, bh)

                for h in range(HEADS):
                    if h:
                        act.wait_ge(var_done, l * HEADS + h)
                        act.activation(o_sum, stat_ps, ACT.Sqrt, bias=eps[:, 0:1]).then_inc(o_std, 1)
                    for f in (2 * h, 2 * h + 1):
                        ahead(G, f, f % 4)
                        act.wait_ge(evac, u0 + G + f + 3)
                        act.activation(blk(d2, f), tmp[f % 2][:], ACT.Silu).then_inc(gate_done, 1)
                        if f % 2 == 0:
                            act.wait_ge(o_out, l * HEADS + h + 1)
                            act.wait_ge(gate_done, l * 24 + f + 3)
                            for o, square in zip(o_at[h], (tmp2[:], tmp[0][:])):
                                act.activation(square, o, ACT.Square).then_inc(o_sq, 1)
                act.wait_ge(var_done, l * HEADS + HEADS)
                act.activation(o_sum, stat_ps, ACT.Sqrt, bias=eps[:, 0:1]).then_inc(o_std, 1)

                act.wait_ge(y_done, l * HEADS + HEADS)

                def ga_units(f, j):
                    ahead(GA, f, j)
                    act.wait_ge(evac, u0 + GA + f + 3)
                    act.activation(blk(d1, f), tmp[j % 2][:], ACT.Sigmoid).then_inc(gate_done, 1)
                units(act, KB, ga_units)
                only_ahead(CONV)

                def gb_units(f, j):
                    ahead(GB, f, j)
                    act.wait_ge(evac, u0 + GB + f + 3)
                    act.activation(blk(cf, f), tmp[j % 2][:], ACT.Sigmoid).then_inc(gate_done, 1)
                    act.activation(blk(bh, f), blk(d2, f), ACT.Copy).then_inc(in_hi, 1)
                units(act, KB, gb_units)
                hi_units(RET, 8, ah)

                def norm_units(first, dst, gain):
                    def body(f, j):
                        ahead(first, f, j)
                        act.wait_ge(evac, u0 + first + f + 3)
                        act.activation(blk(dst, f), blk(x, f), ACT.Copy,
                                       scale=gains[:, bass.ds(l * 2 + gain, 1), bass.ds(f, 1)].rearrange("p a b -> p (a b)")).then_inc(in_hi, 1)
                        act.activation(sq, blk(x, f), ACT.Square).then_inc(sq_done, 1)
                    units(act, KB, body)
                norm_units(WO, bh, 1)
                sqrt_ms(l * 2 + 2)
                hi_units(UP0, 16, ah)
                hi_units(UP1, 24, ch)
                only_ahead(DN0)
                hi_units(UP2, 32, ah)
                only_ahead(DN1)
                hi_units(UP3, 40, ch)
                only_ahead(DN2)
                norm_units(DN3, ah, 2)
            sqrt_ms(LAYERS * 2 + 1, src=aux[:, 2], bias=eps[:, 1:2])
            sqrt_ms(LAYERS * 2 + 2, dst=rstd_x)

            def ahead2(u):
                act.wait_ge(mm, u + 1)
                if u + 4 < U_END:
                    split_w(u + 4, u % 4)

            def loop_ahead(u0, n, body=None):
                with act.Fori(0, n // 4) as i:
                    for j in range(4):
                        u = u0 + j
                        act.wait_ge(mm, i * 4 + (u + 1))
                        slot = u % 4
                        act.wait_ge(raw_in[u % 2], i * 32 + 16 * ((u + 4) // 2 + 1))
                        act.activation(wh[slot][:], raw[u % 2][:], ACT.Copy).then_inc(w_hi, 1)
                        if body:
                            body(i * 4 + j, j)

            ahead2(U2)
            act.wait_ge(mem_in, 16)
            for c in range(2):
                act.activation(bf[:, 4 * T:4 * T + D], mem_raw[:, c], ACT.Square, accum_out=mem_ms[:, c:c + 1]).then_inc(mem_sq, 1)
                act.wait_ge(mem_sq, c + 1)
            act.activation(mem_ms[:], mem_ms[:], ACT.Sqrt, scale=1.0 / D, bias=eps[:, 0:1]).then_inc(mem_rms, 1)
            for f in range(1, Z_GT):
                ahead2(U2 + f)

            def z_gate(f, func, dst, lanes=P):
                ahead2(U2 + f)
                act.wait_ge(evac, U2 + f + 3)
                act.activation(dst, tmp[f % 2][0:lanes], func).then_inc(z_act, 1)

            for f in (Z_GT, Z_GT + 1):
                z_gate(f, ACT.Sigmoid, tmp[f % 2][:])
            z_gate(Z_GL, ACT.Sigmoid, tmp[Z_GL % 2][0:GATES], GATES)
            z_gate(Z_U, ACT.Gelu_apprx_tanh, gm_u[0])
            z_gate(Z_U + 1, ACT.Gelu_apprx_tanh, gm_u[1])
            z_gate(Z_V, ACT.Gelu_apprx_tanh, y_gm[0])
            for i in range(2):
                act.wait_ge(cmp_mm, 2 * i + 2)
                for g in range(2):
                    lanes = slice(g * HD, g * HD + HD)
                    act.activation(cmp_hid[i][lanes], aux[lanes, 2 * i + g, 0:N_CMP], ACT.Gelu_apprx_tanh).then_inc(cmp_gelu, 1)
            z_gate(Z_V + 1, ACT.Gelu_apprx_tanh, y_gm[1])
            ahead2(U2 + Z_Q)
            for k in range(KB):
                act.wait_ge(mem_tr, k // 2 + 1)
                act.activation(memh[:, k * MEM:(k + 1) * MEM], aux[:, k // 2, (k % 2) * MEM:(k % 2 + 1) * MEM], ACT.Copy,
                               scale=gains2[:, 3, k:k + 1]).then_inc(mem_hi, 1)
            ahead2(U2 + Z_Q + 1)
            act.wait_ge(gm_var, 1)
            act.activation(mv[:, :, 1], mv[:, :, 1], ACT.Sqrt, bias=eps[:, 0:1]).then_inc(gm_std, 1)
            for f in (Z_Q + 2, Z_Q + 3):
                ahead2(U2 + f)

            scale = HD ** -0.5
            pts = [0]

            def exp_head(k, h):
                it, b, c, g = STEPS2[k]
                nk = (c + 1) * P
                act.wait_ge(shift_att, k + 1)
                act.activation(p_att[b][:, h, 0:nk], aux[:, h, 0:nk], ACT.Exp, scale=scale, bias=row[:, 4 * b, h:h + 1],
                               accum_out=row[:, 4 * b + 1, h:h + 1]).then_inc(exp_att, 1)

            def exp_compressed(it):
                act.wait_ge(shift_cmp, it + 1)
                act.activation(p_cmp[:], p_cmp[:], ACT.Exp, scale=scale).then_inc(exp_cmp, 1)

            def take_t(dst, src):
                act.wait_ge(t_att, pts[0] + 1)
                act.activation(dst, src, ACT.Copy).then_inc(pt_ready, 1)
                pts[0] += 1

            for h in range(REP):
                exp_head(0, h)
            exp_compressed(0)
            act.wait_ge(mixed, 2)
            for i in range(2):
                act.activation(part_sq[i], y_gm[i], ACT.Square).then_inc(part_sqd, 1)

            def mixer_norms(k):
                if k == CV_STEP:
                    act.wait_ge(cv_cen, 1)
                    for i in range(2):
                        act.activation(part_sq[i], y_cv[i], ACT.Square).then_inc(cv_sq, 1)
                elif k == CV_STEP + 1:
                    act.wait_ge(cv_var, 1)
                    act.activation(part_r[2], unit_ps[0][:], ACT.Sqrt, bias=eps[:, 0:1]).then_inc(cv_std, 1)
                    act.wait_ge(gm_ms_out, 1)
                    act.activation(part_r[1], part_r[1], ACT.Sqrt, bias=eps[:, 0:1]).then_inc(part_std, 1)
                elif k == CV_STEP + 2:
                    act.wait_ge(cv_n, 1)
                    for i in range(2):
                        act.activation(y_cv[i], y_cv[i], ACT.Silu, scale=conv_taps[:, TAPS + 1, i:i + 1], bias=conv_taps[:, TAPS + 2, i:i + 1]).then_inc(cv_y, 1)
                    for i in range(2):
                        act.wait_ge(cv_y, i + 1)
                        act.activation(part_sq[i], y_cv[i], ACT.Square).then_inc(part_sqd, 1)
                elif k == CV_STEP + 3:
                    act.wait_ge(part_ms, 2)
                    act.activation(part_r[2], unit_ps[0][:], ACT.Sqrt, bias=eps[:, 0:1]).then_inc(part_std, 1)

            for k, (it, b, c, g) in enumerate(STEPS2):
                mixer_norms(k)
                if b and it + 1 < len(ITS):
                    exp_compressed(it + 1)
                if b == 0:
                    take_t(tmp[0][0:N_CMP, :], o_ps[0][0:N_CMP, :])
                ahead2(MK + k)
                for n in range(REP):
                    if n <= c:
                        take_t(pt_att[b][:, n * T:(n + 1) * T], o_ps[(n + (c if b else 1)) % 2])
                    if k + 1 < len(STEPS2):
                        exp_head(k + 1, n)

            act.wait_ge(o_taken, 2 * len(ITS))
            for f in range(4):
                act.activation(part_sq[f], y_nsa[f], ACT.Square).then_inc(part_sqd, 1)
            for n, k in enumerate(PART_ORDER):
                if n == 3:
                    act.wait_ge(part_ms, 3)
                    act.activation(part_r[0], aux[:, 0], ACT.Sqrt, bias=eps[:, 0:1]).then_inc(part_std, 1)
                act.wait_ge(src2, n + 1)
                act.activation(blk(ah, k), part_x[n % 2], ACT.Copy).then_inc(in_hi, 1)
            for m in range(2):
                for half in range(2):
                    act.wait_ge(mv_tr, 2 * m + half + 1)
                    act.activation(mem_v[:, m, half * T:(half + 1) * T], aux[:, 1 + half] if m else o_ps[half], ACT.Copy).then_inc(mv_ready, 1)

            def norm_units2(first, gain, dst):
                def body(f, j):
                    act.wait_ge(evac, f + (first + 3))
                    act.activation(blk(dst, f), blk(x, f), ACT.Copy, scale=gains2[:, gain, bass.ds(f, 1)]).then_inc(in_hi, 1)
                    act.activation(sq, blk(x, f), ACT.Square).then_inc(sq_done, 1)
                loop_ahead(first, KB, body)

            norm_units2(OUT, 2, ch)
            sqrt_ms(LAYERS * 2 + 3)

            def x_exps(h):
                act.wait_ge(xs_shift, h + 1)
                s_x = aux[:, 2 * (h % 2):2 * (h % 2) + 2].rearrange("p b (c m) -> p (b c) m", m=MEM)
                for c in range(NC):
                    act.activation(x_p[:, c], s_x[:, c], ACT.Exp, scale=DV ** -0.5,
                                   bias=row[:, 0, c:c + 1], accum_out=row[:, 1, c:c + 1]).then_inc(x_exp, 1)

            def x_turned(h):
                for m in range(2):
                    act.wait_ge(xt_mm, 2 * h + m + 1)
                    act.activation(x_pt[:, m], o_ps[m], ACT.Copy).then_inc(xt_copy, 1)

            def x_hi(h):
                for b in range(2):
                    act.wait_ge(xo_mm, 2 * h + b + 1)
                    act.activation(blk(ah, 2 * h + b), aux[:, 2 * (h % 2) + b], ACT.Copy).then_inc(in_hi, 1)

            for f in range(KB):
                ahead2(XQ + f)
                if f % 2:
                    if f >= 3:
                        x_turned((f - 3) // 2)
                elif f >= 2:
                    if f >= 4:
                        x_hi((f - 4) // 2)
                    x_exps((f - 2) // 2)
            x_exps(XH - 1)
            x_hi(XH - 2)
            x_turned(XH - 1)
            x_hi(XH - 1)
            norm_units2(XO, 4, ch)
            sqrt_ms(LAYERS * 2 + 4)

            def up_pairs(first, b0, n, dst):
                with act.Fori(0, n // 2) as i:
                    for j in range(4):
                        u = first + j
                        act.wait_ge(mm, i * 4 + (u + 1))
                        act.wait_ge(raw_in[u % 2], i * 32 + 16 * ((u + 4) // 2 + 1))
                        act.activation(wh[u % 4][:], raw[u % 2][:], ACT.Copy).then_inc(w_hi, 1)
                        b = i * 2 + ((j % 2) * FB + b0 + j // 2)
                        act.wait_ge(evac, i * 4 + (u + 3))
                        act.activation(part_r[j % 2], tmp[j % 2][:], ACT.Identity, scale=ffn_taps[:, FFN_TAPS - 1, bass.ds(b, 1)],
                                       bias=ffn_taps[:, FFN_TAPS, bass.ds(b, 1)]).then_inc(ffn_tap, 1)
                        if j % 2 == 0:
                            act.wait_ge(ffn_pre, i * 2 + (b0 + j // 2 + 1))
                            act.activation(part_r[0], part_r[0], ACT.Silu).then_inc(ffn_silu, 1)
                        else:
                            act.wait_ge(ffn_src, i * 2 + (b0 + j // 2 + 1))
                            act.activation(blk(dst, i * 2 + j // 2), tmp2[:], ACT.Copy).then_inc(in_hi, 1)

            up_pairs(UPG[0], *GROUPS[0], ah)
            up_pairs(UPG[1], *GROUPS[1], bh)
            loop_ahead(DNG[0], KB)
            up_pairs(UPG[2], *GROUPS[2], ah)
            loop_ahead(DNG[1], KB)

            def last_units(f, j):
                act.wait_ge(evac, f + (DNG[2] + 3))
                act.activation(sq, blk(x, f), ACT.Square).then_inc(sq_done, 1)
                act.wait_ge(sq_done, LAYERS * 16 + 3 * KB + f + 1)
                act.activation(blk(x, f), blk(x, f), ACT.Copy, scale=gains2[:, 5, f:f + 1]).then_inc(gained, 1)
            for f in range(KB):
                ahead2(DNG[2] + f)
                last_units(f, f % 4)
            sqrt_ms(LAYERS * 2 + 5)

        @block.vector
        def _(dve):
            step = [0]

            def done(ins):
                step[0] = step[0] + 1
                ins.then_inc(dve_step, 1)

            def wait_step():
                dve.wait_ge(dve_step, step[0])

            dve.sem_inc(evac, 2)
            dve.sem_inc(v_done, 2)
            dve.sem_inc(qk_done, 1)
            dve.wait_ge(vec_in, 16)
            dve.wait_ge(ones_set, 1)

            done(dve.tensor_tensor(gains[:, 2 * LAYERS], gains2[:, 0], gains2[:, 6], ALU.mult))
            done(dve.tensor_tensor(gain_sq, gains2[:, 6], gains2[:, 6], ALU.mult))
            dve.wait_ge(pos_in, 16)
            done(dve.tensor_copy(tmp[0][:], tmp2[:].bitcast(I32)))
            wait_step()
            done(dve.tensor_scalar(tmp[1][:], tmp[0][:], inv_freq, None, ALU.mult))
            for dst, turn in ((sin, 0.0), (cos, 0.25)):
                wait_step()
                done(dve.tensor_scalar(tmp2[:], tmp[1][:], float(np.float32(1 / TWO_PI)), turn, ALU.mult, ALU.add))
                wait_step()
                done(dve.tensor_scalar(tmp2[:], tmp2[:], float(ROUND), None, ALU.add))
                wait_step()
                done(dve.tensor_scalar(tmp2[:], tmp2[:], float(-ROUND), None, ALU.add))
                src = tmp[1]
                for part in (PI_1, PI_2, PI_3):
                    wait_step()
                    done(dve.scalar_tensor_tensor(out=dst[:], in0=tmp2[:], scalar=float(-part), in1=src[:], op0=ALU.mult, op1=ALU.add))
                    src = dst
                wait_step()
                done(dve.tensor_scalar(dst[:], dst[:], turn * TWO_PI, PI_UNDER, ALU.add, ALU.min))
                wait_step()
                ins = dve.tensor_scalar(dst[:], dst[:], -PI_UNDER, None, ALU.max)
                if turn:
                    ins.then_inc(ang_done, 1)
                else:
                    done(ins)
            for k in range(KB):
                dve.wait_ge(in_hi, k + 1)
                dve.scalar_tensor_tensor(out=blk(al, k), in0=blk(x, k), scalar=gains[:, 0, k:k + 1], in1=blk(ah, k).bitcast(F32),
                                         op0=ALU.mult, op1=ALU.subtract).then_inc(in_lo, 1)
            for k in range(1, KB):
                dve.wait_ge(sq_done, k + 1)
                wait_step()
                done(dve.tensor_tensor(acc, acc if k > 1 else blk(d1, 0), blk(d1, k), ALU.add))
            wait_step()
            dve.sem_inc(ssq_src, 1)
            dve.wait_ge(trig_done, 2)
            done(dve.tensor_scalar(sin[64:128], sin[64:128], -1.0, None, ALU.mult))

            base = step[0]
            STEPS = 61
            with dve.Fori(0, LAYERS) as l:
                u0 = l * UNITS
                begun = l * STEPS + base
                step[0] = begun
                cnt = [0]

                def done_l(ins):
                    cnt[0] += 1
                    ins.then_inc(dve_step, 1)

                def wait_l():
                    dve.wait_ge(dve_step, l * STEPS + (base + cnt[0]))

                def loop(n, per, body):
                    with dve.Fori(0, n // 4) as i:
                        for j in range(4):
                            used = [0]

                            def step_done(ins):
                                used[0] += 1
                                ins.then_inc(dve_step, 1)

                            def step_wait(i=i, j=j, used=used):
                                dve.wait_ge(dve_step, l * STEPS + i * (4 * per) + (base + cnt[0] + j * per + used[0]))

                            body(i * 4 + j, j, step_done, step_wait)
                            assert used[0] == per, (used, per)
                    cnt[0] += n * per

                def unit_done(first, f):
                    dve.wait_ge(mm, u0 + first + f + 1)

                def norm_factor(n):
                    dve.wait_ge(std_done, n)
                    done_l(dve.reciprocal(rstd[:], rstd[:]))
                    wait_l()
                    dve.sem_inc(dve_begun, 1)

                norm_factor(l * 2 + 1)
                def v_units(f, j, step_done, step_wait):
                    unit_done(VV, f)
                    dve.wait_ge(qk_done, l * KB + 1)
                    dve.tensor_tensor(tmp[j % 2][:], unit_ps[j % 2][:], rstd[:], ALU.mult).then_inc(evac, 1)
                    dve.wait_ge(v_tr, l * KB + f + 1)
                    dve.tensor_copy(v_tok[:, :, bass.ds(f * P, P)], aux[:, j % 2].rearrange("p (c v) -> p c v", c=NC)).then_inc(v_done, 1)
                    if j % 2:
                        head = v_tok[:, :, bass.ds(f * P + (-P), DV)]
                        dve.wait_ge(v_done, l * KB + f + 3)
                        dve.tensor_reduce(v_mean[:], head, AX, ALU.add).then_inc(v_mean_done, 1)
                        dve.wait_ge(v_mean_done, l * KB + f)
                        dve.tensor_scalar(v_mean[:], v_mean[:], -1.0 / DV, None, ALU.mult).then_inc(v_mean_done, 1)
                        dve.wait_ge(v_mean_done, l * KB + f + 1)
                        dve.tensor_tensor(head, head, v_mean[:].unsqueeze(2).broadcast_to([P, NC, DV]), ALU.add).then_inc(v_centred, 1)
                for f in range(KB):
                    v_units(f, f % 4, None, None)
                    if f == 3:
                        done_l(dve.tensor_tensor(cos_r, cos[:], rstd[:], ALU.mult))
                        done_l(dve.tensor_tensor(sin_r, sin[:], rstd[:], ALU.mult))
                        done_l(dve.tensor_tensor(rstd2, rstd[:], rstd[:], ALU.mult))
                wait_l()
                dve.sem_inc(dve_begun, 1)

                def rope(f, j, step_done, step_wait):
                    ps = unit_ps[j % 2]
                    unit_done(QK, f)
                    dve.wait_ge(qk_done, l * KB + f + 1)
                    dve.tensor_tensor(tmp[0][:], ps[:], cos_r, ALU.mult)
                    dve.tensor_tensor(tmp[1][0:64], ps[64:128], sin_r[64:128], ALU.mult)
                    dve.tensor_tensor(tmp[1][64:128], ps[0:64], sin_r[0:64], ALU.mult).then_inc(evac, 1)
                    dve.wait_ge(evac, u0 + QK + f + 3)
                    dve.tensor_tensor(blk(cf, f), tmp[0][:], tmp[1][:], ALU.add).then_inc(qk_done, 1)
                loop(KB, 0, rope)

                def c_units(f, j, step_done, step_wait):
                    unit_done(CC, f)
                    dve.tensor_tensor(blk(d1, f), unit_ps[j % 2][:], rstd2, ALU.mult).then_inc(evac, 1)
                loop(KB, 0, c_units)

                def tap(n, f):
                    return conv_w[:, bass.ds(l * 3 + n, 1), bass.ds(f, 1)].rearrange("p a b -> p (a b)")

                def u_units(f, j, step_done, step_wait):
                    unit_done(CU, f)
                    dve.tensor_tensor(blk(d1, f), unit_ps[j % 2][:], blk(d1, f), ALU.mult).then_inc(evac, 1)
                    dve.wait_ge(tap_done, l * KB + f + 1)
                    for shift, n in ((1, 1), (2, 0)):
                        into = d2[:, bass.ds(f * T + shift, T - shift)]
                        step_done(dve.scalar_tensor_tensor(out=into, in0=d1[:, bass.ds(f * T, T - shift)], scalar=tap(n, f), in1=into,
                                                           op0=ALU.mult, op1=ALU.add))
                        step_wait()
                loop(KB, 2, u_units)

                def split_lo(dst_h, dst_l, f, n):
                    dve.wait_ge(in_hi, l * LAYER_SPLITS + KB + n + f + 1)
                    dve.tensor_tensor(blk(dst_l, f), tmp2[:], blk(dst_h, f).bitcast(F32), ALU.subtract).then_inc(in_lo, 1)

                def b_units(f, j, step_done, step_wait):
                    unit_done(CB, f)
                    dve.tensor_tensor(tmp[0][:], unit_ps[j % 2][:], rstd[:], ALU.mult).then_inc(evac, 1)
                    dve.wait_ge(evac, u0 + CB + f + 3)
                    dve.wait_ge(in_lo, l * LAYER_SPLITS + KB + f)
                    dve.tensor_tensor(tmp2[:], tmp[0][:], blk(d2, f), ALU.mult).then_inc(in_src, 1)
                    split_lo(bh, bl, f, 0)
                loop(KB, 0, b_units)

                def g_unit(f):
                    unit_done(G, f)
                    dve.wait_ge(gate_done, l * 24 + f + 1)
                    dve.tensor_tensor(tmp[f % 2][:], unit_ps[f % 2][:], rstd[:], ALU.mult).then_inc(evac, 1)

                def decay_scores(h):
                    if h == 0:
                        dve.wait_ge(const_in, 16 * 2)
                    dve.wait_ge(s_done, l * HEADS + h + 1)
                    for n in range(NC):
                        bank, col = S_AT[n]
                        ins = dve.tensor_tensor(p_dec[h % 2][:, P_AT[n]:P_AT[n] + S_COLS[n]], aux[:, bank, col:col + S_COLS[n]],
                                                decay[:, h * T:h * T + S_COLS[n]], ALU.mult)
                    ins.then_inc(p_done, 1)

                def take_o(h):
                    dve.wait_ge(pv_done, l * HEADS + h + 1)
                    dve.tensor_copy(o_at[h][0], o_ps[0][:])
                    dve.tensor_copy(o_at[h][1], o_ps[1][:]).then_inc(o_out, 1)

                def sum_squares(h):
                    dve.wait_ge(o_sq, l * KB + 2 * h + 2)
                    dve.tensor_tensor(tmp2[:], tmp2[:], tmp[0][:], ALU.add).then_inc(o_sq_sum, 1)

                def head_norm(h):
                    dve.wait_ge(o_std, l * HEADS + h + 1)
                    done_l(dve.reciprocal(o_sum, o_sum))
                    if h + 1 < HEADS:
                        sum_squares(h + 1)
                    wait_l()
                    for n in range(2):
                        f = 2 * h + n
                        done_l(dve.scalar_tensor_tensor(out=o_at[h][n], in0=o_at[h][n], scalar=ret_g[:, bass.ds(l, 1), f:f + 1].rearrange("p a b -> p (a b)"),
                                                        in1=o_sum, op0=ALU.mult, op1=ALU.mult))
                    dve.wait_ge(gate_done, l * 24 + 2 * h + 2 + 2)
                    for n in range(2):
                        f = 2 * h + n
                        wait_l()
                        ins = dve.tensor_tensor(blk(d2, f), o_at[h][n], blk(d2, f), ALU.mult)
                    ins.then_inc(y_done, 1)

                decay_scores(0)
                for h in range(HEADS):
                    if h:
                        dve.wait_ge(var_done, l * HEADS + h)
                    g_unit(2 * h)
                    if h + 1 < HEADS:
                        decay_scores(h + 1)
                    take_o(h)
                    if h:
                        head_norm(h - 1)
                    else:
                        sum_squares(0)
                    g_unit(2 * h + 1)
                head_norm(HEADS - 1)

                def gate_units(first, n):
                    def body(f, j, step_done, step_wait):
                        unit_done(first, f)
                        dve.wait_ge(gate_done, l * 24 + n + f + 1)
                        dve.tensor_tensor(tmp[j % 2][:], unit_ps[j % 2][:], rstd[:], ALU.mult).then_inc(evac, 1)
                        if first == GB:
                            dve.wait_ge(in_hi, l * LAYER_SPLITS + KB + 8 + f + 1)
                            dve.tensor_tensor(blk(bl, f), blk(d2, f), blk(bh, f).bitcast(F32), ALU.subtract).then_inc(in_lo, 1)
                    return body
                loop(KB, 0, gate_units(GA, 8))

                dve.wait_ge(gate_done, l * 24 + 16 + 2)
                dve.sem_inc(dve_begun, 1)

                def conv_units(f, j, step_done, step_wait):
                    unit_done(CONV, f)
                    dve.tensor_tensor(blk(d1, f), unit_ps[j % 2][:], blk(d1, f), ALU.mult).then_inc(evac, 1)
                loop(KB, 0, conv_units)
                loop(KB, 0, gate_units(GB, 16))

                dve.wait_ge(gate_done, l * 24 + 24 + 2)
                dve.sem_inc(dve_begun, 1)

                def ret_units(f, j, step_done, step_wait):
                    unit_done(RET, f)
                    dve.tensor_tensor(tmp[0][:], unit_ps[j % 2][:], blk(cf, f), ALU.mult).then_inc(evac, 1)
                    dve.wait_ge(evac, u0 + RET + f + 3)
                    dve.wait_ge(in_lo, l * LAYER_SPLITS + KB + 16 + f)
                    dve.tensor_tensor(tmp2[:], tmp[0][:], blk(d1, f), ALU.add).then_inc(in_src, 1)
                    split_lo(ah, al, f, 16)
                loop(KB, 0, ret_units)

                def norm_units(first, dst_h, dst_l, gain, n, sq0):
                    done_l(dve.memset(acc, 0.0))
                    if gain == 2:
                        done_l(dve.memset(acc2, 0.0))

                    def body(f, j, step_done, step_wait):
                        unit_done(first, f)
                        dve.tensor_tensor(blk(x, f), unit_ps[j % 2][:], blk(x, f), ALU.add).then_inc(evac, 1)
                        dve.wait_ge(in_hi, l * LAYER_SPLITS + KB + n + f + 1)
                        dve.scalar_tensor_tensor(out=blk(dst_l, f), in0=blk(x, f), scalar=gains[:, bass.ds(l * 2 + gain, 1), bass.ds(f, 1)].rearrange("p a b -> p (a b)"),
                                                 in1=blk(dst_h, f).bitcast(F32), op0=ALU.mult, op1=ALU.subtract).then_inc(in_lo, 1)
                        dve.wait_ge(sq_done, l * 16 + KB + sq0 + f + 1)
                        step_wait()
                        if gain == 2:
                            step_done(dve.scalar_tensor_tensor(out=acc2, in0=sq, scalar=gain_sq[:, bass.ds(f, 1)], in1=acc2, op0=ALU.mult, op1=ALU.add))
                        step_done(dve.tensor_tensor(acc, acc, sq, ALU.add))
                    loop(KB, 2 if gain == 2 else 1, body)
                    wait_l()
                    if gain == 2:
                        done_l(dve.scalar_tensor_tensor(out=acc2, in0=acc, scalar=EPS, in1=acc2, op0=ALU.mult, op1=ALU.add))
                        wait_l()
                    dve.sem_inc(ssq_src, 1)
                norm_units(WO, bh, bl, 1, 24, 0)

                norm_factor(l * 2 + 2)

                def up_units(first, dst_h, dst_l, n):
                    def body(f, j, step_done, step_wait):
                        unit_done(first, f)
                        dve.tensor_tensor(tmp[0][:], unit_ps[j % 2][:], rstd[:], ALU.mult).then_inc(evac, 1)
                        dve.wait_ge(evac, u0 + first + f + 3)
                        dve.wait_ge(in_lo, l * LAYER_SPLITS + KB + n + f)
                        dve.scalar_tensor_tensor(out=tmp2[:], in0=tmp[0][:], scalar=0.0, in1=tmp[0][:], op0=ALU.max, op1=ALU.mult).then_inc(in_src, 1)
                        split_lo(dst_h, dst_l, f, n)
                    loop(KB, 0, body)

                def down_units(first):
                    def body(f, j, step_done, step_wait):
                        unit_done(first, f)
                        dve.tensor_tensor(blk(x, f), unit_ps[j % 2][:], blk(x, f), ALU.add).then_inc(evac, 1)
                    loop(KB, 0, body)

                up_units(UP0, ah, al, 32)
                up_units(UP1, ch, cl, 40)
                down_units(DN0)
                up_units(UP2, ah, al, 48)
                down_units(DN1)
                up_units(UP3, ch, cl, 56)
                down_units(DN2)
                norm_units(DN3, ah, al, 2, 64, 8)
                assert cnt[0] == STEPS, cnt
            step[0] = base + LAYERS * STEPS

            IL = KB + LAYERS * LAYER_SPLITS
            SQ = LAYERS * 2 * KB
            count = {id(dve_step): step[0], id(evac): 2 + U2, id(in_lo): IL}
            last = [(dve_step, step[0])]

            def go():
                dve.wait_ge(*last[0])

            def did(ins, s=dve_step):
                count[id(s)] = count.get(id(s), 0) + 1
                ins.then_inc(s, 1)
                last[0] = (s, count[id(s)])

            def mult(dst, a, b, s=dve_step):
                go()
                did(dve.tensor_tensor(dst, a, b, ALU.mult), s)

            def copy(dst, src, s=dve_step):
                go()
                did(dve.tensor_copy(dst, src), s)

            def factor(n):
                dve.wait_ge(std_done, n)
                go()
                did(dve.reciprocal(rstd[:], rstd[:]))

            factor(LAYERS * 2 + 1)

            def first_norm(k):
                go()
                did(dve.scalar_tensor_tensor(out=blk(x, k), in0=blk(x, k), scalar=gains2[:, 6, k:k + 1], in1=rstd_x,
                                             op0=ALU.mult, op1=ALU.mult))

            def z_done(f):
                dve.wait_ge(mm, U2 + f + 1)

            def z_ps(f):
                return unit_ps[f % 2]

            def z_scaled(f, dst):
                z_done(f)
                mult(dst, z_ps(f)[:], rstd[:], evac)

            for i in range(2):
                z_scaled(i, cmp_in[i])
                dve.wait_ge(vec2_in, 16)
                dve.wait_ge(std_done, LAYERS * 2 + 2)
                go()
                src = cmp_in[i]
                win_src = bass.AP(src.tensor, src.offset, [src.ap[0], [1, CMP_BLOCK], [CMP_STRIDE, N_CMP]])
                did(dve.tensor_tensor(cmp_win[i], win_src, cmp_pe[i].unsqueeze(2).broadcast_to([P, CMP_BLOCK, N_CMP]), ALU.add), win_done)

            def z_keys(f, b):
                z_done(f)
                for g in range(2):
                    src = slice(g * HD, g * HD + HD)
                    for half in range(2):
                        mult(k_att[b][g][half * HD:half * HD + HD], z_ps(f)[src], rstd[src], evac if (g, half) == (1, 1) else dve_step)

            def z_values(b):
                dve.wait_ge(z_tr, b + 1)
                copy(v_att[b], aux[:, b].rearrange("p (c v) -> p c v", c=NC), att_v)

            def taps():
                for n in range(TAPS):
                    for i in range(2):
                        src, w = hp[i][:, n:n + T], conv_taps[:, n, i:i + 1]
                        go()
                        if n == 0:
                            did(dve.tensor_scalar(cv_a[i], src, w, conv_taps[:, TAPS, i:i + 1], ALU.mult, ALU.add))
                        else:
                            did(dve.scalar_tensor_tensor(out=cv_a[i], in0=src, scalar=w, in1=cv_a[i], op0=ALU.mult, op1=ALU.add))
                        yield
            tap = taps()

            def some_taps(n):
                for _ in range(n):
                    next(tap, None)

            go()
            did(dve.reciprocal(rstd_x, rstd_x))
            z_keys(2, 0)
            z_scaled(3, tmp[1][:])
            z_keys(4, 1)
            z_values(0)
            z_scaled(5, tmp[1][:])
            z_scaled(Z_A, cv_a[0])
            z_values(1)
            first_norm(0)
            first_norm(1)
            z_scaled(Z_A + 1, cv_a[1])
            first_norm(2)
            first_norm(3)
            z_scaled(Z_GT, tmp[0][:])
            first_norm(4)
            first_norm(5)
            for i in range(2):
                go()
                did(dve.memset(hp[i][:, 0:TAPS - 1], 0.0))
            dve.wait_ge(z_act, 1)
            mult(hp[0][:, TAPS - 1:], cv_a[0], tmp[0][:])
            z_scaled(Z_GT + 1, tmp[1][:])
            first_norm(6)
            first_norm(7)
            dve.wait_ge(z_act, 2)
            mult(hp[1][:, TAPS - 1:], cv_a[1], tmp[1][:])
            some_taps(1)
            z_done(Z_GL)
            mult(tmp[0][0:GATES], z_ps(Z_GL)[0:GATES], rstd[0:GATES], evac)
            some_taps(4)
            z_scaled(Z_U, tmp[1][:])
            dve.wait_ge(z_tr, 3)
            copy(gates[:], aux[:, 2, 0:NC * GATES].rearrange("p (c h) -> p c h", c=NC), gate_tok)
            z_scaled(Z_U + 1, tmp[0][:])
            some_taps(2)
            dve.wait_ge(mem_rms, 1)
            go()
            did(dve.reciprocal(mem_ms[:], mem_ms[:]))
            for c in range(2):
                go()
                did(dve.tensor_scalar(mem_raw[:, c], mem_raw[:, c], mem_ms[:, c:c + 1], None, ALU.mult), mem_scaled)
            go()
            did(dve.memset(one_row[:], 1.0))
            dve.wait_ge(z_act, 4)
            z_scaled(Z_V, tmp[1][:])
            some_taps(10)
            dve.wait_ge(z_act, 5)
            z_scaled(Z_V + 1, tmp[0][:])
            dve.wait_ge(cmp_mm, 6)
            for g in range(2):
                copy(k_cmp[g][0:HD], o_ps[g][0:HD, 0:N_CMP])
                copy(k_cmp[g][HD:2 * HD], o_ps[g][0:HD, 0:N_CMP])
                copy(v_cmp[:, g], o_ps[g][0:N_CMP, HD:2 * HD], cmp_out)
            dve.wait_ge(c2_in, C2_LOADS * 16)
            ws = gm_ws.rearrange("p (g s) -> p g s", g=4)
            mult(ws, ws, tril[:].unsqueeze(1).broadcast_to([P, 4, P]), ws_ready)
            z_scaled(Z_Q, q_t[0])
            for k in range(KB):
                dve.wait_ge(mem_hi, k // 2 * 2 + 2)
                lanes = slice(k * MEM, (k + 1) * MEM)
                go()
                did(dve.scalar_tensor_tensor(out=meml[:, lanes], in0=aux[:, k // 2, (k % 2) * MEM:(k % 2 + 1) * MEM], scalar=gains2[:, 3, k:k + 1],
                                             in1=memh[:, lanes].bitcast(F32), op0=ALU.mult, op1=ALU.subtract), mem_lo)
            z_scaled(Z_Q + 1, q_t[1])
            dve.wait_ge(gm_tr, 1)
            for n in range(2):
                copy(v_ln[:, 2 * n:2 * n + 2], aux[:, n].rearrange("p (c v) -> p c v", c=2))
            dve.wait_ge(gm_tr, 2)
            copy(gm_wt, aux[:, 2], ws_ready)
            for c in range(NC):
                go()
                did(dve.bn_stats(bn[:, c], v_ln[:, c]))
            for c in range(NC):
                go()
                did(dve.bn_aggr(mv[:, c], bn[:, c]), gm_var if c == NC - 1 else dve_step)
            dve.wait_ge(gm_std, 1)
            go()
            did(dve.reciprocal(mv[:, :, 1], mv[:, :, 1]))
            for c in range(NC):
                go()
                did(dve.tensor_scalar(v_ln[:, c], v_ln[:, c], mv[:, c, 0:1], mv[:, c, 1:2], ALU.subtract, ALU.mult))
            mult(v_ln, v_ln, ln_rows[:, 0].unsqueeze(1).broadcast_to([P, NC, DV]))
            go()
            did(dve.tensor_tensor(v_ln, v_ln, ln_rows[:, 1].unsqueeze(1).broadcast_to([P, NC, DV]), ALU.add), gm_ready)
            for f in (2, 3):
                z_scaled(Z_Q + f, q_t[f])
            def mem_unit(f):
                dve.wait_ge(mm, MK + f + 1)
                src = unit_ps[0][:, (f % 2) * MEM:(f % 2 + 1) * MEM]
                copy((mem_k if f < KB else mem_vt)[:, f % KB * MEM:(f % KB + 1) * MEM], src, evac)

            scale = HD ** -0.5

            def shift(k):
                it, b, c, g = STEPS2[k]
                nk = (c + 1) * P
                dve.wait_ge(s_att, 2 * (k + 1))
                here = aux[:, :, c * P:nk]
                go()
                did(dve.tensor_tensor(here, here, diag[:].unsqueeze(1).broadcast_to([P, REP, P]), ALU.add))
                go()
                did(dve.tensor_reduce(row[:, 4 * b + 2], aux[:, :, 0:nk], AX, ALU.max))
                go()
                did(dve.tensor_scalar(row[:, 4 * b], row[:, 4 * b + 2], -scale, None, ALU.mult), shift_att)

            def gate_of(c, g, branch):
                return gates[:, c, g * REP * 3 + branch:(g + 1) * REP * 3 - 2 + branch:3]

            def weigh(k):
                it, b, c, g = STEPS2[k]
                nk = (c + 1) * P
                dve.wait_ge(exp_att, REP * (k + 1))
                go()
                did(dve.reciprocal(row[:, 4 * b + 3], row[:, 4 * b + 1]))
                mult(row[:, 4 * b + 3], row[:, 4 * b + 3], gate_of(c, g, 1 + b))
                for h in range(REP):
                    go()
                    did(dve.tensor_scalar(p_att[b][:, h, 0:nk], p_att[b][:, h, 0:nk], row[:, 4 * b + 3, h:h + 1], None, ALU.mult),
                        p_ready if h == REP - 1 else dve_step)

            def compressed_scores(it):
                c, g = ITS[it]
                dve.wait_ge(s_cmp, 2 * it + 2)
                go()
                for b in range(2):
                    did(dve.tensor_tensor(p_cmp[:, b::2], o_ps[b][:, 0:64].rearrange("p (r n) -> p r n", n=32)[:, :, 0:N_CMP],
                                          cmp_add[:, c].unsqueeze(1).broadcast_to([P, 2, N_CMP]), ALU.add))
                go()
                did(dve.tensor_reduce(row[:, 8], p_cmp[:], AX, ALU.max))
                go()
                did(dve.tensor_tensor(p_cmp[:], p_cmp[:], row[:, 8].unsqueeze(2).broadcast_to([P, REP, N_CMP]), ALU.subtract), shift_cmp)

            def compressed_weights(it):
                c, g = ITS[it]
                dve.wait_ge(exp_cmp, it + 1)
                mult(p_cmp[:], p_cmp[:], cmp_keep[:, c].unsqueeze(1).broadcast_to([P, REP, N_CMP]))
                go()
                did(dve.tensor_reduce(row[:, 9], p_cmp[:], AX, ALU.add))
                go()
                did(dve.tensor_scalar(row[:, 9], row[:, 9], TINY, None, ALU.max))
                go()
                did(dve.reciprocal(row[:, 9], row[:, 9]))
                mult(row[:, 9], row[:, 9], gate_of(c, g, 0))
                mult(p_cmp[:], p_cmp[:], row[:, 9].unsqueeze(2).broadcast_to([P, REP, N_CMP]), pc_ready)

            shift(0)
            dve.wait_ge(mix_mm, 1)
            for i in range(2):
                mult(y_gm[i], gm_u[i], o_ps[i][:], mixed)
            compressed_scores(0)
            compressed_weights(0)

            def sum_of(dst, a, b, s):
                go()
                did(dve.tensor_tensor(dst, a, b, ALU.add), s)

            def mixer_norms_first(k):
                if k == GM_STEP:
                    dve.wait_ge(part_ms, 1)
                    copy(part_r[1], unit_ps[0][:], gm_ms_out)
                elif k == CV_STEP:
                    dve.wait_ge(cv_mean, 1)
                    for i in range(2):
                        go()
                        did(dve.tensor_tensor(y_cv[i], cv_a[i], unit_ps[0][:], ALU.subtract), cv_cen if i else dve_step)

            def mixer_norms_last(k):
                if k == 1:
                    dve.wait_ge(part_sqd, 2)
                    sum_of(part_acc[1], part_sq[0], part_sq[1], part_src)
                elif k == CV_STEP + 3:
                    dve.wait_ge(part_std, 1)
                    go()
                    did(dve.reciprocal(part_r[1], part_r[1]))
                elif k == CV_STEP - 1:
                    some_taps(2 * TAPS)
                    sum_of(part_acc[2], cv_a[0], cv_a[1], cv_sum)
                elif k == CV_STEP:
                    dve.wait_ge(cv_sq, 2)
                    sum_of(part_acc[2], part_sq[0], part_sq[1], cv_sqs)
                elif k == CV_STEP + 1:
                    dve.wait_ge(cv_std, 1)
                    go()
                    did(dve.reciprocal(part_r[2], part_r[2]))
                    for i in range(2):
                        mult(y_cv[i], y_cv[i], part_r[2], cv_n if i else dve_step)
                elif k == CV_STEP + 2:
                    dve.wait_ge(part_sqd, 4)
                    sum_of(part_acc[2], part_sq[0], part_sq[1], part_src)
                elif k == CV_STEP + 4:
                    dve.wait_ge(part_std, 2)
                    go()
                    did(dve.reciprocal(part_r[2], part_r[2]))

            for k, (it, b, c, g) in enumerate(STEPS2):
                mixer_norms_first(k)
                weigh(k)
                if k + 1 < len(STEPS2):
                    if b:
                        compressed_scores(it + 1)
                    shift(k + 1)
                    if b:
                        compressed_weights(it + 1)
                mem_unit(k)
                some_taps(TAPS_IN_STEP[c])
                mixer_norms_last(k)
                if b:
                    dve.wait_ge(o_att, it + 1)
                    o = unit_ps[1][0:HD].rearrange("p (b r t) -> p b r t", b=2, r=2)
                    for half in range(2):
                        dst = d2[half * HD:half * HD + HD, 2 * g * T:(2 * g + 2) * T].rearrange("p (b t) -> p b t", b=2)[:, :, c * P:(c + 1) * P]
                        copy(dst, o[:, :, half], o_taken)
            for f in range(1, 4):
                dve.wait_ge(part_sqd, 4 + f + 1)
                sum_of(part_acc[0], part_acc[0] if f > 1 else part_sq[0], part_sq[f], part_src if f == 3 else dve_step)
            part_of = [0] * 4 + [1] * 2 + [2] * 2

            def part_norm(n):
                k = PART_ORDER[n]
                if k == 0:
                    dve.wait_ge(part_std, 3)
                    go()
                    did(dve.reciprocal(part_r[0], part_r[0]))
                go()
                did(dve.scalar_tensor_tensor(out=part_x[n % 2], in0=d2[:, k * T:(k + 1) * T], scalar=gains2[:, 1, k:k + 1], in1=part_r[part_of[k]],
                                             op0=ALU.mult, op1=ALU.mult), src2)

            def part_lo(n):
                k = PART_ORDER[n]
                dve.wait_ge(in_hi, IL + n + 1)
                go()
                did(dve.tensor_tensor(blk(al, k), part_x[n % 2], blk(ah, k).bitcast(F32), ALU.subtract), in_lo)

            part_norm(0)
            for n in range(1, KB):
                part_norm(n)
                part_lo(n - 1)
            part_lo(KB - 1)
            IL += KB
            SQ += KB

            def norm_product(first, gain, il, sq_n):
                go()
                did(dve.memset(acc, 0.0))
                go()
                base = count[id(dve_step)]
                dve.sem_inc(dve_begun, 1)
                with dve.Fori(0, KB // 4) as i:
                    for j in range(4):
                        f = i * 4 + j
                        dve.wait_ge(mm, i * 4 + (first + j + 1))
                        dve.tensor_tensor(blk(x, f), unit_ps[(first + j) % 2][:], blk(x, f), ALU.add).then_inc(evac, 1)
                        dve.wait_ge(in_hi, i * 4 + (il + j + 1))
                        dve.scalar_tensor_tensor(out=blk(cl, f), in0=blk(x, f), scalar=gains2[:, gain, bass.ds(f, 1)],
                                                 in1=blk(ch, f).bitcast(F32), op0=ALU.mult, op1=ALU.subtract).then_inc(in_lo, 1)
                        dve.wait_ge(sq_done, i * 4 + (sq_n + j + 1))
                        dve.wait_ge(dve_step, i * 4 + (base + j))
                        dve.tensor_tensor(acc, acc, sq, ALU.add).then_inc(dve_step, 1)
                for s in (evac, in_lo, dve_step):
                    count[id(s)] += KB
                last[0] = (dve_step, count[id(dve_step)])
                go()
                dve.sem_inc(ssq_src, 1)

            norm_product(OUT, 2, IL, SQ)
            IL += KB
            SQ += KB
            factor(LAYERS * 2 + 3)
            go()

            def x_softmax(h):
                s_x = aux[:, 2 * (h % 2):2 * (h % 2) + 2].rearrange("p b (c m) -> p (b c) m", m=MEM)
                dve.wait_ge(xs_mm, h + 1)
                go()
                did(dve.tensor_reduce(row[:, 2], s_x, AX, ALU.max))
                go()
                did(dve.tensor_scalar(row[:, 0], row[:, 2], -(DV ** -0.5), None, ALU.mult), xs_shift)
                dve.wait_ge(x_exp, NC * (h + 1))
                go()
                did(dve.reciprocal(row[:, 3], row[:, 1]))
                mult(x_p, x_p, row[:, 3].unsqueeze(2).broadcast_to([P, NC, MEM]), xp_ready)

            def x_lo(h):
                for b in range(2):
                    k = 2 * h + b
                    dve.wait_ge(in_hi, IL + k + 1)
                    go()
                    did(dve.tensor_tensor(blk(al, k), aux[:, 2 * (h % 2) + b], blk(ah, k).bitcast(F32), ALU.subtract), in_lo)

            for f in range(KB):
                dve.wait_ge(mm, XQ + f + 1)
                mult(xq_t[f], unit_ps[(XQ + f) % 2][:], rstd[:], evac)
                if f % 2 == 0 and f >= 2:
                    if f >= 4:
                        x_lo((f - 4) // 2)
                    x_softmax((f - 2) // 2)
            x_softmax(XH - 1)
            x_lo(XH - 2)
            x_lo(XH - 1)
            IL += KB
            norm_product(XO, 4, IL, SQ)
            IL += KB
            SQ += KB

            factor(LAYERS * 2 + 4)

            def up_pairs(first, b0, n, dst_h, dst_l):
                go()
                base = count[id(dve_step)]
                dve.sem_inc(dve_begun, 1)
                with dve.Fori(0, n // 2) as i:
                    for j in range(4):
                        u = first + j
                        used = 3 * (j // 2) + j % 2
                        pair = j // 2 + b0
                        b = i * 2 + ((j % 2) * FB + b0 + j // 2)
                        dve.wait_ge(mm, i * 4 + (u + 1))
                        dve.wait_ge(in_lo, i * 2 + (IL + pair))
                        dve.tensor_tensor(tmp[j % 2][:], unit_ps[u % 2][:], rstd[:], ALU.mult).then_inc(evac, 1)
                        dve.wait_ge(ffn_tap, i * 4 + (2 * b0 + j + 1))
                        for late, tap_no, signal in ((1, 1, dve_step), (2, 0, dve_step if j % 2 else ffn_pre)):
                            into = part_r[j % 2][:, late:T]
                            dve.scalar_tensor_tensor(out=into, in0=tmp[j % 2][:, 0:T - late], scalar=ffn_taps[:, tap_no, bass.ds(b, 1)], in1=into,
                                                     op0=ALU.mult, op1=ALU.add).then_inc(signal, 1)
                            if signal is dve_step:
                                used += 1
                                dve.wait_ge(dve_step, i * 6 + (base + used))
                        if j % 2:
                            dve.wait_ge(ffn_silu, i * 2 + (pair + 1))
                            dve.tensor_tensor(tmp2[:], part_r[0], part_r[1], ALU.mult).then_inc(ffn_src, 1)
                            dve.wait_ge(in_hi, i * 2 + (IL + pair + 1))
                            dve.tensor_tensor(blk(dst_l, i * 2 + j // 2), tmp2[:], blk(dst_h, i * 2 + j // 2).bitcast(F32), ALU.subtract).then_inc(in_lo, 1)
                count[id(evac)] += 2 * n
                count[id(in_lo)] += n
                count[id(dve_step)] += 3 * n
                last[0] = (in_lo, count[id(in_lo)])

            def down(first):
                go()
                dve.sem_inc(dve_begun, 1)
                with dve.Fori(0, KB // 4) as i:
                    for j in range(4):
                        u = first + j
                        f = i * 4 + j
                        dve.wait_ge(mm, i * 4 + (u + 1))
                        dve.wait_ge(evac, i * 4 + (u + 2))
                        dve.tensor_tensor(blk(x, f), unit_ps[u % 2][:], blk(x, f), ALU.add).then_inc(evac, 1)
                count[id(evac)] += KB
                last[0] = (evac, count[id(evac)])

            up_pairs(UPG[0], *GROUPS[0], ah, al)
            up_pairs(UPG[1], *GROUPS[1], bh, bl)
            down(DNG[0])
            up_pairs(UPG[2], *GROUPS[2], ah, al)
            down(DNG[1])
            go()
            did(dve.memset(acc, 0.0))
            for f in range(KB):
                u = DNG[2] + f
                dve.wait_ge(mm, u + 1)
                go()
                did(dve.tensor_tensor(blk(x, f), unit_ps[u % 2][:], blk(x, f), ALU.add), evac)
                dve.wait_ge(sq_done, SQ + f + 1)
                go()
                did(dve.tensor_tensor(acc, acc, sq, ALU.add))
            go()
            dve.sem_inc(ssq_src, 1)
            dve.wait_ge(std_done, LAYERS * 2 + 5)
            for half in range(2):
                go()
                did(dve.reciprocal(rstd[:, half * T // 2:(half + 1) * T // 2], rstd[:, half * T // 2:(half + 1) * T // 2]), rstd_half)
            dve.wait_ge(gained, KB)
            for k in range(KB):
                late = x[:, k * T + T // 2:(k + 1) * T]
                mult(late, late, rstd[:, T // 2:], fin_x[1])

        @block.tensor
        def _(pe):
            def ssq(n, dst=stat_ps, src=acc):
                pe.wait_ge(ssq_src, n)
                pe.matmul(dst, mean_d[:], src, start=True, stop=True).then_inc(ssq_mm, 1)

            with pe.Fori(0, LAYERS) as l:
                u0 = l * UNITS

                def unit(first, f, j, x_hi, x_lo, ready=None):
                    u = u0 + first + f
                    pe.wait_ge(w_lo, u + 3)
                    pe.wait_ge(evac, u + 1)
                    for k in range(KB):
                        if ready is not None:
                            pe.wait_ge(in_lo, l * LAYER_SPLITS + (ready + k + 1))
                        for n, (w, v) in enumerate(((wh, x_hi), (wh, x_lo), (wl, x_hi))):
                            last = pe.matmul(unit_ps[j % 2][:], w[j][:, k], v[:, k * T:(k + 1) * T],
                                             start=(k == 0 and n == 0), stop=(k == KB - 1 and n == 2))
                    last.then_inc(mm, 1)

                def product(first, x_hi, x_lo, splits=None, n=KB):
                    units(pe, n, lambda f, j: unit(first, f, j, x_hi, x_lo, splits if j == 0 else None))

                def norm_product(n, first, x_hi, x_lo, splits):
                    unit(first, 0, 0, x_hi, x_lo, splits)
                    ssq(n)
                    for f in range(1, KB):
                        unit(first, f, f % 4, x_hi, x_lo)

                def v_transposes(f, j):
                    pe.wait_ge(evac, u0 + VV + f + 3)
                    pe.wait_ge(v_done, l * KB + f + 1)
                    pe.wait_ge(const_in, 16 * 2)
                    for c in range(NC):
                        last = pe.transpose(aux[:, j % 2, c * P:(c + 1) * P], tmp[j % 2][:, c * P:(c + 1) * P], ident[:])
                    last.then_inc(v_tr, 1)

                for f in range(KB):
                    unit(VV, f, f % 4, ah, al, None if f else 0)
                    if f == 0:
                        ssq(l * 2 + 1)
                    else:
                        v_transposes(f - 1, (f - 1) % 4)
                for f in range(KB):
                    unit(QK, f, f % 4, ah, al)
                    if f == 0:
                        v_transposes(KB - 1, 3)
                product(CC, ah, al, n=24)

                def scores(h):
                    if h:
                        pe.wait_ge(p_done, l * HEADS + h)
                    for n in range(NC):
                        bank, col = S_AT[n]
                        last = pe.matmul(aux[:, bank, col:col + S_COLS[n]], cf[:, (HEADS + h) * T + n * P:(HEADS + h) * T + (n + 1) * P],
                                         cf[:, h * T + n * P:(h + 1) * T], start=True, stop=True)
                    last.then_inc(s_done, 1)

                def values(h):
                    pe.wait_ge(p_done, l * HEADS + h + 1)
                    pe.wait_ge(v_centred, l * HEADS + h + 1)
                    if h:
                        pe.wait_ge(o_out, l * HEADS + h)
                    for b in range(2):
                        for n in range(NC):
                            col = h * DV + b * P
                            last = pe.matmul(o_ps[b][:, n * P:T], v_tok[:, n, col:col + P], p_dec[h % 2][:, P_AT[n]:P_AT[n] + S_COLS[n]],
                                             start=(n == 0), stop=(n == NC - 1))
                    last.then_inc(pv_done, 1)

                def head_var(h):
                    pe.wait_ge(o_sq_sum, l * HEADS + h + 1)
                    pe.matmul(stat_ps, mean_v[:], tmp2[:], start=True, stop=True).then_inc(var_done, 1)

                pe.wait_ge(qk_done, l * KB + KB + 1)
                pe.wait_ge(v_done, l * KB + KB + 2)
                scores(0)
                for h in range(HEADS):
                    unit(G, 2 * h, 2 * h % 4, ah, al)
                    if h + 1 < HEADS:
                        scores(h + 1)
                    values(h)
                    unit(G, 2 * h + 1, (2 * h + 1) % 4, ah, al)
                    head_var(h)
                product(GA, ah, al)
                product(CONV, bh, bl, 8)
                product(GB, ah, al)
                product(RET, bh, bl, 16)
                product(WO, ah, al, 24)
                norm_product(l * 2 + 2, UP0, bh, bl, 32)
                product(UP1, bh, bl)
                product(DN0, ah, al, 40)
                product(UP2, bh, bl)
                product(DN1, ch, cl, 48)
                product(UP3, bh, bl)
                product(DN2, ah, al, 56)
                product(DN3, ch, cl, 64)
            IL = KB + LAYERS * LAYER_SPLITS

            def run(u, x_hi, x_lo, dst, n_k=KB, n=T, ready=None):
                pe.wait_ge(w_lo, u + 3)
                pe.wait_ge(evac, u + 1)
                for k in range(n_k):
                    if ready is not None:
                        pe.wait_ge(in_lo, ready + k + 1)
                    for q, (w, v) in enumerate(((wh, x_hi), (wh, x_lo), (wl, x_hi))):
                        last = pe.matmul(dst, w[u % 4][:, k], v[:, k * n:(k + 1) * n], start=(k == 0 and q == 0), stop=(k == n_k - 1 and q == 2))
                last.then_inc(mm, 1)

            def loop_units(first, n, x_hi, x_lo, n_k=KB, ready=None, order=None):
                order = order or range(n_k)
                with pe.Fori(0, n // 4) as i:
                    for j in range(4):
                        u = first + j
                        pe.wait_ge(w_lo, i * 4 + (u + 3))
                        pe.wait_ge(evac, i * 4 + (u + 1))
                        for at, k in enumerate(order):
                            if ready is not None and j == 0:
                                pe.wait_ge(in_lo, ready + at + 1)
                            for q, (w, v) in enumerate(((wh, x_hi), (wh, x_lo), (wl, x_hi))):
                                last = pe.matmul(unit_ps[u % 2][:], w[u % 4][:, k], v[:, k * T:(k + 1) * T],
                                                 start=(at == 0 and q == 0), stop=(at == n_k - 1 and q == 2))
                        last.then_inc(mm, 1)

            def norm_units(n, first, n_u, x_hi, x_lo, ready):
                for f in range(4):
                    run(first + f, x_hi, x_lo, unit_ps[(first + f) % 2][:], ready=None if f else ready)
                    if f == 0:
                        ssq(n)
                loop_units(first + 4, n_u - 4, x_hi, x_lo)

            def z(f, ready=None):
                run(U2 + f, ah, al, unit_ps[f % 2][:], ready=ready)

            def turn(dst, src):
                for c in range(NC):
                    last = pe.transpose(dst[:, c * P:(c + 1) * P], src[:, c * P:(c + 1) * P], ident[:])
                return last

            z(0, IL - KB)
            ssq(LAYERS * 2 + 1, aux[:, 2], acc2)
            ssq(LAYERS * 2 + 1)
            for f in range(1, 5):
                z(f)
            pe.wait_ge(evac, U2 + 3 + 3)
            turn(aux[:, 0], tmp[1][:]).then_inc(z_tr, 1)
            z(5)
            z(6)
            pe.wait_ge(evac, U2 + 5 + 3)
            turn(aux[:, 1], tmp[1][:]).then_inc(z_tr, 1)
            for f in range(7, 12):
                z(f)
            pe.wait_ge(z_act, 3)
            for c in range(NC):
                last = pe.transpose(aux[:, 2, c * GATES:(c + 1) * GATES], tmp[0][0:GATES, c * P:(c + 1) * P], ident[0:GATES, 0:GATES])
            last.then_inc(z_tr, 1)
            z(12)
            z(13)
            pe.wait_ge(c2_in, C2_LOADS * 16)
            pe.wait_ge(win_done, 2)
            pe.wait_ge(att_v, 2)
            pe.wait_ge(gate_tok, 1)
            for i in range(2):
                for g in range(2):
                    lanes = slice(g * HD, g * HD + HD)
                    for n in range(CMP_BLOCK):
                        last = pe.matmul(aux[lanes, 2 * i + g, 0:N_CMP], cmp_w1[i][lanes, n], cmp_win[i][lanes, n],
                                         start=(n == 0), stop=(n == CMP_BLOCK - 1))
                    last.then_inc(cmp_mm, 1)
            z(14)
            pe.wait_ge(cmp_gelu, 4)
            for g in range(2):
                lanes = slice(g * HD, g * HD + HD)
                pe.matmul(o_ps[g][0:HD, 0:N_CMP], cmp_w2[0][lanes], cmp_hid[0][lanes], start=True, stop=True)
                last = pe.matmul(o_ps[g][0:N_CMP, HD:2 * HD], cmp_hid[1][lanes], cmp_w2[1][lanes], start=True, stop=True)
                last.then_inc(cmp_mm, 1)
            z(15)
            pe.wait_ge(mem_scaled, 2)
            for k in range(KB):
                for c in range(2):
                    col = (k % 2) * MEM + c * P
                    last = pe.transpose(aux[:, k // 2, col:col + P], mem_raw[:, c, k * P:(k + 1) * P], ident[:])
                if k % 2:
                    last.then_inc(mem_tr, 1)
            z(16)
            pe.wait_ge(z_act, 7)
            pe.wait_ge(mem_lo, KB)
            for c in range(NC):
                for i in range(2):
                    last = pe.transpose(aux[:, c // 2, (c % 2) * DV + i * P:(c % 2) * DV + (i + 1) * P], y_gm[i][:, c * P:(c + 1) * P], ident[:])
            last.then_inc(gm_tr, 1)
            pe.wait_ge(ws_ready, 1)
            turn(aux[:, 2], gm_ws).then_inc(gm_tr, 1)
            z(17)
            z(18)
            def mem_unit(f):
                u = MK + f
                pe.wait_ge(evac, u + 2)
                run(u, memh, meml, unit_ps[0][:, (f % 2) * MEM:(f % 2 + 1) * MEM], n=MEM)

            def mixer_norms(k):
                for step, ready, count, src, done in ((GM_STEP, part_src, 1, part_acc[1], part_ms), (CV_STEP, cv_sum, 1, part_acc[2], cv_mean),
                                                      (CV_STEP + 1, cv_sqs, 1, part_acc[2], cv_var), (CV_STEP + 3, part_src, 2, part_acc[2], part_ms)):
                    if k == step:
                        pe.wait_ge(ready, count)
                        pe.wait_ge(evac, MK + k + 2)
                        pe.matmul(unit_ps[0][:], mean_v[:], src, start=True, stop=True).then_inc(done, 1)

            norm_read = {GM_STEP: (gm_ms_out, 1), CV_STEP: (cv_cen, 1), CV_STEP + 1: (cv_std, 1), CV_STEP + 3: (part_std, 2)}

            def query(c, g, r):
                lanes = slice((r % 2) * HD, (r % 2) * HD + HD)
                return lanes, q_t[2 * g + r // 2][lanes, c * P:(c + 1) * P]

            def att_scores(k):
                it, b, c, g = STEPS2[k]
                for r in range(REP):
                    lanes, q = query(c, g, r)
                    last = pe.matmul(aux[:, r, 0:(c + 1) * P], q, k_att[b][g][lanes, 0:(c + 1) * P], start=True, stop=True)
                    if r >= 2:
                        last.then_inc(s_att, 1)

            def compressed_scores(it):
                c, g = ITS[it]
                for r in range(REP):
                    lanes, q = query(c, g, r)
                    last = pe.matmul(o_ps[r % 2][:, r // 2 * 32:r // 2 * 32 + N_CMP], q, k_cmp[g][lanes], start=True, stop=True)
                    if r >= 2:
                        last.then_inc(s_cmp, 1)

            taken = [0]

            def turned(last):
                last.then_inc(t_att, 1)
                taken[0] += 1
                return taken[0]

            def turn_block(k, n):
                it, b, c, g = STEPS2[k]
                bank = o_ps[(n + (c if b else 1)) % 2]
                for r in range(REP):
                    last = pe.transpose(bank[:, r * P:(r + 1) * P], p_att[b][:, r, n * P:(n + 1) * P], ident[:])
                return turned(last)

            def att_values(k, first):
                it, b, c, g = STEPS2[k]
                for n in range(1, c + 2):
                    if n <= c:
                        pe.wait_ge(pt_ready, first + n - 2)
                        turn_block(k, n)
                    m = n - 1
                    pe.wait_ge(pt_ready, first + m)
                    last = pe.matmul(unit_ps[1][0:HD], v_att[b][:, m, g * HD:(g + 1) * HD], pt_att[b][:, m * T:(m + 1) * T],
                                     start=False, stop=(b == 1 and m == c))
                return last

            pe.wait_ge(ws_ready, 2)
            att_scores(0)
            pe.wait_ge(gm_ready, 1)
            pe.wait_ge(cmp_out, 2)
            for g in range(4):
                lanes = slice((g % 2) * HD, (g % 2) * HD + HD)
                for c in range(NC):
                    dst = o_ps[g // 2][lanes, c * P:(c + 1) * P]
                    pe.matmul(dst, v_ln[:, c, g * HD:(g + 1) * HD], gm_wt[:, g * P:(g + 1) * P], start=True, stop=False)
                    last = pe.matmul(dst, one_row[:], tmp2[0:1, g * P:(g + 1) * P], start=False, stop=True)
            last.then_inc(mix_mm, 1)
            pe.wait_ge(mixed, 2)
            compressed_scores(0)
            for k, (it, b, c, g) in enumerate(STEPS2):
                mixer_norms(k)
                if k + 1 < len(STEPS2):
                    if b:
                        pe.wait_ge(pt_ready, taken[0])
                        compressed_scores(it + 1)
                    pe.wait_ge(exp_att, REP * (k + 1))
                    att_scores(k + 1)
                if b == 0:
                    pe.wait_ge(pc_ready, it + 1)
                    pe.wait_ge(pt_ready, taken[0])
                    for r in range(REP):
                        last = pe.transpose(o_ps[0][0:N_CMP, r * P:(r + 1) * P], p_cmp[:, r], ident[:])
                    compressed = turned(last)
                elif it + 1 < len(ITS):
                    pe.wait_ge(shift_cmp, it + 2)
                if k in norm_read:
                    pe.wait_ge(*norm_read[k])
                mem_unit(k)
                if b == 0:
                    if it:
                        pe.wait_ge(o_taken, 2 * it)
                    pe.wait_ge(pt_ready, compressed)
                    pe.matmul(unit_ps[1][0:HD], v_cmp[:, g], tmp[0][0:N_CMP, :], start=True, stop=False)
                pe.wait_ge(p_ready, k + 1)
                last = att_values(k, turn_block(k, 0))
                if b:
                    last.then_inc(o_att, 1)

            pe.wait_ge(evac, MV + KB + 2)
            pe.wait_ge(pt_ready, taken[0])
            for m in range(2):
                for half in range(2):
                    dst = aux[:, 1 + half] if m else o_ps[half]
                    for q in range(4):
                        col = (half * 4 + q) * MEM + m * P
                        last = pe.transpose(dst[:, q * P:(q + 1) * P], mem_vt[:, col:col + P], ident[:])
                    last.then_inc(mv_tr, 1)
            pe.wait_ge(part_src, 3)
            pe.matmul(aux[:, 0], mean_n[:], part_acc[0], start=True, stop=True).then_inc(part_ms, 1)
            loop_units(OUT, KB, ah, al, ready=IL, order=PART_ORDER)
            IL += 2 * KB
            def x_scores(h):
                pe.wait_ge(evac, XQ + 2 * h + 1 + 3)
                if h == 0:
                    pe.wait_ge(mv_ready, 4)
                if h >= 2:
                    pe.wait_ge(in_lo, IL + 2 * (h - 2) + 2)
                for c in range(NC):
                    for b in range(2):
                        last = pe.matmul(aux[:, 2 * (h % 2) + c // 2, (c % 2) * MEM:(c % 2 + 1) * MEM], xq_t[2 * h + b][:, c * P:(c + 1) * P],
                                         mem_k[:, (2 * h + b) * MEM:(2 * h + b + 1) * MEM], start=(b == 0), stop=(b == 1))
                last.then_inc(xs_mm, 1)

            def x_turns(h):
                pe.wait_ge(xp_ready, h + 1)
                if h:
                    pe.wait_ge(xt_copy, 2 * h)
                for m in range(2):
                    for c in range(NC):
                        last = pe.transpose(o_ps[m][:, c * P:(c + 1) * P], x_p[:, c, m * P:(m + 1) * P], ident[:])
                    last.then_inc(xt_mm, 1)

            def x_values(h):
                pe.wait_ge(xt_copy, 2 * h + 2)
                for b in range(2):
                    k = 2 * h + b
                    for m in range(2):
                        last = pe.matmul(aux[:, 2 * (h % 2) + b], mem_v[:, m, k * P:(k + 1) * P], x_pt[:, m], start=(m == 0), stop=(m == 1))
                    last.then_inc(xo_mm, 1)

            for f in range(KB):
                run(XQ + f, ch, cl, unit_ps[(XQ + f) % 2][:], ready=None if f else IL - KB)
                if f == 0:
                    ssq(LAYERS * 2 + 2)
                elif f % 2:
                    if f >= 3:
                        x_turns((f - 3) // 2)
                else:
                    if f >= 4:
                        x_values((f - 4) // 2)
                    x_scores((f - 2) // 2)
            x_scores(XH - 1)
            x_values(XH - 2)
            x_turns(XH - 1)
            x_values(XH - 1)
            IL += KB
            loop_units(XO, KB, ah, al, ready=IL - KB)
            IL += KB

            norm_units(LAYERS * 2 + 3, UPG[0], 16, ch, cl, IL - KB)
            loop_units(UPG[1], 16, ch, cl)
            pe.wait_ge(in_lo, IL + 8)
            pe.sem_inc(pe_begun, 1)
            loop_units(DNG[0], KB, ah, al)
            loop_units(UPG[2], 12, ch, cl)
            pe.wait_ge(in_lo, IL + 16)
            pe.sem_inc(pe_begun, 1)
            loop_units(DNG[1], KB, bh, bl)
            pe.wait_ge(in_lo, IL + FB)
            pe.sem_inc(pe_begun, 1)
            loop_units(DNG[2], KB, ah, al, GROUPS[2][1])
            ssq(LAYERS * 2 + 4)

        @block.sync
        def _(sp):
            n_k = KB // 2
            x_out, o = x[:].rearrange("p (k t) -> p k t", k=KB), out.rearrange("(k p) t -> p k t", p=P)
            for k in range(0, KB, n_k):
                for half in (1, 0):
                    tokens = slice(half * T // 2, (half + 1) * T // 2)
                    sp.wait_ge(fin_x[half], k + n_k)
                    sp.dma_start(o[:, k:k + n_k, tokens], x_out[:, k:k + n_k, tokens]).then_inc(out_st, 16)
            sp.wait_ge(out_st, 16 * 4)


def shape_constants():
    half = P // 2
    freq = (10000.0 ** (-np.arange(half, dtype=np.float64) / half)).astype(np.float32)
    log_gamma = np.log1p(-np.exp2(-5.0 - np.arange(HEADS, dtype=np.float64)))
    rel = np.arange(T)[None, :] - np.arange(P)[:, None]
    dec = [np.where(rel >= 0, np.exp(g * np.maximum(rel, 0)), 0.0) * P ** -0.5 for g in log_gamma]
    i = np.arange(P)
    tril = i[:, None] >= i[None, :]
    t = i[:, None, None] + P * np.arange(NC)[None, :, None]
    seen = np.arange(N_CMP)[None, None, :] * CMP_STRIDE + CMP_BLOCK - 1 <= t
    return {
        "inv_freq": np.concatenate([freq, freq])[:, None].copy(),
        "ident": np.eye(P, dtype=np.float32),
        "decay": np.concatenate(dec, axis=1).astype(np.float32),
        "tril": tril.astype(np.float32),
        "diag": np.where(tril, 0.0, NEG).astype(np.float32),
        "cmp_add": np.where(seen, 0.0, NEG).astype(np.float32),
        "cmp_keep": seen.astype(np.float32),
    }


def kernel(x, positions, norm_mix, w_in, conv_w, w_conv_out, ret_norm, w_ret_out, w_o, norm_mlp, w_up, w_down, norm_final,
           mem_2, mix_norm_g_2, w_in_2, cmp_pe_2, cmp_w1_2, cmp_w2_2, gmlp_ln_g_2, gmlp_ln_b_2, gmlp_ws_2, gmlp_bs_2,
           conv_dw_w_2, conv_dw_b_2, conv_ln_g_2, conv_ln_b_2, mix_out_g_2, w_out_2, xattn_norm_g_2, mem_norm_g_2,
           xattn_wq_2, xattn_wk_2, xattn_wv_2, xattn_wo_2, ffn_norm_g_2, ffn_w_up_2, ffn_dw_w_2, ffn_dw_b_2, ffn_w_down_2,
           final_norm_g_2):
    import concourse.bacc as bacc
    from concourse.bass_utils import run_bass_kernel_spmd

    nc = bacc.Bacc("TRN2", target_bir_lowering=False, num_devices=1)
    constants = shape_constants()
    freq = constants.pop("inv_freq")

    def columns(*vectors):
        rows = np.concatenate([np.asarray(v).reshape(-1, np.shape(v)[-1]) for v in vectors])
        return rows.reshape(-1, P).T
    arrays = {
        "x": np.asarray(x).reshape(T, D).T,
        "positions": np.asarray(positions).reshape(1, T),
        "w_in": w_in, "w_conv_out": w_conv_out, "w_ret_out": w_ret_out, "w_o": w_o, "w_up": w_up, "w_down": w_down,
        "mem": np.asarray(mem_2).reshape(MEM, D),
        "w_in_2": w_in_2[0], "w_out_2": w_out_2[0], "wq_2": xattn_wq_2[0], "wk_2": xattn_wk_2[0], "wv_2": xattn_wv_2[0],
        "wo_2": xattn_wo_2[0], "up_2": ffn_w_up_2[0], "down_2": ffn_w_down_2[0],
        "cmp_w1": cmp_w1_2[0], "cmp_w2": cmp_w2_2[0],
        "gmlp_ws": gmlp_ws_2[0], "gmlp_bs": np.asarray(gmlp_bs_2).reshape(1, 4 * P),
        "gmlp_ln_g": gmlp_ln_g_2, "gmlp_ln_b": gmlp_ln_b_2,
        **constants,
    }
    arrays["vectors1"] = np.concatenate([
        columns(mix_norm_g_2, mix_out_g_2, xattn_norm_g_2, mem_norm_g_2, ffn_norm_g_2, final_norm_g_2, norm_final),
        columns(conv_w), columns(ret_norm), freq, columns(*(g for pair in zip(norm_mix, norm_mlp) for g in pair))], axis=1)
    pe = np.asarray(cmp_pe_2[0]).transpose(2, 0, 1).reshape(HD, 2 * CMP_BLOCK)
    arrays["vectors2"] = np.concatenate([
        columns(conv_dw_w_2, conv_dw_b_2, conv_ln_g_2, conv_ln_b_2), columns(ffn_dw_w_2, ffn_dw_b_2), np.concatenate([pe, pe])], axis=1)
    arrays = {n: np.ascontiguousarray(a) for n, a in arrays.items()}
    d = {n: nc.dram_tensor(n + "_dram", a.shape, mybir.dt.from_np(a.dtype), kind="ExternalInput").ap() for n, a in arrays.items()}
    out = nc.dram_tensor("out_dram", (D, T), F32, kind="ExternalOutput").ap()
    layer_stack_kernel(nc, d, out)
    r = run_bass_kernel_spmd(nc, [{n + "_dram": a for n, a in arrays.items()}], core_ids=[0])
    return r.results[0]["out_dram"].T.reshape(1, T, D)
```
